# Optimizing a Trainium2 kernel written in Bass

```python
import jax, jax.numpy as jnp
from jax import lax
import numpy as np

D_MODEL = 1024
BATCH = 1
SEQ = 128
DEPTH = 2
DEC_BATCH = 1
DEC_SEQ = 256
PAST_LEN = 128

GRID_W = 64
Q_BLOCK = 128
ROPE_THETA = 10000.0
EPS = 1e-6
F_FLOOR = 1e-30

H_A = 8
KV_A = 2
HD_A = 64
H_B = 8
Q_RANK = 384
KV_RANK = 256
NOPE_B = 64
ROPE_B = 32
V_B = 64
H_C = 8
DK_C = 64
DV_C = 64
CHUNK_C = 16
N_BRANCH = 3
BRANCH_W = 512
N_GROUPS = 4
E_PER_GROUP = 4
N_EXPERTS = N_GROUPS * E_PER_GROUP
TOP_K = 2
D_EXPERT = 512

IN_SPLITS = (H_A * HD_A, KV_A * HD_A, KV_A * HD_A,
             Q_RANK, KV_RANK, ROPE_B,
             H_C * DK_C, H_C * DK_C, H_C * DK_C,
             H_C * DV_C, H_C * DV_C,
             N_BRANCH * D_MODEL)
IN_COLS = sum(IN_SPLITS)

kernel_name = "hybrid_gqa_mla_hgrn2_hmoe_diffusion_step"

def _split_points():
    return np.cumsum(IN_SPLITS)[:-1].tolist()

def rms_norm(x, g):
    xf = x.astype(jnp.float32)
    y = xf * lax.rsqrt(jnp.mean(xf * xf, axis=-1, keepdims=True) + EPS)
    return (y * g.astype(jnp.float32)).astype(x.dtype)

def grid_positions(n):
    rows = n // GRID_W
    row = jnp.repeat(jnp.arange(rows, dtype=jnp.int32), GRID_W)
    col = jnp.tile(jnp.arange(GRID_W, dtype=jnp.int32), rows)
    return row, col

def axial_rope(x, row, col):
    half = x.shape[-1] // 2

    def rotate(xs, pos):
        inv = ROPE_THETA ** (-jnp.arange(0, half, 2, dtype=jnp.float32) / half)
        ang = pos.astype(jnp.float32)[:, None, None] * inv
        cos, sin = jnp.cos(ang), jnp.sin(ang)
        x1, x2 = xs[..., : half // 2], xs[..., half // 2:]
        return jnp.concatenate([x1 * cos - x2 * sin, x1 * sin + x2 * cos], axis=-1)

    xf = x.astype(jnp.float32)
    return jnp.concatenate([rotate(xf[..., :half], row), rotate(xf[..., half:], col)], axis=-1).astype(x.dtype)

def blocked_attention(q, k, v, scale):
    b, nq, g, r, d = q.shape
    nb = nq // Q_BLOCK
    qb = q.reshape(b, nb, Q_BLOCK, g, r, d).transpose(1, 0, 2, 3, 4, 5)

    def one_block(qblk):
        s = jnp.einsum('bqgrd,bkgd->bgrqk', qblk, k, preferred_element_type=jnp.float32) * scale
        p = jax.nn.softmax(s, axis=-1)
        return jnp.einsum('bgrqk,bkge->bqgre', p.astype(v.dtype), v)

    o = lax.map(one_block, qb)
    return o.transpose(1, 0, 2, 3, 4, 5).reshape(b, nq, g, r, v.shape[-1])

def mla_keys(ckv, k_rope, w_kv):
    b, n, _ = ckv.shape
    kv = (ckv @ w_kv).reshape(b, n, H_B, NOPE_B + V_B)
    k = jnp.concatenate([kv[..., :NOPE_B], jnp.broadcast_to(k_rope, (b, n, H_B, ROPE_B))], axis=-1)
    return k, kv[..., NOPE_B:]

def log_forget(pre, lb):
    f = lb + (1.0 - lb) * jax.nn.sigmoid(pre.astype(jnp.float32))
    return jnp.log(jnp.maximum(f, F_FLOOR))

def hgrn2_chunk_scan(q, k, v, log_f, s0):
    b, h, n, _ = q.shape
    nc = n // CHUNK_C
    ch = lambda t: t.reshape(b, h, nc, CHUNK_C, t.shape[-1]).astype(jnp.float32)
    q, k, v, log_f = ch(q), ch(k), ch(v), ch(log_f)
    cum = jnp.cumsum(log_f, axis=3)
    last = cum[:, :, :, -1:, :]
    causal = jnp.tril(jnp.ones((CHUNK_C, CHUNK_C), dtype=bool))[:, :, None]
    diff = cum[:, :, :, :, None, :] - cum[:, :, :, None, :, :]
    decay = jnp.where(causal, jnp.exp(jnp.where(causal, diff, 0.0)), 0.0)
    scores = jnp.einsum('bhctk,bhcsk,bhctsk->bhcts', q, k, decay)
    o_intra = jnp.einsum('bhcts,bhcsv->bhctv', scores, v)
    u = jnp.einsum('bhcsk,bhcsv->bhckv', k * jnp.exp(last - cum), v)
    a = jnp.exp(last[:, :, :, 0, :])

    def step(s, inp):
        a_c, u_c = inp
        return a_c[..., None] * s + u_c, s

    s_final, s_prev = lax.scan(step, s0.astype(jnp.float32),
                               (a.transpose(2, 0, 1, 3), u.transpose(2, 0, 1, 3, 4)))
    s_prev = s_prev.transpose(1, 2, 0, 3, 4)
    o_inter = jnp.einsum('bhctk,bhckv->bhctv', q * jnp.exp(cum), s_prev)
    return (o_intra + o_inter).reshape(b, h, n, v.shape[-1]), s_final

def token_mixer(h, ctx, lb, w_in, a_qn, a_kn, b_qn, b_wq, b_kvn, b_wkv, c_on, w_branch, w_out):
    b, n, _ = h.shape
    latent = ctx is not None
    (qa, ka, va, qra, kva, kra, fpre_f, fpre_b, qc, ic, gc, gpre) = jnp.split(h @ w_in, _split_points(), axis=-1)
    if latent:
        row, col = grid_positions(n)

    q_a = rms_norm(qa.reshape(b, n, H_A, HD_A), a_qn)
    k_a = rms_norm(ka.reshape(b, n, KV_A, HD_A), a_kn)
    v_a = va.reshape(b, n, KV_A, HD_A)
    if latent:
        q_a = axial_rope(q_a, row, col)
        keys_a = jnp.concatenate([axial_rope(k_a, row, col), ctx[0]], axis=1)
        vals_a = jnp.concatenate([v_a, ctx[1]], axis=1)
    else:
        keys_a, vals_a = k_a, v_a
    o_a = blocked_attention(q_a.reshape(b, n, KV_A, H_A // KV_A, HD_A), keys_a, vals_a,
                            HD_A ** -0.5).reshape(b, n, BRANCH_W)

    qb = (rms_norm(qra, b_qn) @ b_wq).reshape(b, n, H_B, NOPE_B + ROPE_B)
    q_nope, q_rope = qb[..., :NOPE_B], qb[..., NOPE_B:]
    ckv = rms_norm(kva, b_kvn)
    k_rope = kra[:, :, None, :]
    if latent:
        q_rope = axial_rope(q_rope, row, col)
        k_rope = axial_rope(k_rope, row, col)
    keys_b, vals_b = mla_keys(ckv, k_rope, b_wkv)
    if latent:
        ck_b, cv_b = mla_keys(ctx[2], ctx[3][:, :, None, :], b_wkv)
        keys_b = jnp.concatenate([keys_b, ck_b], axis=1)
        vals_b = jnp.concatenate([vals_b, cv_b], axis=1)
    q_b = jnp.concatenate([q_nope, q_rope], axis=-1)[:, :, :, None, :]
    o_b = blocked_attention(q_b, keys_b, vals_b, (NOPE_B + ROPE_B) ** -0.5).reshape(b, n, BRANCH_W)

    heads = lambda t: t.reshape(b, n, H_C, -1).transpose(0, 2, 1, 3)
    flip = lambda t: jnp.flip(t, axis=2)
    logf_f = heads(log_forget(fpre_f, lb[0]))
    logf_b = heads(log_forget(fpre_b, lb[1]))
    q_c, v_c = heads(qc), heads(ic)
    if latent:
        s0_f, s0_b = ctx[4], ctx[5]
    else:
        s0_f = s0_b = jnp.zeros((b, H_C, DK_C, DV_C), jnp.float32)
    o_f, s_f = hgrn2_chunk_scan(q_c, -jnp.expm1(logf_f), v_c, logf_f, s0_f)
    o_r, s_b = hgrn2_chunk_scan(flip(q_c), flip(-jnp.expm1(logf_b)), flip(v_c), flip(logf_b), s0_b)
    o_c = (o_f + flip(o_r)).transpose(0, 2, 1, 3).astype(h.dtype)
    o_c = (rms_norm(o_c, c_on) * jax.nn.silu(gc.reshape(b, n, H_C, DV_C))).reshape(b, n, BRANCH_W)

    gates = jax.nn.sigmoid(gpre.reshape(b, n, N_BRANCH, D_MODEL))
    proj = jnp.einsum('bnjw,jwd->bnjd', jnp.stack([o_a, o_b, o_c], axis=2), w_branch)
    out = jnp.sum(gates * proj, axis=2) @ w_out
    return out, (k_a, v_a, ckv, kra, s_f, s_b)

def hier_moe(h, wg, bg, we, be, e_gate, e_up, e_down):
    b, n, d = h.shape
    t = h.reshape(b * n, d)
    glog = (t @ wg + bg).astype(jnp.float32)
    _, gidx = lax.top_k(glog, 1)
    gsel = jax.nn.one_hot(gidx[:, 0], N_GROUPS, dtype=jnp.float32)
    gp = jnp.sum(jax.nn.softmax(glog, axis=-1) * gsel, axis=-1, keepdims=True)
    elog = (t @ we + be).astype(jnp.float32).reshape(-1, N_GROUPS, E_PER_GROUP)
    elog_g = jnp.einsum('tge,tg->te', elog, gsel)
    ev, ei = lax.top_k(elog_g, TOP_K)
    ew = jax.nn.softmax(ev, axis=-1) * gp
    eid = gidx * E_PER_GROUP + ei
    combine = jnp.einsum('tk,tke->te', ew, jax.nn.one_hot(eid, N_EXPERTS, dtype=jnp.float32))
    hg = jnp.einsum('td,edf->tef', t, e_gate)
    hu = jnp.einsum('td,edf->tef', t, e_up)
    act = jax.nn.silu(hg) * hu * combine.astype(t.dtype)[..., None]
    return jnp.einsum('tef,efd->td', act, e_down).reshape(b, n, d)

def trunk_layer(x, cvec, ctx, lb, lp):
    (w_mod, b_mod, n1, n2, w_in, a_qn, a_kn, b_qn, b_wq, b_kvn, b_wkv, c_on, w_branch, w_out,
     wg, bg, we, be, e_gate, e_up, e_down) = lp
    mod = jax.nn.silu(cvec) @ w_mod + b_mod
    sh1, sc1, g1, sh2, sc2, g2 = jnp.split(mod[..., None, :], 6, axis=-1)
    h = rms_norm(x, n1) * (1 + sc1) + sh1
    mix, ctx_out = token_mixer(h, ctx, lb, w_in, a_qn, a_kn, b_qn, b_wq, b_kvn, b_wkv, c_on, w_branch, w_out)
    x = x + g1 * mix
    h = rms_norm(x, n2) * (1 + sc2) + sh2
    x = x + g2 * hier_moe(h, wg, bg, we, be, e_gate, e_up, e_down)
    return x, ctx_out

def setup_inputs(seed: int = 0) -> dict:
    key = jax.random.key(seed)
    ks = iter(jax.random.split(key, 40))
    nrm = lambda shape, s=1.0: s * jax.random.normal(next(ks), shape, jnp.float32)
    gain = lambda shape: 1.0 + 0.01 * jax.random.normal(next(ks), shape, jnp.float32)
    d = D_MODEL
    return {
        "x_prompt": nrm((BATCH, SEQ, d)),
        "x_sample": nrm((DEC_BATCH, DEC_SEQ, d)),
        "cache_gqa_k": nrm((DEC_BATCH, DEPTH, PAST_LEN, KV_A, HD_A)),
        "cache_gqa_v": nrm((DEC_BATCH, DEPTH, PAST_LEN, KV_A, HD_A)),
        "cache_mla_ckv": nrm((DEC_BATCH, DEPTH, PAST_LEN, KV_RANK)),
        "cache_mla_krope": nrm((DEC_BATCH, DEPTH, PAST_LEN, ROPE_B)),
        "state_hgrn": nrm((DEC_BATCH, DEPTH, 2, H_C, DK_C, DV_C), 0.5),
        "c": nrm((DEC_BATCH, d)),
        "c_ctx": nrm((d,)),
        "w_mod": nrm((DEPTH, d, 6 * d), 0.5 * d ** -0.5),
        "b_mod": nrm((DEPTH, 6 * d), 0.01),
        "norm1_g": gain((DEPTH, d)),
        "norm2_g": gain((DEPTH, d)),
        "w_in": nrm((DEPTH, d, IN_COLS), d ** -0.5),
        "a_qnorm": gain((DEPTH, HD_A)),
        "a_knorm": gain((DEPTH, HD_A)),
        "b_qnorm": gain((DEPTH, Q_RANK)),
        "b_wq": nrm((DEPTH, Q_RANK, H_B * (NOPE_B + ROPE_B)), Q_RANK ** -0.5),
        "b_kvnorm": gain((DEPTH, KV_RANK)),
        "b_wkv": nrm((DEPTH, KV_RANK, H_B * (NOPE_B + V_B)), KV_RANK ** -0.5),
        "c_lb_logits": nrm((DEPTH, 2, H_C * DK_C)),
        "c_onorm": gain((DEPTH, DV_C)),
        "w_branch": nrm((DEPTH, N_BRANCH, BRANCH_W, d), BRANCH_W ** -0.5),
        "w_out": nrm((DEPTH, d, d), d ** -0.5),
        "r_group_w": nrm((DEPTH, d, N_GROUPS), d ** -0.5),
        "r_group_b": nrm((DEPTH, N_GROUPS), 0.01),
        "r_expert_w": nrm((DEPTH, d, N_EXPERTS), d ** -0.5),
        "r_expert_b": nrm((DEPTH, N_EXPERTS), 0.01),
        "e_gate": nrm((DEPTH, N_EXPERTS, d, D_EXPERT), d ** -0.5),
        "e_up": nrm((DEPTH, N_EXPERTS, d, D_EXPERT), d ** -0.5),
        "e_down": nrm((DEPTH, N_EXPERTS, D_EXPERT, d), D_EXPERT ** -0.5),
        "final_g": gain((d,)),
    }

def reference(x_prompt, x_sample, cache_gqa_k, cache_gqa_v, cache_mla_ckv, cache_mla_krope, state_hgrn,
              c, c_ctx, w_mod, b_mod, norm1_g, norm2_g, w_in, a_qnorm, a_knorm, b_qnorm, b_wq, b_kvnorm,
              b_wkv, c_lb_logits, c_onorm, w_branch, w_out, r_group_w, r_group_b, r_expert_w, r_expert_b,
              e_gate, e_up, e_down, final_g):
    p = jax.nn.softmax(c_lb_logits.astype(jnp.float32), axis=0)
    lbs = jnp.cumsum(p, axis=0) - p[0:1]
    xp, xs = x_prompt, x_sample
    new_k, new_v, new_ckv, new_kr, new_s = [], [], [], [], []
    for l in range(DEPTH):
        lp = (w_mod[l], b_mod[l], norm1_g[l], norm2_g[l], w_in[l], a_qnorm[l], a_knorm[l], b_qnorm[l],
              b_wq[l], b_kvnorm[l], b_wkv[l], c_onorm[l], w_branch[l], w_out[l], r_group_w[l], r_group_b[l],
              r_expert_w[l], r_expert_b[l], e_gate[l], e_up[l], e_down[l])
        xp, (k_a, v_a, ckv, kr, s_f, s_b) = trunk_layer(xp, c_ctx, None, lbs[l], lp)
        new_k.append(k_a)
        new_v.append(v_a)
        new_ckv.append(ckv)
        new_kr.append(kr)
        new_s.append(jnp.stack([s_f, s_b], axis=1))
        ctx_l = (cache_gqa_k[:, l], cache_gqa_v[:, l], cache_mla_ckv[:, l], cache_mla_krope[:, l],
                 state_hgrn[:, l, 0], state_hgrn[:, l, 1])
        xs, _ = trunk_layer(xs, c, ctx_l, lbs[l], lp)
    y_prompt = rms_norm(xp, final_g)
    y_sample = rms_norm(xs, final_g)
    return (y_prompt, y_sample, jnp.stack(new_k, axis=1), jnp.stack(new_v, axis=1),
            jnp.stack(new_ckv, axis=1), jnp.stack(new_kr, axis=1), jnp.stack(new_s, axis=1))


_drawn_inputs = setup_inputs


def setup_inputs(seed=0):
    import zlib

    import numpy as np

    out = dict(_drawn_inputs(seed))
    spreads = {}
    factors = {'cache_gqa_k': 5.193,
     'cache_gqa_v': 4.113,
     'cache_mla_ckv': 4.132,
     'cache_mla_krope': 7.304,
     'state_hgrn': 3.424,
     'b_mod': 2.939,
     'norm1_g': 5.884,
     'norm2_g': 3.662,
     'a_qnorm': 8.0,
     'a_knorm': 5.651,
     'b_qnorm': 8.0,
     'b_kvnorm': 5.964,
     'c_onorm': 8.0,
     'r_group_b': 5.576,
     'r_expert_b': 8.0,
     'final_g': 5.806}
    for name, (base, spread) in spreads.items():
        noise = np.random.default_rng([zlib.crc32(name.encode()), seed]).standard_normal(out[name].shape)
        drawn = base * np.exp(spread * noise) if base else spread * noise
        out[name] = __import__('jax').numpy.asarray(drawn.astype(out[name].dtype))
    for name, factor in factors.items():
        out[name] = (out[name] * factor).astype(out[name].dtype)
    return out
```

```python
from contextlib import ExitStack

import numpy as np

import concourse.bass as bass
from concourse import mybir

F32 = mybir.dt.float32
U8 = mybir.dt.uint8
ALU = mybir.AluOpType
ACT = mybir.ActivationFunctionType
AX = mybir.AxisListType.X

P = 128
D = 1024
KT = D // P
DEPTH = 2
CTX, LAT, PAST = 128, 256, 128
T = CTX + LAT
TT = T // P
KEYS = T + PAST
GRID_W = 64
EPS = 1e-6
F_FLOOR = 1e-30
HD = 64
HEADS = 8
KV_A = 2
Q_RANK, KV_RANK = 384, 256
NOPE, ROPE = 64, 32
QB_W = NOPE + ROPE
QT, CT = Q_RANK // P, KV_RANK // P
BW = 512
BT = BW // P
N_BRANCH = 3
NCDMA = 7
NCACHE = 4
NG, EG = 4, 4
NE = NG * EG
FE = 512
FT = FE // P
SLAB = 4096
RING = 4
GATES = 2
REGION = 19328
BANKS = 8
MODT = 6 * KT
LEVELS = [1 << i for i in range(7)]
GROUPS = ((0, 0, CTX), (1, CTX, T))
SCALE_A = HD ** -0.5
SCALE_B = QB_W ** -0.5
BIG = 1e30

N1, N2, BM, AQ, AK, BQ, BK, CO, RB, RW = np.cumsum([0, KT, KT, MODT, 1, 1, QT, CT, 1, NG + NE]).tolist()
NPAR = RW + KT * (NG + NE)
ONES, BLK, IDN, CA, SA, CB, SB = np.cumsum([0, P, P, P, LAT, LAT, LAT]).tolist()
NCON = SB + LAT

MIXER = ([("qa", SLAB), ("kv", SLAB), ("qr", SLAB), ("bwq", QT * HEADS * QB_W), ("bwkv", CT * HEADS * 2 * HD), ("ic", SLAB),
          ("fb0", SLAB), ("qc0", SLAB // 2), ("br0", SLAB), ("g00", SLAB), ("g01", SLAB),
          ("fb1", SLAB), ("qc1", SLAB // 2), ("br1", SLAB), ("g10", SLAB), ("g11", SLAB),
          ("gc", SLAB), ("br2", SLAB), ("g20", SLAB), ("g21", SLAB), ("o0", SLAB), ("o1", SLAB)])
NMOD = MODT // 4


def slab_order():
    out = [(0, f"m{i}", SLAB) for i in range(NMOD)]
    for l in range(DEPTH):
        out += [(l, n, s) for n, s in MIXER]
        for e in range(NE + 1):
            if e < NE:
                out += [(l, f"eg{e}", SLAB), (l, f"eu{e}", SLAB)]
            if e:
                out.append((l, f"ed{e - 1}", SLAB))
                if l + 1 < DEPTH and e <= NMOD:
                    out.append((l + 1, f"m{e - 1}", SLAB))
    return out


class Tally:

    def __init__(self, known):
        self.known, self.here, self.count, self.last = known, {}, {}, None

    def next(self, name, key):
        self.count[name] = self.count.get(name, 0) + 1
        self.last = self.here[name, key] = (name, self.count[name])

    def also(self, name, key):
        self.here[name, key] = self.last

    def of(self, name, key):
        return self.known.get((name, key), ("dummy", 1)) if not self.known else self.known[name, key]


def program(nc, A, known):
    tally = Tally(known)
    order = slab_order()
    held_by_bank, closing = {}, {}

    with ExitStack() as ctx:
        def sb(name, shape, dt=F32):
            return ctx.enter_context(nc.sbuf_tensor("sb_" + name, shape, dt))

        sems = {}

        def sem(name):
            if name not in sems:
                sems[name] = ctx.enter_context(nc.semaphore(name))
            return sems[name]

        def signal(name, key):
            tally.next(name, key)
            return sem(name), 1

        def made(name, key):
            s, n = tally.of(name, key)
            return sem(s), n

        psum = [ctx.enter_context(nc.psum_tensor(f"bank{b}", [P, 512], F32)) for b in range(BANKS)]
        bank_full = [sem(f"bank_full{b}") for b in range(BANKS)]
        bank_free = [sem(f"bank_free{b}") for b in range(BANKS)]
        uses = [0]

        def take(key):
            b, n = uses[0] % BANKS, uses[0] // BANKS
            uses[0] += 1
            held_by_bank[key] = (b, n)
            return psum[b], (bank_free[b], n) if n else None

        def held(key):
            return psum[held_by_bank[key][0]]

        def fills(key):
            return bank_full[held_by_bank[key][0]], 1

        def full(key):
            b, n = held_by_bank[key]
            return bank_full[b], n + 1

        def frees(key):
            b, n = held_by_bank[key]
            tally.last = (f"bank_free{b}", n + 1)
            return bank_free[b], 1

        def freed_by(key):
            b, n = held_by_bank[key]
            return bank_free[b], n + 1

        con = sb("con", [P, NCON])
        lmask = sb("lmask", [P, len(LEVELS), P], U8)
        par = sb("par", [P, DEPTH, NPAR])
        lbl = sb("lbl", [P, DEPTH, HEADS])
        lbw = sb("lbw", [P, 4, HEADS])
        lb = sb("lb", [P, DEPTH, HEADS])
        oml = sb("oml", [P, DEPTH, HEADS])
        fing = sb("fing", [P, KT])
        cv = sb("cv", [P, KT, 2])
        eps = sb("eps", [P, 1])
        mod = sb("mod", [P, DEPTH, MODT, 2])
        gain = sb("gain", [P, 2, KT, 2])
        xT = sb("xT", [P, KT, T])
        hT = sb("hT", [P, KT, T])
        tmp = sb("tmp", [P, KT, T])
        slabs = sb("slabs", [P, RING, SLAB])
        oBr = [sb(f"o{c}", [P, BT, T]) for c in "ABC"]
        std = sb("std", [P, 3, T])
        small = sb("small", [P, 16])

        region = sb("region", [P, REGION])
        at = [0]

        def part(shape, dt=F32):
            n = int(np.prod(shape[1:]))
            v = region[0:shape[0], at[0]:at[0] + n]
            at[0] += n
            assert at[0] <= REGION, at[0]
            names = "abcd"[:len(shape) - 1]
            if len(shape) > 2:
                v = v.rearrange(f"p ({' '.join(names)}) -> p {' '.join(names)}", **{c: s for c, s in zip(names, shape[1:])})
            return v

        qA = part([P, BT, T])
        knT = part([P, T])
        keysA = part([P, KV_A, KEYS])
        vA = part([P, 4, P])
        qr = part([P, QT, T])
        ckvT = part([P, CT, KEYS])
        krT = part([P, KEYS])
        qB = part([P, HEADS, T])
        keysB = part([P, HEADS, KEYS])
        vB = part([P, 4, BW])
        swp = part([P, LAT])
        nmx = part([P, 2, 2])
        rsum = part([P, 2, 2])
        pr = tmp[:, 0:2, :].rearrange("p a t -> p (a t)").rearrange("p (a t) -> p a t", a=2)
        probs = tmp[:, 0:4, :].rearrange("p (u i) t -> p u i t", u=2)
        probsT = tmp[:, 4:8, :].rearrange("p (u i) t -> p u i t", u=2)
        at[0] = 0
        Fg = part([P, 4, T])
        Kg = part([P, 4, T])
        qd = part([P, 4, T])
        vC = part([P, TT, BW])
        Ql = [part([P, 4, P]) for _ in LEVELS]
        Kl = [part([P, 4, P]) for _ in LEVELS]
        Pp = part([P, 4, P])
        Rr = part([P, 4, P])
        KRt = part([P, 4, P])
        QP = part([P, 2, 4, P])
        Am = part([P, 4, P])
        Sin = part([P, 2, HEADS, HD])
        Sout = part([P, HEADS, HD])
        dec = part([P, TT, HEADS])
        gsb = part([P, GATES, T])
        prod = part([P, T])
        at[0] = 0
        Y = part([P, KT, T])
        act = part([P, 2, FT, T])
        hg4 = part([P, FT, T])
        cb = part([P, 2, T])
        mt = part([P, T])
        combT = part([P, T])
        rt = part([P, 640])

        dma_con = sem("dma_con")
        dma_cache = sem("dma_cache")
        dma_state = sem("dma_state")
        dma_out = sem("dma_out")
        dma_slab = [sem(f"dma_slab{i}") for i in range(RING)]
        outs = [0]

        def W(l, name):
            i = [(a, b) for a, b, _ in order].index((l, name))
            return slabs[:, i % RING, :]

        def tile(l, name, c, k=KT):
            return W(l, name)[:, c * k * P:(c + 1) * k * P].rearrange("p (k n) -> p k n", k=k)

        units = [(br, hp, qt) for br in range(2) for hp in range(4) for qt in range(TT)]
        key_cols = lambda qt: (0, CTX) if qt == 0 else (CTX, KEYS)
        key_tiles = lambda qt: [0] if qt == 0 else [1, 2, 3]
        batches = [(hh, tt) for hh in range(2) for tt in range(TT)]
        fill = {(hh, tt): [(hh, j) for j in range(3 * tt, min(3 * tt + 3, KT))] for hh, tt in batches}

        def decay_steps(E, eng, l, hh, tt, prev, r, qs, ks, tag, step):
            cols = slice(tt * P, (tt + 1) * P)
            if prev:
                eng.wait_ge(*full(("kt", l, *prev)))
            E.memset(Rr[r], 1.0)
            step(E.tensor_copy(Pp[r], Fg[r, :, cols]))
            yield
            for n, b in enumerate(LEVELS):
                def halves(x, s, i=None):
                    v = x.rearrange("p a (m s b) -> p a m s b", s=2, b=b)[:, :, :, s, :]
                    if i is None:
                        return v
                    return v[:, :, :, i:i + 1].broadcast_to([HD, 4, P // (2 * b), b])

                edge = b - 1 if qs == 1 else 0
                if prev:
                    eng.wait_ge(*full(("A", l, *prev, n + 1)))
                E.tensor_tensor(halves(Ql[n][r], qs), halves(qd[r, :, cols], qs), halves(Pp[r], qs), ALU.mult)
                E.tensor_tensor(halves(Kl[n][r], ks), halves(Kg[r, :, cols], ks), halves(Rr[r], ks), ALU.mult).then_inc(*signal(f"lev_{tag}", (l, hh, tt, n)))
                eng.wait_ge(*made(f"lev_{tag}", (l, hh, tt, n)))
                step(E.tensor_tensor(halves(Rr[r], ks), halves(Rr[r], ks), halves(Pp[r], qs, edge), ALU.mult))
                step(E.tensor_tensor(halves(Pp[r], qs), halves(Pp[r], qs), halves(Pp[r], ks, edge), ALU.mult))
                yield
            last = P - 1 if qs == 1 else 0
            E.tensor_copy(dec[r, tt, 4 * hh:4 * hh + 4], Pp[r, :, last])
            if tt:
                if hh:
                    eng.wait_ge(*full(("oe", l, 0)))
                E.tensor_tensor(QP[r, tt - 1], qd[r, :, cols], Pp[r], ALU.mult)
            E.tensor_tensor(Rr[r], Rr[r], Kg[r, :, cols], ALU.mult).then_inc(*signal(f"kr_{tag}", (l, hh, tt)))
            if tt == 2:
                tally.also(f"qp_{tag}", (l, hh))
            yield

        def route(ve, V, l, step):
            L = rt[:, 0:TT * (NG + NE)].rearrange("p (t n) -> p t n", t=TT)
            comb = rt[:, 64:64 + TT * NE].rearrange("p (t g e) -> p t g e", t=TT, g=NG)
            gx = rt[:, 112:124].rearrange("p (t n) -> p t n", t=TT)
            ge = rt[:, 128:140].rearrange("p (t n) -> p t n", t=TT)
            ed, ee = rt[:, 140:143], rt[:, 144:147]
            w4 = [rt[:, 160 + 12 * i:172 + 12 * i].rearrange("p (t n) -> p t n", t=TT) for i in range(8)]
            w1 = [rt[:, 280 + 4 * i:283 + 4 * i] for i in range(12)]
            w16 = rt[:, 340:388].rearrange("p (t g e) -> p t g e", t=TT, g=NG)
            pref = rt[:, 392:396]
            b4 = lambda v: v.unsqueeze(2).broadcast_to([P, TT, 4])

            def first_of(out, eq, work, m):
                step(V.tensor_tensor(work, eq, pref.unsqueeze(1).broadcast_to([P, TT, 4]), ALU.mult))
                step(V.tensor_reduce(m, work, AX, ALU.max))
                step(V.tensor_tensor(out, work, b4(m), ALU.is_equal))

            for i in range(4):
                step(V.memset(rt[:, 392 + i:393 + i], float(4 - i)))
            ve.wait_ge(*full(("r", l)))
            ps = held(("r", l))
            V.tensor_tensor(L, ps[:, 0:TT * 32].rearrange("p (t n) -> p t n", t=TT)[:, :, 0:NG + NE],
                                  par[:, l, RB:RB + NG + NE].unsqueeze(1).broadcast_to([P, TT, NG + NE]), ALU.add).then_inc(*frees(("r", l)))
            ve.wait_ge(*freed_by(("r", l)))
            step(V.tensor_reduce(w1[0], L[:, :, 0:NG], AX, ALU.max))
            V.tensor_tensor(gx, L[:, :, 0:NG], b4(w1[0]), ALU.subtract).then_inc(*signal("glog", l))
            step(V.tensor_tensor(w4[0], L[:, :, 0:NG], b4(w1[0]), ALU.is_equal))
            first_of(w4[1], w4[0], w4[2], w1[1])
            step(V.tensor_tensor(w16, L[:, :, NG:NG + NE].rearrange("p t (g e) -> p t g e", g=NG),
                                 w4[1].unsqueeze(3).broadcast_to([P, TT, NG, EG]), ALU.mult))
            step(V.tensor_tensor(w4[3], w16[:, :, 0, :], w16[:, :, 1, :], ALU.add))
            step(V.tensor_tensor(w4[3], w4[3], w16[:, :, 2, :], ALU.add))
            step(V.tensor_tensor(w4[3], w4[3], w16[:, :, 3, :], ALU.add))
            step(V.tensor_reduce(w1[2], w4[3], AX, ALU.max))
            step(V.tensor_tensor(w4[0], w4[3], b4(w1[2]), ALU.is_equal))
            first_of(w4[4], w4[0], w4[2], w1[1])
            step(V.scalar_tensor_tensor(w4[5], w4[4], -BIG, w4[3], ALU.mult, ALU.add))
            step(V.tensor_reduce(w1[3], w4[5], AX, ALU.max))
            V.tensor_tensor(ed, w1[3], w1[2], ALU.subtract).then_inc(*signal("ediff", l))
            step(V.tensor_tensor(w4[0], w4[5], b4(w1[3]), ALU.is_equal))
            first_of(w4[6], w4[0], w4[2], w1[1])
            ve.wait_ge(*made("gexp", l))
            step(V.tensor_reduce(w1[4], ge, AX, ALU.add))
            step(V.reciprocal(w1[5], w1[4]))
            ve.wait_ge(*made("eexp", l))
            step(V.tensor_scalar(w1[6], ee, 1.0, None, ALU.add))
            step(V.reciprocal(w1[7], w1[6]))
            step(V.tensor_tensor(w1[8], w1[7], w1[5], ALU.mult))
            step(V.tensor_tensor(w1[9], w1[8], ee, ALU.mult))
            step(V.tensor_tensor(w4[4], w4[4], b4(w1[8]), ALU.mult))
            step(V.tensor_tensor(w4[6], w4[6], b4(w1[9]), ALU.mult))
            step(V.tensor_tensor(w4[7], w4[4], w4[6], ALU.add))
            V.tensor_tensor(comb, w4[1].unsqueeze(3).broadcast_to([P, TT, NG, EG]), w4[7].unsqueeze(2).broadcast_to([P, TT, NG, EG]),
                                 ALU.mult).then_inc(*signal("comb", l))

        block = ctx.enter_context(nc.Block())

        @block.tensor
        def _(pe):
            cur = [-1]

            def slab(l, name):
                i = [(a, b) for a, b, _ in order].index((l, name))
                if i != cur[0]:
                    assert i == cur[0] + 1, (l, name)
                    cur[0] = i
                    pe.wait_ge(dma_slab[i % RING], 16 * (i // RING + 1))

            def closes(key):
                closing[cur[0]] = key

            def gemm(key, out, pairs):
                n = len(pairs)
                for i, (w, a) in enumerate(pairs):
                    mm = nc.tensor.matmul(out, lhsT=w, rhs=a, start=(i == 0), stop=(i == n - 1))
                mm.then_inc(*fills(key))

            def norm(l, which):
                ps, reader = take(("n", l, which))
                if reader:
                    pe.wait_ge(*reader)
                for k in range(KT):
                    pe.wait_ge(*made("square", ("x", l, which, k)))
                    mm = nc.tensor.matmul(ps[:, 0:T], lhsT=con[:, ONES:ONES + P], rhs=tmp[:, k, :], start=(k == 0), stop=(k == KT - 1))
                mm.then_inc(*fills(("n", l, which)))

            def modulation(l, i):
                slab(l, f"m{i}")
                key = ("mod", l, i)
                ps, reader = take(key)
                if reader:
                    pe.wait_ge(*reader)
                for c in range(4):
                    w = tile(l, f"m{i}", c)
                    for k in range(KT):
                        mm = nc.tensor.matmul(ps[:, 2 * c:2 * c + 2], lhsT=w[:, k, :], rhs=cv[:, k, :], start=(k == 0), stop=(k == KT - 1))
                mm.then_inc(*fills(key))
                closes(key)

            def project(l, name, c, key, last=False):
                slab(l, name)
                ps, reader = take(key)
                if reader:
                    pe.wait_ge(*reader)
                w = tile(l, name, c)
                gemm(key, ps[:, 0:T], [(w[:, k, :], hT[:, k, :]) for k in range(KT)])
                if last:
                    closes(key)

            def head_norm(l, key, lhs, sqs):
                ps, reader = take(("hn", l, key))
                if reader:
                    pe.wait_ge(*reader)
                for i, s in enumerate(sqs):
                    pe.wait_ge(*made("square", (key, l, i)))
                    mm = nc.tensor.matmul(ps[:, 0:T], lhsT=con[:, lhs:lhs + P], rhs=s, start=(i == 0), stop=(i == len(sqs) - 1))
                mm.then_inc(*fills(("hn", l, key)))

            def merge(l, n, j):
                if j == 0:
                    slab(l, f"br{n}")
                    br_slab = cur[0]
                    held[n] = br_slab
                project(l, f"g{n}{j // 4}", j % 4, ("g", l, n, j), last=(j % 4 == 3))
                key = ("p", l, n, j)
                ps, reader = take(key)
                if reader:
                    pe.wait_ge(*reader)
                if j == 0:
                    if n < 2:
                        pe.wait_ge(*made("o_ready", (l, n)))
                    else:
                        pe.wait_ge(*made("oc_gated", (l, BT - 1)))
                w = W(l, f"br{n}").rearrange("p (c k n) -> p c k n", c=KT, k=BT)[:, j]
                gemm(key, ps[:, 0:T], [(w[:, k, :], oBr[n][:, k, :]) for k in range(BT)])
                if j == KT - 1:
                    closing[held[n]] = key

            held = {}

            pe.wait_ge(dma_con, 16 * NCDMA)
            for i in range(NMOD):
                if i == 0:
                    pe.wait_ge(*made("cond", 0))
                modulation(0, i)

            for l in range(DEPTH):
                norm(l, 1)
                for k in range(KT):
                    pe.wait_ge(*made("h_ready", (l, 1, k)))
                for c in range(BT):
                    project(l, "qa", c, ("qa", l, c), last=(c == BT - 1))
                    if c:
                        head_norm(l, f"qa{c - 1}", BLK, [tmp[:, c - 1, :]])
                project(l, "kv", 0, ("ka", l))
                head_norm(l, "qa3", BLK, [tmp[:, 3, :]])
                va = tile(l, "kv", 1)
                ps, reader = take(("va", l))
                if reader:
                    pe.wait_ge(*reader)
                for t in range(TT):
                    for k in range(KT):
                        mm = nc.tensor.matmul(ps[:, t * P:(t + 1) * P], lhsT=hT[:, k, t * P:(t + 1) * P], rhs=va[:, k, :],
                                              start=(k == 0), stop=(k == KT - 1))
                mm.then_inc(*fills(("va", l)))
                head_norm(l, "ka", BLK, [tmp[:, 4, :]])
                kr = tile(l, "kv", 2)
                ps, reader = take(("kr", l))
                if reader:
                    pe.wait_ge(*reader)
                gemm(("kr", l), ps[NOPE:NOPE + ROPE, 0:T], [(kr[:, k, 0:ROPE], hT[:, k, :]) for k in range(KT)])
                project(l, "kv", 3, ("qr", l, 0), last=True)
                project(l, "qr", 0, ("qr", l, 1))
                project(l, "qr", 1, ("qr", l, 2))
                project(l, "qr", 2, ("kc", l, 0))
                head_norm(l, "qr", ONES, [tmp[:, 5 + c, :] for c in range(QT)])
                project(l, "qr", 3, ("kc", l, 1), last=True)
                head_norm(l, "kc", ONES, [tmp[:, c, :] for c in range(CT)])
                slab(l, "bwq")
                w = W(l, "bwq")[:, 0:QT * HEADS * QB_W].rearrange("p (k n) -> p k n", k=QT)
                for c in range(QT):
                    pe.wait_ge(*made("normed", (f"qr{c}", l)))
                for h in range(HEADS):
                    ps, reader = take(("qb", l, h))
                    if reader:
                        pe.wait_ge(*reader)
                    gemm(("qb", l, h), ps[0:QB_W, 0:T], [(w[:, k, h * QB_W:(h + 1) * QB_W], qr[:, k, :]) for k in range(QT)])
                closes(("qb", l, HEADS - 1))
                slab(l, "bwkv")
                w = W(l, "bwkv")[:, 0:CT * BW].rearrange("p (k n) -> p k n", k=CT)
                wv = W(l, "bwkv")[:, CT * BW:2 * CT * BW].rearrange("p (k n) -> p k n", k=CT)
                for c in range(CT):
                    pe.wait_ge(*made("normed", (f"kc{c}", l)))
                pe.wait_ge(dma_cache, 16 * NCACHE * (l + 1))
                for h in range(HEADS):
                    ps, reader = take(("kb", l, h))
                    if reader:
                        pe.wait_ge(*reader)
                    gemm(("kb", l, h), ps[0:NOPE, :], [(w[:, k, h * HD:(h + 1) * HD], ckvT[:, k, :]) for k in range(CT)])
                for t in range(4):
                    ps, reader = take(("vb", l, t))
                    if reader:
                        pe.wait_ge(*reader)
                    gemm(("vb", l, t), ps[:, :], [(ckvT[:, k, t * P:(t + 1) * P], wv[:, k, :]) for k in range(CT)])
                closes(("vb", l, 3))

                def scores(u):
                    br, hp, qt = units[u]
                    c0, c1 = key_cols(qt)
                    for i in range(2):
                        h = 2 * hp + i
                        ps, reader = take(("s", l, u, i))
                        if reader:
                            pe.wait_ge(*reader)
                        if br == 0:
                            r = slice(HD * i, HD * i + HD)
                            if u == 0 and i == 0:
                                pe.wait_ge(*made("dup", (l, 3)))
                            pe.wait_ge(*made("roped", (l, hp)))
                            q, k = qA[r, hp, qt * P:(qt + 1) * P], keysA[r, h // 4, c0:c1]
                        else:
                            pe.wait_ge(*made("roped", (l, "qb")))
                            pe.wait_ge(*made("kr_copied", l))
                            pe.wait_ge(*freed_by(("kb", l, h)))
                            q, k = qB[0:QB_W, h, qt * P:(qt + 1) * P], keysB[0:QB_W, h, c0:c1]
                        gemm(("s", l, u, i), ps[:, 0:c1 - c0], [(q, k)])

                def turn(u):
                    br, hp, qt = units[u]
                    for i in range(2):
                        ps, reader = take(("t", l, u, i))
                        if reader:
                            pe.wait_ge(*reader)
                        pe.wait_ge(*made("probs", (l, u, i)))
                        for t in range(len(key_tiles(qt))):
                            mm = nc.tensor.transpose(ps[:, t * P:(t + 1) * P], probs[:, u % 2, i, t * P:(t + 1) * P], con[:, IDN:IDN + P])
                        mm.then_inc(*fills(("t", l, u, i)))

                def values(u):
                    br, hp, qt = units[u]
                    ps, reader = take(("o", l, u))
                    if reader:
                        pe.wait_ge(*reader)
                    if u == 0:
                        pe.wait_ge(*freed_by(("va", l)))
                    if br == 1:
                        pe.wait_ge(*freed_by(("vb", l, 3)))
                    for i in range(2):
                        h = 2 * hp + i
                        pe.wait_ge(*freed_by(("t", l, u, i)))
                        for t, kt in enumerate(key_tiles(qt)):
                            v = vA[:, kt, (h // 4) * HD:(h // 4 + 1) * HD] if br == 0 else vB[:, kt, h * HD:(h + 1) * HD]
                            mm = nc.tensor.matmul(ps[HD * i:HD * i + HD, 0:P], lhsT=v, rhs=probsT[:, u % 2, i, t * P:(t + 1) * P],
                                                  start=(t == 0), stop=(t == len(key_tiles(qt)) - 1))
                    mm.then_inc(*fills(("o", l, u)))

                for s in range(len(units) + 2):
                    if s < len(units):
                        scores(s)
                    if 1 <= s <= len(units):
                        turn(s - 1)
                    if s >= 2:
                        values(s - 2)

                slab(l, "ic")
                w = W(l, "ic").rearrange("p (k n) -> p k n", k=KT)
                for t in range(TT):
                    ps, reader = take(("ic", l, t))
                    if reader:
                        pe.wait_ge(*reader)
                    gemm(("ic", l, t), ps[:, :], [(hT[:, k, t * P:(t + 1) * P], w[:, k, :]) for k in range(KT)])
                closes(("ic", l, TT - 1))
                for hh in range(2):
                    for c in range(4):
                        project(l, f"fb{hh}", c, ("fb", l, hh, c), last=(c == 3))
                    for c in range(2):
                        project(l, f"qc{hh}", c, ("qc", l, hh, c), last=(c == 1))
                    for tt in range(TT):
                        cols = slice(tt * P, (tt + 1) * P)
                        todo = list(fill[hh, tt])
                        for n in range(len(LEVELS) + 1):
                            ps, reader = take(("A", l, hh, tt, n))
                            if reader:
                                pe.wait_ge(*reader)
                            if n == 0:
                                pe.wait_ge(*made("fk_ready", (l, hh, 3)))
                                pe.wait_ge(*freed_by(("qc", l, hh, 1)))
                            else:
                                pe.wait_ge(*made("lev_f", (l, hh, tt, n - 1)))
                                pe.wait_ge(*made("lev_b", (l, hh, tt, n - 1)))
                            for d in range(4):
                                kk, qq = (Kg[:, d, cols], qd[:, d, cols]) if n == 0 else (Kl[n - 1][:, d, :], Ql[n - 1][:, d, :])
                                mm = nc.tensor.matmul(ps[:, d * P:(d + 1) * P], lhsT=kk, rhs=qq, start=True, stop=True)
                            mm.then_inc(*fills(("A", l, hh, tt, n)))
                            if n in (1, 3) and todo:
                                merge(l, *todo.pop(0))
                        ps, reader = take(("kt", l, hh, tt))
                        if reader:
                            pe.wait_ge(*reader)
                        pe.wait_ge(*made("kr_f", (l, hh, tt)))
                        pe.wait_ge(*made("kr_b", (l, hh, tt)))
                        for d in range(4):
                            mm = nc.tensor.transpose(ps[:, d * P:(d + 1) * P], Rr[:, d, :], con[:, IDN:IDN + P])
                        mm.then_inc(*fills(("kt", l, hh, tt)))
                        while todo:
                            merge(l, *todo.pop(0))
                        if hh == 0 and tt == 0:
                            pe.wait_ge(*freed_by(("ic", l, TT - 1)))
                        ps, reader = take(("U", l, hh, tt))
                        if reader:
                            pe.wait_ge(*reader)
                        pe.wait_ge(*freed_by(("kt", l, hh, tt)))
                        for d in range(4):
                            h = 4 * hh + d
                            mm = nc.tensor.matmul(ps[:, d * HD:(d + 1) * HD], lhsT=KRt[:, d, :], rhs=vC[:, tt, h * HD:(h + 1) * HD],
                                                  start=True, stop=True)
                        mm.then_inc(*fills(("U", l, hh, tt)))
                        ps, reader = take(("oi", l, hh, tt))
                        if reader:
                            pe.wait_ge(*reader)
                        pe.wait_ge(*freed_by(("A", l, hh, tt, len(LEVELS))))
                        for d in range(4):
                            h = 4 * hh + d
                            mm = nc.tensor.matmul(ps[HD * (d % 2):HD * (d % 2) + HD, (d // 2) * P:(d // 2 + 1) * P],
                                                  lhsT=vC[:, tt, h * HD:(h + 1) * HD], rhs=Am[:, d, :], start=True, stop=True)
                        mm.then_inc(*fills(("oi", l, hh, tt)))
                    ps, reader = take(("oe", l, hh))
                    if reader:
                        pe.wait_ge(*reader)
                    pe.wait_ge(*made("s_f", (l, hh)))
                    pe.wait_ge(*made("s_b", (l, hh)))
                    pe.wait_ge(*made("qp_f", (l, hh)))
                    pe.wait_ge(*made("qp_b", (l, hh)))
                    for t in range(2):
                        for d in range(4):
                            h = 4 * hh + d
                            o = (d // 2) * 2 * P + t * P
                            mm = nc.tensor.matmul(ps[HD * (d % 2):HD * (d % 2) + HD, o:o + P], lhsT=Sin[:, t, h, :], rhs=QP[:, t, d, :],
                                                  start=True, stop=True)
                    mm.then_inc(*fills(("oe", l, hh)))
                for c in range(BT):
                    project(l, "gc", c, ("gc", l, c), last=(c == BT - 1))
                    head_norm(l, f"oc{c}", BLK, [gsb[:, c % 2, :]])
                for j in range(KT):
                    merge(l, 2, j)
                for j in range(KT):
                    slab(l, f"o{j // 4}")
                    w = tile(l, f"o{j // 4}", j % 4)
                    if j == 0:
                        pe.wait_ge(*made("merged", (l, 2, KT - 1)))
                    ps, reader = take(("out", l, j))
                    if reader:
                        pe.wait_ge(*reader)
                    gemm(("out", l, j), ps[:, 0:T], [(w[:, k, :], tmp[:, k, :]) for k in range(KT)])
                    if j % 4 == 3:
                        closes(("out", l, j))

                norm(l, 2)
                for k in range(KT):
                    pe.wait_ge(*made("h_ready", (l, 2, k)))
                ps, reader = take(("r", l))
                if reader:
                    pe.wait_ge(*reader)
                rw = par[:, l, RW:RW + KT * (NG + NE)].rearrange("p (k n) -> p k n", k=KT)
                for t in range(TT):
                    for k in range(KT):
                        mm = nc.tensor.matmul(ps[:, t * 32:t * 32 + NG + NE], lhsT=hT[:, k, t * P:(t + 1) * P], rhs=rw[:, k, :],
                                              start=(k == 0), stop=(k == KT - 1))
                mm.then_inc(*fills(("r", l)))

                def up(e):
                    for f in range(FT):
                        slab(l, f"eg{e}")
                        w = tile(l, f"eg{e}", f)
                        ps, reader = take(("eg", l, e, f))
                        if reader:
                            pe.wait_ge(*reader)
                        gemm(("eg", l, e, f), ps[:, 0:T], [(w[:, k, :], hT[:, k, :]) for k in range(KT)])
                        if f == FT - 1:
                            closes(("eg", l, e, f))
                    slab(l, f"eu{e}")
                    if e == 0:
                        ps, reader = take(("cT", l))
                        if reader:
                            pe.wait_ge(*reader)
                        pe.wait_ge(*made("comb", l))
                        for t in range(TT):
                            mm = nc.tensor.transpose(ps[0:NE, t * P:(t + 1) * P], rt[:, 64 + t * NE:64 + (t + 1) * NE], con[:, IDN:IDN + P])
                        mm.then_inc(*fills(("cT", l)))
                        pe.wait_ge(*freed_by(("cT", l)))
                    ps, reader = take(("cb", l, e))
                    if reader:
                        pe.wait_ge(*reader)
                    gemm(("cb", l, e), ps[:, 0:T], [(con[0:NE, IDN + e:IDN + e + 1].broadcast_to([NE, P]), combT[0:NE, :])])
                    for f in range(FT):
                        w = tile(l, f"eu{e}", f)
                        ps, reader = take(("eu", l, e, f))
                        if reader:
                            pe.wait_ge(*reader)
                        gemm(("eu", l, e, f), ps[:, 0:T], [(w[:, k, :], hT[:, k, :]) for k in range(KT)])
                    closes(("eu", l, e, FT - 1))

                def down(e):
                    slab(l, f"ed{e}")
                    w = W(l, f"ed{e}").rearrange("p (c k n) -> p c k n", c=KT, k=FT)
                    for f in range(FT):
                        pe.wait_ge(*made("act", (l, e, f)))
                    for j in range(KT):
                        ps, reader = take(("ed", l, e, j))
                        if reader:
                            pe.wait_ge(*reader)
                        gemm(("ed", l, e, j), ps[:, 0:T], [(w[:, j, k, :], act[:, e % 2, k, :]) for k in range(FT)])
                    closes(("ed", l, e, KT - 1))

                for e in range(NE + 1):
                    if e < NE:
                        up(e)
                    if e:
                        down(e - 1)
                        if l + 1 < DEPTH and e <= NMOD:
                            modulation(l + 1, e - 1)
            norm(DEPTH, 1)

        @block.scalar
        def _(sc):
            def squares_x(l, which):
                for k in range(KT):
                    if not (l == 0 and which == 1):
                        sc.wait_ge(*made("x_ready", (l, which, k)))
                    nc.scalar.activation(tmp[:, k, :], xT[:, k, :], ACT.Square).then_inc(*signal("square", ("x", l, which, k)))
                root(("n", l, which), 1.0 / D, ("n", l, which))

            nroot = [0]

            def root(bkey, scale, key):
                sc.wait_ge(*full(bkey))
                ps = held(bkey)
                s = nroot[0] % 3
                if nroot[0] >= 3:
                    sc.wait_ge(*made("std_used", nroot[0] - 3))
                nc.scalar.activation(std[:, s, :], ps[:, 0:T], ACT.Sqrt, scale=scale, bias=eps[:, 0:1]).then_inc(*frees(bkey))
                nroot[0] += 1

            def split(bkey, dst, sq, key, l, i, wait=None):
                sc.wait_ge(*full(bkey))
                ps = held(bkey)
                if wait:
                    wait()
                nc.scalar.activation(sq, ps[:, 0:T], ACT.Square).then_inc(*signal("square", (key, l, i)))
                nc.scalar.activation(dst, ps[:, 0:T], ACT.Copy).then_inc(*frees(bkey))

            sc.wait_ge(dma_con, 16 * NCDMA)
            sc.wait_ge(*made("eps", 0))
            nc.scalar.activation(cv[:, :, :], cv[:, :, :], ACT.Silu).then_inc(*signal("cond", 0))
            sc.wait_ge(*made("lbmax", 0))
            nc.scalar.activation(lbw[:, 2:4, :], lbw[:, 0:2, :], ACT.Exp).then_inc(*signal("lbexp", 0))

            for l in range(DEPTH):
                squares_x(l, 1)
                for c in range(BT):
                    split(("qa", l, c), qA[:, c, :], tmp[:, c, :], f"qa{c}", l, 0)
                    if c:
                        root(("hn", l, f"qa{c - 1}"), 1.0 / HD, ("qa", c - 1))
                split(("ka", l), knT[:, :], tmp[:, 4, :], "ka", l, 0)
                root(("hn", l, "qa3"), 1.0 / HD, ("qa", 3))
                sc.wait_ge(*full(("va", l)))
                ps = held(("va", l))
                ins = nc.scalar.activation(vA[:, 0:TT, :].rearrange("p a n -> p (a n)"), ps[:, 0:T], ACT.Copy)
                ins.then_inc(*frees(("va", l)))
                root(("hn", l, "ka"), 1.0 / HD, "ka")
                sc.wait_ge(*full(("kr", l)))
                ps = held(("kr", l))
                nc.scalar.activation(krT[NOPE:NOPE + ROPE, 0:T], ps[NOPE:NOPE + ROPE, 0:T], ACT.Copy).then_inc(*frees(("kr", l)))
                for c in range(QT):
                    split(("qr", l, c), qr[:, c, :], tmp[:, 5 + c, :], "qr", l, c)
                split(("kc", l, 0), ckvT[:, 0, 0:T], tmp[:, 0, :], "kc", l, 0)
                root(("hn", l, "qr"), 1.0 / Q_RANK, "qr")
                split(("kc", l, 1), ckvT[:, 1, 0:T], tmp[:, 1, :], "kc", l, 1)
                root(("hn", l, "kc"), 1.0 / KV_RANK, "kc")
                sc.wait_ge(*made("roped", (l, "ka")))
                for j in range(KV_A):
                    for r in range(2):
                        nc.scalar.activation(keysA[HD * r:HD * r + HD, j, 0:T], knT[HD * j:HD * j + HD, :], ACT.Copy).then_inc(*signal("dup", (l, 2 * j + r)))
                for h in range(HEADS):
                    sc.wait_ge(*full(("qb", l, h)))
                    ps = held(("qb", l, h))
                    nc.scalar.activation(qB[0:QB_W, h, :], ps[0:QB_W, 0:T], ACT.Copy).then_inc(*frees(("qb", l, h)))
                for h in range(HEADS):
                    sc.wait_ge(*full(("kb", l, h)))
                    ps = held(("kb", l, h))
                    nc.scalar.activation(keysB[0:NOPE, h, :], ps[0:NOPE, :], ACT.Copy).then_inc(*frees(("kb", l, h)))
                for t in range(4):
                    sc.wait_ge(*full(("vb", l, t)))
                    ps = held(("vb", l, t))
                    nc.scalar.activation(vB[:, t, :], ps[:, :], ACT.Copy).then_inc(*frees(("vb", l, t)))

                def exps(u):
                    br, hp, qt = units[u]
                    c0, c1 = key_cols(qt)
                    for i in range(2):
                        sc.wait_ge(*made("negmax", (l, u, i)))
                        sc.wait_ge(*full(("s", l, u, i)))
                        ps = held(("s", l, u, i))
                        if u < 2 and i == 0:
                            sc.wait_ge(*made("roped", (l, "qb")))
                        if u >= 2:
                            sc.wait_ge(*full(("t", l, u - 2, i)))
                        nc.scalar.activation(probs[:, u % 2, i, 0:c1 - c0], ps[:, 0:c1 - c0], ACT.Exp, bias=nmx[:, u % 2, i:i + 1],
                                                   scale=(SCALE_A, SCALE_B)[br], accum_out=rsum[:, u % 2, i:i + 1]).then_inc(*frees(("s", l, u, i)))

                def probs_turned(u):
                    br, hp, qt = units[u]
                    n = P * len(key_tiles(qt))
                    sc.wait_ge(*full(("t", l, u, 1)))
                    ps = held(("t", l, u, 1))
                    if u >= 2:
                        sc.wait_ge(*full(("o", l, u - 2)))
                    nc.scalar.activation(probsT[:, u % 2, 1, 0:n], ps[:, 0:n], ACT.Copy).then_inc(*frees(("t", l, u, 1)))

                for s in range(len(units) + 1):
                    if s < len(units):
                        exps(s)
                    if s >= 1:
                        probs_turned(s - 1)

                sc.wait_ge(*made("o_ready", (l, 1)))
                sc.wait_ge(dma_out, 16 * (5 * l + 4))
                for t in range(TT):
                    sc.wait_ge(*full(("ic", l, t)))
                    ps = held(("ic", l, t))
                    nc.scalar.activation(vC[:, t, :], ps[:, :], ACT.Copy).then_inc(*frees(("ic", l, t)))
                gates = [0]

                def gate(n, j):
                    sc.wait_ge(*full(("g", l, n, j)))
                    ps = held(("g", l, n, j))
                    if gates[0] >= GATES:
                        sc.wait_ge(*made("gate_used", (l, gates[0] - GATES)))
                    nc.scalar.activation(gsb[:, gates[0] % GATES, :], ps[:, 0:T], ACT.Sigmoid).then_inc(*frees(("g", l, n, j)))
                    gates[0] += 1

                for hh in range(2):
                    for c in range(4):
                        sc.wait_ge(*full(("fb", l, hh, c)))
                        ps = held(("fb", l, hh, c))
                        if hh:
                            sc.wait_ge(*full(("oi", l, 0, TT - 1)))
                            sc.wait_ge(*made("kr_f", (l, 0, TT - 1)))
                            sc.wait_ge(*made("kr_b", (l, 0, TT - 1)))
                        nc.scalar.activation(Fg[:, c, :], ps[:, 0:T], ACT.Sigmoid).then_inc(*frees(("fb", l, hh, c)))
                    for c in range(2):
                        sc.wait_ge(*full(("qc", l, hh, c)))
                        ps = held(("qc", l, hh, c))
                        for i in range(2):
                            for r in range(2):
                                ins = nc.scalar.activation(qd[HD * r:HD * r + HD, 2 * c + i, :], ps[HD * i:HD * i + HD, 0:T], ACT.Copy)
                                if (i, r) == (1, 1):
                                    ins.then_inc(*frees(("qc", l, hh, c)))
                                else:
                                    ins.then_inc(*signal("qd_part", (l, hh, c, i, r)))
                    for tt in range(TT):
                        todo = list(fill[hh, tt])
                        for _ in range(2):
                            if todo:
                                gate(*todo.pop(0))
                        sc.wait_ge(*full(("kt", l, hh, tt)))
                        ps = held(("kt", l, hh, tt))
                        if not (hh == 0 and tt == 0):
                            ph, pt = batches[batches.index((hh, tt)) - 1]
                            sc.wait_ge(*full(("U", l, ph, pt)))
                        nc.scalar.activation(KRt[:, :, :].rearrange("p a n -> p (a n)"), ps[:, :], ACT.Copy).then_inc(*frees(("kt", l, hh, tt)))
                        while todo:
                            gate(*todo.pop(0))
                        sc.wait_ge(*full(("oi", l, hh, tt)))
                        ps = held(("oi", l, hh, tt))
                        nc.scalar.activation(oBr[2][:, 2 * hh:2 * hh + 2, tt * P:(tt + 1) * P],
                                                   ps[:, 0:2 * P].rearrange("p (a n) -> p a n", a=2), ACT.Copy).then_inc(*frees(("oi", l, hh, tt)))
                sc.wait_ge(*made("oc_sum", (l, 1)))
                sc.wait_ge(*made("gate_used", (l, gates[0] - 1)))
                for c in range(BT):
                    if c >= 2:
                        sc.wait_ge(*full(("hn", l, f"oc{c - 2}")))
                    nc.scalar.activation(gsb[:, c % 2, :], oBr[2][:, c, :], ACT.Square).then_inc(*signal("square", (f"oc{c}", l, 0)))
                    root(("hn", l, f"oc{c}"), 1.0 / HD, "oc")
                for c in range(BT):
                    sc.wait_ge(*full(("gc", l, c)))
                    ps = held(("gc", l, c))
                    nc.scalar.activation(Fg[:, c, :], ps[:, 0:T], ACT.Silu).then_inc(*frees(("gc", l, c)))
                gates[0] = 0
                sc.wait_ge(*made("oc_gated", (l, BT - 1)))
                sc.wait_ge(*full(("hn", l, "oc3")))
                for j in range(KT):
                    sc.wait_ge(*full(("g", l, 2, j)))
                    ps = held(("g", l, 2, j))
                    if j >= GATES:
                        sc.wait_ge(*made("gate_used", (l, "c", j - GATES)))
                    nc.scalar.activation(gsb[:, j % GATES, :], ps[:, 0:T], ACT.Sigmoid).then_inc(*frees(("g", l, 2, j)))

                sc.wait_ge(*full(("out", l, KT - 1)))
                squares_x(l, 2)
                sc.wait_ge(*made("glog", l))
                nc.scalar.activation(rt[:, 128:128 + TT * NG], rt[:, 112:112 + TT * NG], ACT.Exp).then_inc(*signal("gexp", l))
                sc.wait_ge(*made("ediff", l))
                nc.scalar.activation(rt[:, 144:144 + TT], rt[:, 140:140 + TT], ACT.Exp).then_inc(*signal("eexp", l))
                for e in range(NE):
                    for f in range(FT):
                        sc.wait_ge(*full(("eg", l, e, f)))
                        ps = held(("eg", l, e, f))
                        if e:
                            sc.wait_ge(*made("act", (l, e - 1, f)))
                        nc.scalar.activation(hg4[:, f, :], ps[:, 0:T], ACT.Silu).then_inc(*frees(("eg", l, e, f)))
                    if e == 0:
                        sc.wait_ge(*full(("cT", l)))
                        ps = held(("cT", l))
                        nc.scalar.activation(combT[0:NE, :], ps[0:NE, 0:T], ACT.Copy).then_inc(*frees(("cT", l)))
                    sc.wait_ge(*full(("cb", l, e)))
                    ps = held(("cb", l, e))
                    if e >= 2:
                        sc.wait_ge(*made("act", (l, e - 2, FT - 1)))
                    nc.scalar.activation(cb[:, e % 2, :], ps[:, 0:T], ACT.Copy).then_inc(*frees(("cb", l, e)))
            squares_x(DEPTH, 1)

        @block.vector
        def _(ve):
            V = nc.vector
            steps = [0]

            def step(ins):
                ins.then_inc(*signal("dve_step", steps[0]))
                steps[0] += 1
                ve.wait_ge(sem("dve_step"), steps[0])

            nrec = [0]

            def rstd(bkey):
                s = nrec[0] % 3
                nrec[0] += 1
                ve.wait_ge(*freed_by(bkey))
                step(V.reciprocal(std[:, s, :], std[:, s, :]))
                return std[:, s, :]

            def std_used():
                tally.also("std_used", nrec[0] - 1)

            def modulation(l, i):
                ve.wait_ge(*full(("mod", l, i)))
                ps = held(("mod", l, i))
                V.tensor_tensor(mod[:, l, 4 * i:4 * i + 4, :], ps[:, 0:8].rearrange("p (c g) -> p c g", g=2),
                                      par[:, l, BM + 4 * i:BM + 4 * i + 4].unsqueeze(2).broadcast_to([P, 4, 2]), ALU.add).then_inc(*frees(("mod", l, i)))

            def norm(l, which):
                sh, n0 = (0, N1) if which == 1 else (3 * KT, N2)
                ve.wait_ge(*freed_by(("mod", l, NMOD - 1)))
                step(V.scalar_tensor_tensor(gain[:, which - 1, :, :], mod[:, l, sh + KT:sh + 2 * KT, :], 1.0,
                                            par[:, l, n0:n0 + KT].unsqueeze(2).broadcast_to([P, KT, 2]), ALU.add, ALU.mult))
                r = rstd(("n", l, which))
                ve.wait_ge(*full(("n", l, which)))
                for k in range(KT):
                    step(V.tensor_tensor(tmp[:, k, :], xT[:, k, :], r, ALU.mult))
                    for g, a, b in GROUPS:
                        ins = V.tensor_scalar(hT[:, k, a:b], tmp[:, k, a:b], gain[:, which - 1, k, g:g + 1], mod[:, l, sh + k, g:g + 1],
                                              ALU.mult, ALU.add)
                    ins.then_inc(*signal("h_ready", (l, which, k)))
                std_used()

            def normalise(l, key, dst, name, col, r):
                V.scalar_tensor_tensor(dst, dst, par[:, l, col:col + 1], r, ALU.mult, ALU.mult).then_inc(*signal("normed", (name, l)))
                std_used()

            def rope(dst, work, c, s, half, key):
                step(V.stream_shuffle(work, dst, [(i // (2 * half)) * 2 * half + (i + half) % (2 * half) for i in range(32)]))
                step(V.tensor_tensor(work, work, s, ALU.mult))
                step(V.tensor_tensor(dst, dst, c, ALU.mult))
                V.tensor_tensor(dst, dst, work, ALU.add).then_inc(*signal("roped", key))

            V.memset(eps[:, :], EPS).then_inc(*signal("eps", 0))
            ve.wait_ge(dma_con, 16 * NCDMA)
            step(V.tensor_copy(lmask[:, :, :].rearrange("p n t -> p (n t)"), region[:, REGION - len(LEVELS) * P:]))
            step(V.tensor_tensor(small[:, 0:HEADS], lbl[:, 0, :], lbl[:, 1, :], ALU.max))
            V.tensor_tensor(lbw[:, 0:2, :], lbl[:, :, :], small[:, 0:HEADS].unsqueeze(1).broadcast_to([P, 2, HEADS]), ALU.subtract).then_inc(*signal("lbmax", 0))
            ve.wait_ge(*made("lbexp", 0))
            step(V.tensor_tensor(small[:, 0:HEADS], lbw[:, 2, :], lbw[:, 3, :], ALU.add))
            step(V.reciprocal(small[:, 8:16], small[:, 0:HEADS]))
            step(V.tensor_tensor(lbw[:, 0:2, :], lbw[:, 2:4, :], small[:, 8:16].unsqueeze(1).broadcast_to([P, 2, HEADS]), ALU.mult))
            step(V.tensor_tensor(lb[:, 0, :], lbw[:, 0, :], lbw[:, 0, :], ALU.subtract))
            step(V.tensor_tensor(small[:, 0:HEADS], lbw[:, 0, :], lbw[:, 1, :], ALU.add))
            step(V.tensor_tensor(lb[:, 1, :], small[:, 0:HEADS], lbw[:, 0, :], ALU.subtract))
            step(V.tensor_scalar(oml[:, :, :], lb[:, :, :], -1.0, 1.0, ALU.mult, ALU.add))
            for i in range(NMOD):
                modulation(0, i)

            for l in range(DEPTH):
                norm(l, 1)
                for c in range(BT):
                    r = rstd(("hn", l, f"qa{c}"))
                    normalise(l, None, qA[:, c, :], f"qa{c}", AQ, r)
                    ve.wait_ge(*made("normed", (f"qa{c}", l)))
                    rope(qA[:, c, CTX:T], swp, con[:, CA:CA + LAT], con[:, SA:SA + LAT], 16, (l, c))
                r = rstd(("hn", l, "ka"))
                normalise(l, None, knT[:, :], "ka", AK, r)
                ve.wait_ge(*made("normed", ("ka", l)))
                rope(knT[:, CTX:T], swp, con[:, CA:CA + LAT], con[:, SA:SA + LAT], 16, (l, "ka"))
                rows = slice(NOPE, NOPE + ROPE)
                ve.wait_ge(*freed_by(("kr", l)))
                ve.wait_ge(*made("roped", (l, "ka")))
                rope(krT[rows, CTX:T], swp[rows, :], con[rows, CB:CB + LAT], con[rows, SB:SB + LAT], 8, (l, "kr"))
                r = rstd(("hn", l, "qr"))
                for c in range(QT):
                    normalise(l, None, qr[:, c, :], f"qr{c}", BQ + c, r)
                r = rstd(("hn", l, "kc"))
                for c in range(CT):
                    normalise(l, None, ckvT[:, c, 0:T], f"kc{c}", BK + c, r)
                ve.wait_ge(*freed_by(("qb", l, HEADS - 1)))
                work = tmp[rows, :, :].rearrange("p a t -> p (a t)")[:, 0:HEADS * LAT].rearrange("p (h t) -> p h t", h=HEADS)
                tab = [con[rows, o:o + LAT].unsqueeze(1).broadcast_to([ROPE, HEADS, LAT]) for o in (CB, SB)]
                rope(qB[rows, :, CTX:T], work, tab[0], tab[1], 8, (l, "qb"))

                def maxima(u):
                    br, hp, qt = units[u]
                    c0, c1 = key_cols(qt)
                    for i in range(2):
                        ve.wait_ge(*full(("s", l, u, i)))
                        ps = held(("s", l, u, i))
                        if u >= 2:
                            ve.wait_ge(*freed_by(("s", l, u - 2, i)))
                        step(V.tensor_reduce(nmx[:, u % 2, i:i + 1], ps[:, 0:c1 - c0], AX, ALU.max, negate=True))
                        V.tensor_scalar(nmx[:, u % 2, i:i + 1], nmx[:, u % 2, i:i + 1], (SCALE_A, SCALE_B)[br], None, ALU.mult).then_inc(*signal("negmax", (l, u, i)))

                def softmax(u):
                    br, hp, qt = units[u]
                    n = P * len(key_tiles(qt))
                    for i in range(2):
                        ve.wait_ge(*freed_by(("s", l, u, i)))
                        step(V.reciprocal(rsum[:, u % 2, i:i + 1], rsum[:, u % 2, i:i + 1]))
                        pv = probs[:, u % 2, i, 0:n]
                        V.tensor_scalar(pv, pv, rsum[:, u % 2, i:i + 1], None, ALU.mult).then_inc(*signal("probs", (l, u, i)))

                def turned(u):
                    br, hp, qt = units[u]
                    n = P * len(key_tiles(qt))
                    ve.wait_ge(*full(("t", l, u, 0)))
                    ps = held(("t", l, u, 0))
                    if u >= 2:
                        ve.wait_ge(*full(("o", l, u - 2)))
                    V.tensor_copy(probsT[:, u % 2, 0, 0:n], ps[:, 0:n]).then_inc(*frees(("t", l, u, 0)))

                def outputs(u):
                    br, hp, qt = units[u]
                    ve.wait_ge(*full(("o", l, u)))
                    ps = held(("o", l, u))
                    V.tensor_copy(oBr[br][:, hp, qt * P:(qt + 1) * P], ps[:, 0:P]).then_inc(*frees(("o", l, u)))
                    tally.also("o_ready", (l, br))

                for s in range(len(units) + 2):
                    if s < len(units):
                        maxima(s)
                        softmax(s)
                    if 1 <= s <= len(units):
                        turned(s - 1)
                    if s >= 2:
                        outputs(s - 2)

                ve.wait_ge(dma_out, 16 * (5 * l + 4))
                ve.wait_ge(*made("o_ready", (l, 1)))
                merges = [0]

                def merge(n, j, slot, key):
                    ve.wait_ge(*full(("p", l, n, j)))
                    ps = held(("p", l, n, j))
                    ve.wait_ge(*freed_by(("g", l, n, j)))
                    if n == 0:
                        V.tensor_tensor(tmp[:, j, :], ps[:, 0:T], gsb[:, slot, :], ALU.mult).then_inc(*frees(("p", l, n, j)))
                        tally.also("gate_used", key)
                    else:
                        V.tensor_tensor(prod, ps[:, 0:T], gsb[:, slot, :], ALU.mult).then_inc(*frees(("p", l, n, j)))
                        tally.also("gate_used", key)
                        ve.wait_ge(*freed_by(("p", l, n, j)))
                        V.tensor_tensor(tmp[:, j, :], tmp[:, j, :], prod, ALU.add).then_inc(*signal("merged", (l, n, j)))
                        ve.wait_ge(*made("merged", (l, n, j)))

                def fill_merge(n, j):
                    merge(n, j, merges[0] % GATES, (l, merges[0]))
                    merges[0] += 1

                ve.wait_ge(*made("zeroed", l))
                for hh in range(2):
                    for c in range(4):
                        ve.wait_ge(*freed_by(("fb", l, hh, c)))
                        h = 4 * hh + c
                        step(V.tensor_scalar(Fg[:, c, :], Fg[:, c, :], oml[:, l, h:h + 1], lb[:, l, h:h + 1], ALU.mult, ALU.add))
                        step(V.tensor_scalar(Fg[:, c, :], Fg[:, c, :], F_FLOOR, None, ALU.max))
                        V.tensor_scalar(Kg[:, c, :], Fg[:, c, :], -1.0, 1.0, ALU.mult, ALU.add).then_inc(*signal("fk_ready", (l, hh, c)))
                    ve.wait_ge(*made("fk_ready", (l, hh, 3)))
                    ve.wait_ge(*freed_by(("qc", l, hh, 1)))
                    for tt in range(TT):
                        prev = batches[batches.index((hh, tt)) - 1] if (hh, tt) != batches[0] else None
                        todo = list(fill[hh, tt])
                        decays = decay_steps(V, ve, l, hh, tt, prev, slice(0, HD), 1, 0, "f", step)

                        def place(n):
                            key = ("A", l, hh, tt, n)
                            ve.wait_ge(*full(key))
                            ps = held(key)
                            v = ps[:, :].rearrange("p (d t) -> p d t", d=4)
                            if n == 0:
                                if prev:
                                    ve.wait_ge(*full(("oi", l, *prev)))
                                V.tensor_tensor(Am[:, :, :], v, con[:, IDN:IDN + P].unsqueeze(1).broadcast_to([P, 4, P]), ALU.mult).then_inc(*frees(key))
                            else:
                                V.copy_predicated(Am[:, :, :], lmask[:, n - 1, :].unsqueeze(1).broadcast_to([P, 4, P]), v).then_inc(*frees(key))
                            ve.wait_ge(*freed_by(key))

                        next(decays)
                        for n in range(len(LEVELS) + 1):
                            if n < len(LEVELS):
                                next(decays)
                            else:
                                next(decays)
                            place(n)
                            if n in (1, 3) and todo:
                                fill_merge(*todo.pop(0))
                        while todo:
                            fill_merge(*todo.pop(0))
                        key = ("U", l, hh, tt)
                        ve.wait_ge(*full(key))
                        ps = held(key)
                        hs = slice(4 * hh, 4 * hh + 4)
                        v = ps[:, 0:4 * HD].rearrange("p (d n) -> p d n", d=4)
                        if tt == 0:
                            V.tensor_copy(Sout[:, hs, :], v).then_inc(*frees(key))
                            tally.also("sout", (l, hh))
                        else:
                            ve.wait_ge(dma_state, 32 * (l + 1))
                            r, src, dst = (slice(0, HD), 0, 1) if tt == 1 else (slice(HD, P), 1, 0)
                            if tt == 2:
                                ve.wait_ge(*made("kr_b", (l, hh, 2)))
                            for d in range(4):
                                h = 4 * hh + d
                                ins = V.scalar_tensor_tensor(Sin[r, dst, h, :], Sin[r, src, h, :], dec[r, tt, h:h + 1], v[r, d, :], ALU.mult, ALU.add)
                            ins.then_inc(*frees(key))
                            tally.also("s_f" if tt == 1 else "s_b", (l, hh))
                    key = ("oe", l, hh)
                    ve.wait_ge(*full(key))
                    ps = held(key)
                    ve.wait_ge(*freed_by(("oi", l, hh, 1)))
                    ve.wait_ge(*freed_by(("oi", l, hh, 2)))
                    o = oBr[2][:, 2 * hh:2 * hh + 2, CTX:T]
                    V.tensor_tensor(o, o, ps[:, :].rearrange("p (a n) -> p a n", a=2), ALU.add).then_inc(*frees(key))
                    tally.also("oc_sum", (l, hh))
                for c in range(BT):
                    r = rstd(("hn", l, f"oc{c}"))
                    normalise(l, None, oBr[2][:, c, :], f"oc{c}", CO, r)
                for c in range(BT):
                    ve.wait_ge(*freed_by(("gc", l, c)))
                    ve.wait_ge(*made("normed", (f"oc{c}", l)))
                    V.tensor_tensor(oBr[2][:, c, :], oBr[2][:, c, :], Fg[:, c, :], ALU.mult).then_inc(*signal("oc_gated", (l, c)))
                for j in range(KT):
                    merge(2, j, j % GATES, (l, "c", j))

                def residual(src, key, l2, j, chunk, names):
                    for g, a, b in GROUPS:
                        ins = V.scalar_tensor_tensor(xT[:, j, a:b], src[:, a:b], mod[:, l, chunk * KT + j, g:g + 1], xT[:, j, a:b],
                                                     ALU.mult, ALU.add)
                    return ins

                for j in range(KT):
                    ve.wait_ge(*full(("out", l, j)))
                    ps = held(("out", l, j))
                    residual(ps, None, l, j, 2, None).then_inc(*frees(("out", l, j)))
                    tally.also("x_ready", (l, 2, j))

                norm(l, 2)
                ve.wait_ge(dma_out, 16 * (5 * l + 5))
                route(ve, V, l, step)
                for e in range(NE + 1):
                    if e < NE:
                        ve.wait_ge(*freed_by(("cb", l, e)))
                        for f in range(FT):
                            key = ("eu", l, e, f)
                            ve.wait_ge(*full(key))
                            ps = held(key)
                            ve.wait_ge(*freed_by(("eg", l, e, f)))
                            V.tensor_tensor(mt, ps[:, 0:T], hg4[:, f, :], ALU.mult).then_inc(*frees(key))
                            ve.wait_ge(*freed_by(key))
                            if e >= 2:
                                ve.wait_ge(*full(("ed", l, e - 2, KT - 1)))
                            V.tensor_tensor(act[:, e % 2, f, :], mt, cb[:, e % 2, :], ALU.mult).then_inc(*signal("act", (l, e, f)))
                            ve.wait_ge(*made("act", (l, e, f)))
                    if e:
                        for j in range(KT):
                            key = ("ed", l, e - 1, j)
                            ve.wait_ge(*full(key))
                            ps = held(key)
                            if e > 1:
                                ve.wait_ge(*freed_by(("ed", l, e - 2, j)))
                                ins = V.tensor_tensor(Y[:, j, :], Y[:, j, :], ps[:, 0:T], ALU.add)
                            else:
                                ins = V.tensor_copy(Y[:, j, :], ps[:, 0:T])
                            ins.then_inc(*frees(key))
                        if l + 1 < DEPTH and e <= NMOD:
                            modulation(l + 1, e - 1)
                for j in range(KT):
                    ve.wait_ge(*freed_by(("ed", l, NE - 1, j)))
                    residual(Y[:, j, :], None, l, j, 5, None).then_inc(*signal("x_ready", (l + 1, 1, j)))

            r = rstd(("n", DEPTH, 1))
            ve.wait_ge(*full(("n", DEPTH, 1)))
            for k in range(KT):
                V.scalar_tensor_tensor(hT[:, k, :], xT[:, k, :], fing[:, k:k + 1], r, ALU.mult, ALU.mult).then_inc(*signal("y_ready", k))

        @block.gpsimd
        def _(po):
            G = nc.gpsimd
            steps = [0]

            def step(ins):
                ins.then_inc(*signal("pool_step", steps[0]))
                steps[0] += 1
                po.wait_ge(sem("pool_step"), steps[0])

            rows = slice(NOPE, NOPE + ROPE)
            for l in range(DEPTH):
                if l:
                    po.wait_ge(*made("x_ready", (l, 1, KT - 1)))
                po.dma_start(keysA[:, :, T:KEYS], A["kcT"][l]).then_inc(dma_cache, 16)
                po.dma_start(vA[:, 3, :], A["vc"][l]).then_inc(dma_cache, 16)
                po.dma_start(ckvT[:, :, T:KEYS], A["ckvcT"][l]).then_inc(dma_cache, 16)
                po.dma_start(krT[rows, T:KEYS], A["krcT"][l]).then_inc(dma_cache, 16)
                po.wait_ge(dma_cache, 16 * NCACHE * (l + 1))
                po.wait_ge(*made("roped", (l, "kr")))
                G.tensor_copy(keysB[rows, :, :], krT[rows, :].unsqueeze(1).broadcast_to([ROPE, HEADS, KEYS])).then_inc(*signal("kr_copied", l))
                po.wait_ge(*made("o_ready", (l, 1)))
                po.wait_ge(dma_out, 16 * (5 * l + 4))
                po.dma_start(Sin[0:HD, 0, :, :], A["s0"][l, 0:HD]).then_inc(dma_state, 16)
                po.dma_start(Sin[HD:P, 1, :, :], A["s0"][l, HD:P]).then_inc(dma_state, 16)
                po.wait_ge(*made("kr_copied", l))
                for i in range(len(LEVELS)):
                    G.memset(Ql[i], 0.0)
                    ins = G.memset(Kl[i], 0.0)
                ins.then_inc(*signal("zeroed", l))
                po.wait_ge(*made("zeroed", l))
                for hh, tt in batches:
                    prev = batches[batches.index((hh, tt)) - 1] if (hh, tt) != batches[0] else None
                    po.wait_ge(*made("fk_ready", (l, hh, 3)))
                    po.wait_ge(*freed_by(("qc", l, hh, 1)))
                    for _ in decay_steps(G, po, l, hh, tt, prev, slice(HD, P), 0, 1, "b", step):
                        pass

        @block.sync
        def _(sp):
            for dst, name in ((xT[:, :, :], "xT"), (con[:, :], "con"), (par[:, :, :], "par"), (cv[:, :, :], "cv"),
                              (lbl[:, :, :], "lbl"), (fing[:, :], "fing"), (region[:, REGION - len(LEVELS) * P:], "lmask")):
                sp.dma_start(dst, A[name]).then_inc(dma_con, 16)

            for i, (l, name, size) in enumerate(order):
                if i >= RING:
                    sp.wait_ge(*full(closing[i - RING]))
                sp.dma_start(slabs[:, i % RING, 0:size], A["W"][i, :, 0:size]).then_inc(dma_slab[i % RING], 16)
                if name == "br0":
                    sp.wait_ge(*made("normed", ("ka", l)))
                    sp.dma_start(A["new_k"][l], knT[:, 0:CTX]).then_inc(dma_out, 16)
                    sp.wait_ge(*freed_by(("va", l)))
                    sp.dma_start(A["new_v"][l], vA[:, 0, :]).then_inc(dma_out, 16)
                    sp.wait_ge(*made("normed", ("kc1", l)))
                    sp.dma_start(A["new_ckv"][l], ckvT[:, :, 0:CTX]).then_inc(dma_out, 16)
                    sp.wait_ge(*freed_by(("kr", l)))
                    sp.dma_start(A["new_kr"][l], krT[NOPE:NOPE + ROPE, 0:CTX]).then_inc(dma_out, 16)
                if name == "o1":
                    sp.wait_ge(*made("sout", (l, 1)))
                    sp.dma_start(A["new_s"][l], Sout[:, :, :]).then_inc(dma_out, 16)
            sp.wait_ge(*made("y_ready", KT - 1))
            sp.dma_start(A["y"], hT[:, :, :]).then_inc(dma_out, 16)
            sp.wait_ge(dma_out, 16 * (5 * DEPTH + 1))

    return tally.here


_IN = ["W", "xT", "con", "lmask", "par", "lbl", "fing", "cv", "kcT", "vc", "ckvcT", "krcT", "s0"]
_OUT = [("y", (P, KT, T)), ("new_k", (DEPTH, P, CTX)), ("new_v", (DEPTH, CTX, P)), ("new_ckv", (DEPTH, P, CT, CTX)),
        ("new_kr", (DEPTH, ROPE, CTX)), ("new_s", (DEPTH, P, HEADS, HD))]


def constants():
    con = np.zeros((P, NCON), np.float32)
    p = np.arange(P)
    con[:, ONES:ONES + P] = 1.0
    con[:, BLK:BLK + P] = (p[:, None] // HD == p[None, :] // HD)
    con[:, IDN:IDN + P] = np.eye(P)
    row, col = np.arange(LAT) // GRID_W, np.arange(LAT) % GRID_W

    def rotary(width, d):
        half = width // 2
        inv = (np.float32(10000.0) ** (-np.arange(0, half, 2, dtype=np.float32) / np.float32(half))).astype(np.float32)
        pos = np.where((d // half == 0)[:, None], row[None, :], col[None, :]).astype(np.float32)
        ang = pos * inv[d % (half // 2)][:, None]
        sign = np.where(d % half < half // 2, -1.0, 1.0)[:, None]
        return np.cos(ang), np.sin(ang) * sign

    con[:, CA:CA + LAT], con[:, SA:SA + LAT] = rotary(HD, p % HD)
    con[NOPE:QB_W, CB:CB + LAT], con[NOPE:QB_W, SB:SB + LAT] = rotary(ROPE, np.arange(ROPE))
    mask = np.zeros((P, len(LEVELS), P), np.float32)
    for n, b in enumerate(LEVELS):
        mask[:, n] = (p[:, None] // (2 * b) == p[None, :] // (2 * b)) & (p[:, None] // b != p[None, :] // b)
    return con, mask.reshape(P, -1)


def lay_out(inputs):
    x = {k: np.asarray(v) for k, v in inputs.items()}
    f = np.float32

    def tiles(w):
        K, N = w.shape
        return w.reshape(K // P, P, N // P, P).transpose(1, 2, 0, 3).reshape(P, -1)

    def rows(w):
        K, N = w.shape
        return w.reshape(K // P, P, N).transpose(1, 0, 2).reshape(P, -1)

    order = slab_order()
    W = np.zeros((len(order), P, SLAB), f)
    widths = (BW, KV_A * HD, KV_A * HD, Q_RANK, KV_RANK, ROPE, BW, BW, BW, BW, BW, N_BRANCH * D)
    cut = np.cumsum((0,) + widths)
    for i, (l, name, size) in enumerate(order):
        w_in = x["w_in"][l]
        qa, ka, va, qra, kva, kra, ff, fb, qc, ic, gc, gp = [w_in[:, cut[n]:cut[n + 1]] for n in range(12)]
        if name[0] == "m":
            n = int(name[1:])
            s = tiles(x["w_mod"][l][:, n * 512:(n + 1) * 512])
        elif name == "qa":
            s = tiles(qa)
        elif name == "kv":
            s = tiles(np.concatenate([ka, va, kra, np.zeros((D, P - ROPE), f), qra[:, 0:P]], 1))
        elif name == "qr":
            s = tiles(np.concatenate([qra[:, P:], kva], 1))
        elif name == "bwq":
            s = rows(x["b_wq"][l])
        elif name == "bwkv":
            w = x["b_wkv"][l].reshape(KV_RANK, HEADS, 2 * HD)
            s = np.concatenate([rows(w[:, :, :HD].reshape(KV_RANK, BW)), rows(w[:, :, HD:].reshape(KV_RANK, BW))], 1)
        elif name == "ic":
            s = rows(ic)
        elif name in ("fb0", "fb1"):
            w = np.stack([ff.reshape(D, HEADS, HD), fb.reshape(D, HEADS, HD)], 2).reshape(D, 2 * BW)
            s = tiles(w[:, int(name[2]) * BW:(int(name[2]) + 1) * BW])
        elif name in ("qc0", "qc1"):
            s = tiles(qc[:, int(name[2]) * 256:(int(name[2]) + 1) * 256])
        elif name == "gc":
            s = tiles(gc)
        elif name[:2] == "br":
            s = tiles(x["w_branch"][l, int(name[2])])
        elif name[0] == "g":
            n = int(name[1]) * D + int(name[2]) * BW
            s = tiles(gp[:, n:n + BW])
        elif name[:2] == "eg":
            s = tiles(x["e_gate"][l, int(name[2:])])
        elif name[:2] == "eu":
            s = tiles(x["e_up"][l, int(name[2:])])
        elif name[:2] == "ed":
            s = tiles(x["e_down"][l, int(name[2:])])
        else:
            s = tiles(x["w_out"][l][:, int(name[1]) * 512:(int(name[1]) + 1) * 512])
        assert s.shape[1] == size, (name, s.shape, size)
        W[i, :, :size] = s

    col = lambda v: v.reshape(-1, P).T
    twice = lambda v: np.concatenate([v, v])[:, None]
    par = np.stack([np.concatenate([
        col(x["norm1_g"][l]), col(x["norm2_g"][l]), col(x["b_mod"][l]), twice(x["a_qnorm"][l]), twice(x["a_knorm"][l]),
        col(x["b_qnorm"][l]), col(x["b_kvnorm"][l]), twice(x["c_onorm"][l]),
        np.broadcast_to(np.concatenate([x["r_group_b"][l], x["r_expert_b"][l]])[None, :], (P, NG + NE)),
        rows(np.concatenate([x["r_group_w"][l], x["r_expert_w"][l]], 1))], 1) for l in range(DEPTH)], 1)
    con, mask = constants()
    tok = np.concatenate([x["x_prompt"][0], x["x_sample"][0]], 0)
    kc = x["cache_gqa_k"][0].transpose(0, 3, 2, 1)
    return {
        "W": W, "xT": tok.T.reshape(KT, P, T).transpose(1, 0, 2), "con": con, "lmask": mask, "par": par,
        "lbl": x["c_lb_logits"].reshape(DEPTH, 2, HEADS, HD).transpose(1, 3, 0, 2).reshape(P, DEPTH, HEADS),
        "fing": col(x["final_g"]), "cv": np.stack([col(x["c_ctx"]), col(x["c"][0])], 2),
        "kcT": np.concatenate([kc, kc], 1), "vc": x["cache_gqa_v"][0].reshape(DEPTH, PAST, KV_A * HD),
        "ckvcT": x["cache_mla_ckv"][0].transpose(0, 2, 1).reshape(DEPTH, CT, P, PAST).transpose(0, 2, 1, 3),
        "krcT": x["cache_mla_krope"][0].transpose(0, 2, 1),
        "s0": x["state_hgrn"][0].transpose(0, 1, 3, 2, 4).reshape(DEPTH, P, HEADS, HD),
    }


def kernel(**inputs):
    import concourse.bacc as bacc
    from concourse.bass_utils import run_bass_kernel_spmd

    arrays = {k: np.ascontiguousarray(v) for k, v in lay_out(inputs).items()}

    def build(known):
        nc = bacc.Bacc("TRN2", target_bir_lowering=False, num_devices=1)
        A = {n: nc.dram_tensor(f"in_{n}", arrays[n].shape, mybir.dt.from_np(arrays[n].dtype), kind="ExternalInput").ap() for n in _IN}
        for n, shape in _OUT:
            A[n] = nc.dram_tensor(f"out_{n}", shape, F32, kind="ExternalOutput").ap()
        return nc, program(nc, A, known)

    _, found = build({})
    nc, _ = build(found)
    r = run_bass_kernel_spmd(nc, [{f"in_{n}": arrays[n] for n in _IN}], core_ids=[0])
    o = {n: r.results[0][f"out_{n}"] for n, _ in _OUT}
    y = o["y"].transpose(2, 1, 0).reshape(T, D)
    return (y[None, :CTX], y[None, CTX:],
            o["new_k"].reshape(DEPTH, KV_A, HD, CTX).transpose(0, 3, 1, 2)[None],
            o["new_v"].reshape(DEPTH, CTX, KV_A, HD)[None],
            o["new_ckv"].transpose(0, 3, 2, 1).reshape(DEPTH, CTX, KV_RANK)[None],
            o["new_kr"].transpose(0, 2, 1)[None],
            o["new_s"].reshape(DEPTH, 2, HD, HEADS, HD).transpose(0, 1, 3, 2, 4)[None])
```

```python
from contextlib import ExitStack

import numpy as np

import concourse.bass as bass
from concourse import mybir

F32 = mybir.dt.float32
U8 = mybir.dt.uint8
I32 = mybir.dt.int32
F32R = mybir.dt.float32r
ALU = mybir.AluOpType
ACT = mybir.ActivationFunctionType
AX = mybir.AxisListType.X

P = 128
D = 1024
KT = D // P
DEPTH = 2
CTX, LAT, PAST = 128, 256, 128
T = CTX + LAT
TT = T // P
KEYS = T + PAST
GRID_W = 64
EPS = 1e-6
F_FLOOR = 1e-30
HD = 64
HEADS = 8
KV_A = 2
Q_RANK, KV_RANK = 384, 256
NOPE, ROPE = 64, 32
QB_W = NOPE + ROPE
QT, CT = Q_RANK // P, KV_RANK // P
BW = 512
BT = BW // P
N_BRANCH = 3
NCDMA = 7
NCACHE = 4
NG, EG = 4, 4
NE = NG * EG
SLOTS = 128
UNITS = 6
UNIT = 2048
SPLITS = 3
FE = 512
FT = FE // P
SLAB = 4096
RING = 4
GATES = 2
REGION = 19096
BANKS = 8
MODT = 6 * KT
LEVELS = [1 << i for i in range(7)]
GROUPS = ((0, 0, CTX), (1, CTX, T))
SCALE_A = HD ** -0.5
SCALE_B = QB_W ** -0.5
BIG = 1e30

N1, N2, BM, AQ, AK, BQ, BK, CO, RB, RW = np.cumsum([0, KT, KT, MODT, 1, 1, QT, CT, 1, NG + NE]).tolist()
NPAR = RW + KT * (NG + NE)
ONES, BLK, IDN, TRI, IOTA, CA, SA, CB, SB = np.cumsum([0, P, P, P, P, P, LAT, LAT, LAT]).tolist()
NCON = SB + LAT

MIXER = ([("qa", SLAB), ("kv", SLAB), ("qr", SLAB), ("bwq", QT * HEADS * QB_W), ("bwkv", CT * HEADS * 2 * HD), ("ic", SLAB),
          ("fb0", SLAB), ("qc0", SLAB // 2), ("br0", SLAB), ("g00", SLAB), ("g01", SLAB),
          ("fb1", SLAB), ("qc1", SLAB // 2), ("br1", SLAB), ("g10", SLAB), ("g11", SLAB),
          ("gc", SLAB), ("br2", SLAB), ("g20", SLAB), ("g21", SLAB), ("o0", SLAB), ("o1", SLAB)])
NMOD = MODT // 4


def slab_order():
    out = [(0, f"m{i}", SLAB) for i in range(NMOD)]
    for l in range(DEPTH):
        out += [(l, n, s) for n, s in MIXER]
        for e in range(NE):
            out += [(l, f"eg{e}", SLAB), (l, f"eu{e}", SLAB), (l, f"ed{e}", SLAB)]
            if l + 1 < DEPTH and e < NMOD:
                out.append((l + 1, f"m{e}", SLAB))
    return out


class Tally:

    def __init__(self, known):
        self.known, self.here, self.count, self.last = known, {}, {}, None

    def next(self, name, key):
        self.count[name] = self.count.get(name, 0) + 1
        self.last = self.here[name, key] = (name, self.count[name])

    def also(self, name, key):
        self.here[name, key] = self.last

    def of(self, name, key):
        return self.known.get((name, key), ("dummy", 1)) if not self.known else self.known[name, key]


def program(nc, A, known):
    tally = Tally(known)
    order = slab_order()
    held_by_bank, closing = {}, {}

    with ExitStack() as ctx:
        def sb(name, shape, dt=F32):
            return ctx.enter_context(nc.sbuf_tensor("sb_" + name, shape, dt))

        sems = {}

        def sem(name):
            if name not in sems:
                sems[name] = ctx.enter_context(nc.semaphore(name))
            return sems[name]

        def signal(name, key):
            tally.next(name, key)
            return sem(name), 1

        def made(name, key):
            s, n = tally.of(name, key)
            return sem(s), n

        def made_now(name):
            return sem(name), tally.count[name]

        unit_read = {}
        index_of = {(l, n): i for i, (l, n, _) in enumerate(order)}

        psum = [ctx.enter_context(nc.psum_tensor(f"bank{b}", [P, 512], F32)) for b in range(BANKS)]
        way = [""]
        uses = {}

        def take(key):
            w = way[0]
            b, n = uses.get(w, 0) % BANKS, uses.get(w, 0) // BANKS
            uses[w] = uses.get(w, 0) + 1
            held_by_bank[key] = (w, b, n)
            return psum[b], (sem(f"bank_free{w}{b}"), n) if n else None

        def readers(w):
            total = uses.get(w, 0)
            return [(sem(f"bank_free{w}{b}"), (total - b + BANKS - 1) // BANKS) for b in range(BANKS) if total > b]

        def held(key):
            return psum[held_by_bank[key][1]]

        def fills(key):
            w, b, n = held_by_bank[key]
            return sem(f"bank_full{w}{b}"), 1

        def full(key):
            w, b, n = held_by_bank[key]
            return sem(f"bank_full{w}{b}"), n + 1

        def frees(key):
            w, b, n = held_by_bank[key]
            tally.last = (f"bank_free{w}{b}", n + 1)
            return sem(f"bank_free{w}{b}"), 1

        def freed_by(key):
            w, b, n = held_by_bank[key]
            return sem(f"bank_free{w}{b}"), n + 1

        con = sb("con", [P, NCON])
        lmask = sb("lmask", [P, len(LEVELS), P], U8)
        par = sb("par", [P, DEPTH, NPAR])
        lbl = sb("lbl", [P, DEPTH, HEADS])
        lbw = sb("lbw", [P, 4, HEADS])
        lb = sb("lb", [P, DEPTH, HEADS])
        oml = sb("oml", [P, DEPTH, HEADS])
        fing = sb("fing", [P, KT])
        cv = sb("cv", [P, KT, 2])
        eps = sb("eps", [P, 1])
        mod = sb("mod", [P, DEPTH, MODT, 2])
        gain = sb("gain", [P, 2, KT, 2])
        xT = sb("xT", [P, KT, T])
        tmp = sb("tmp", [P, KT, T])
        slabs = sb("slabs", [P, RING, SLAB])
        flag = sb("flag", [P, 1], I32)
        small = sb("small", [P, 16])

        base = nc.sbuf_base + (-nc.sbuf_base) % 32
        arena = sb("arena", [P, 3 * T + (KT + N_BRANCH * BT) * T + REGION])
        std = arena[:, 0:3 * T].rearrange("p (a t) -> p a t", a=3)
        hT = arena[:, 3 * T:(3 + KT) * T].rearrange("p (a t) -> p a t", a=KT)
        o0 = (3 + KT) * T
        oBr = [arena[:, o0 + n * BT * T:o0 + (n + 1) * BT * T].rearrange("p (a t) -> p a t", a=BT) for n in range(N_BRANCH)]
        r0 = o0 + N_BRANCH * BT * T
        region = arena[:, r0:r0 + REGION]
        at = [0]

        def part(shape, dt=F32):
            n = int(np.prod(shape[1:]))
            v = region[0:shape[0], at[0]:at[0] + n]
            at[0] += n
            assert at[0] <= REGION, at[0]
            names = "abcd"[:len(shape) - 1]
            if len(shape) > 2:
                v = v.rearrange(f"p ({' '.join(names)}) -> p {' '.join(names)}", **{c: s for c, s in zip(names, shape[1:])})
            return v

        qA = part([P, BT, T])
        knT = part([P, T])
        keysA = part([P, KV_A, KEYS])
        vA = part([P, 4, P])
        qr = part([P, QT, T])
        ckvT = part([P, CT, KEYS])
        krT = part([P, KEYS])
        qB = part([P, HEADS, T])
        keysB = part([P, HEADS, KEYS])
        vB = part([P, 4, BW])
        swp = part([P, LAT])
        nmx = part([P, 2, 2])
        rsum = part([P, 2, 2])
        pr = tmp[:, 0:2, :].rearrange("p a t -> p (a t)").rearrange("p (a t) -> p a t", a=2)
        probs = tmp[:, 0:4, :].rearrange("p (u i) t -> p u i t", u=2)
        probsT = tmp[:, 4:8, :].rearrange("p (u i) t -> p u i t", u=2)
        at[0] = 0
        Fg = part([P, 4, T])
        Kg = part([P, 4, T])
        qd = part([P, 4, T])
        vC = part([P, TT, BW])
        Ql = [part([P, 4, P]) for _ in LEVELS]
        Kl = [part([P, 4, P]) for _ in LEVELS]
        Pp = part([P, 4, P])
        Rr = part([P, 4, P])
        KRt = part([P, 4, P])
        QP = part([P, 2, 4, P])
        Am = part([P, 4, P])
        Sin = part([P, 2, HEADS, HD])
        Sout = part([P, HEADS, HD])
        dec = part([P, TT, HEADS])
        gsb = part([P, GATES, T])
        prod = part([P, T])
        at[0] = 0
        act = part([P, 2, FT, T])
        hg4 = part([P, FT, T])
        cb = part([P, 2, T])
        mt = part([P, T])
        combT = part([P, T])
        at[0] = REGION - 400
        rt = part([P, 400])
        def over(name, shape, offset, dt=F32R):
            return nc.alloc_sbuf_tensor_at("sb_" + name, shape, dt, offset=base + 4 * offset)

        htok = over("htok", [P, 2, TT, D], r0)
        split = over("split", [P, SPLITS, 2, UNIT], r0 + 2 * TT * D)
        wsl = over("wsl", [P, 2], r0 + 2 * TT * D + SPLITS * 2 * UNIT, F32)
        hg = over("hg", [P, 2, 2, KT, SLOTS], 0)
        actT = over("actT", [P, 2, FT, SLOTS], 4096)
        yg = over("yg", [P, 2, D], 5120)
        pick = over("pick", [P, TT, SLOTS], 7168)
        back = [over("back0", [P, T], 7552), over("back1", [P, T], 8448)]
        ag = over("ag", [P, FE], 7936, F32)

        dma_con = sem("dma_con")
        dma_cache = sem("dma_cache")
        dma_state = sem("dma_state")
        dma_out = sem("dma_out")
        dma_slab = [sem(f"dma_slab{i}") for i in range(RING)]
        outs = [0]

        def W(l, name):
            i = [(a, b) for a, b, _ in order].index((l, name))
            return slabs[:, i % RING, :]

        def tile(l, name, c, k=KT):
            return W(l, name)[:, c * k * P:(c + 1) * k * P].rearrange("p (k n) -> p k n", k=k)

        units = [(br, hp, qt) for br in range(2) for hp in range(4) for qt in range(TT)]
        key_cols = lambda qt: (0, CTX) if qt == 0 else (CTX, KEYS)
        key_tiles = lambda qt: [0] if qt == 0 else [1, 2, 3]
        batches = [(hh, tt) for hh in range(2) for tt in range(TT)]
        fill = {(hh, tt): [(hh, j) for j in range(3 * tt, min(3 * tt + 3, KT))] for hh, tt in batches}

        def decay_steps(E, eng, l, hh, tt, prev, r, qs, ks, tag, step):
            cols = slice(tt * P, (tt + 1) * P)
            if prev:
                eng.wait_ge(*full(("kt", l, *prev)))
            E.memset(Rr[r], 1.0)
            step(E.tensor_copy(Pp[r], Fg[r, :, cols]))
            yield
            for n, b in enumerate(LEVELS):
                def halves(x, s, i=None):
                    v = x.rearrange("p a (m s b) -> p a m s b", s=2, b=b)[:, :, :, s, :]
                    if i is None:
                        return v
                    return v[:, :, :, i:i + 1].broadcast_to([HD, 4, P // (2 * b), b])

                edge = b - 1 if qs == 1 else 0
                if prev:
                    eng.wait_ge(*full(("A", l, *prev, n + 1)))
                E.tensor_tensor(halves(Ql[n][r], qs), halves(qd[r, :, cols], qs), halves(Pp[r], qs), ALU.mult)
                E.tensor_tensor(halves(Kl[n][r], ks), halves(Kg[r, :, cols], ks), halves(Rr[r], ks), ALU.mult).then_inc(*signal(f"lev_{tag}", (l, hh, tt, n)))
                eng.wait_ge(*made(f"lev_{tag}", (l, hh, tt, n)))
                step(E.tensor_tensor(halves(Rr[r], ks), halves(Rr[r], ks), halves(Pp[r], qs, edge), ALU.mult))
                step(E.tensor_tensor(halves(Pp[r], qs), halves(Pp[r], qs), halves(Pp[r], ks, edge), ALU.mult))
                yield
            last = P - 1 if qs == 1 else 0
            E.tensor_copy(dec[r, tt, 4 * hh:4 * hh + 4], Pp[r, :, last])
            if tt:
                if hh:
                    eng.wait_ge(*full(("oe", l, 0)))
                E.tensor_tensor(QP[r, tt - 1], qd[r, :, cols], Pp[r], ALU.mult)
            E.tensor_tensor(Rr[r], Rr[r], Kg[r, :, cols], ALU.mult).then_inc(*signal(f"kr_{tag}", (l, hh, tt)))
            if tt == 2:
                tally.also(f"qp_{tag}", (l, hh))
            yield

        def route(ve, V, l, step):
            L = rt[:, 0:TT * (NG + NE)].rearrange("p (t n) -> p t n", t=TT)
            comb = rt[:, 64:64 + TT * NE].rearrange("p (t g e) -> p t g e", t=TT, g=NG)
            gx = rt[:, 112:124].rearrange("p (t n) -> p t n", t=TT)
            ge = rt[:, 128:140].rearrange("p (t n) -> p t n", t=TT)
            ed, ee = rt[:, 140:143], rt[:, 144:147]
            w4 = [rt[:, 160 + 12 * i:172 + 12 * i].rearrange("p (t n) -> p t n", t=TT) for i in range(8)]
            w1 = [rt[:, 280 + 4 * i:283 + 4 * i] for i in range(12)]
            w16 = rt[:, 340:388].rearrange("p (t g e) -> p t g e", t=TT, g=NG)
            pref = rt[:, 392:396]
            b4 = lambda v: v.unsqueeze(2).broadcast_to([P, TT, 4])

            def first_of(out, eq, work, m):
                step(V.tensor_tensor(work, eq, pref.unsqueeze(1).broadcast_to([P, TT, 4]), ALU.mult))
                step(V.tensor_reduce(m, work, AX, ALU.max))
                step(V.tensor_tensor(out, work, b4(m), ALU.is_equal))

            for i in range(4):
                step(V.memset(rt[:, 392 + i:393 + i], float(4 - i)))
            ve.wait_ge(*full(("r", l)))
            ps = held(("r", l))
            V.tensor_tensor(L, ps[:, 0:TT * 32].rearrange("p (t n) -> p t n", t=TT)[:, :, 0:NG + NE],
                                  par[:, l, RB:RB + NG + NE].unsqueeze(1).broadcast_to([P, TT, NG + NE]), ALU.add).then_inc(*frees(("r", l)))
            ve.wait_ge(*freed_by(("r", l)))
            step(V.tensor_reduce(w1[0], L[:, :, 0:NG], AX, ALU.max))
            V.tensor_tensor(gx, L[:, :, 0:NG], b4(w1[0]), ALU.subtract).then_inc(*signal("glog", l))
            step(V.tensor_tensor(w4[0], L[:, :, 0:NG], b4(w1[0]), ALU.is_equal))
            first_of(w4[1], w4[0], w4[2], w1[1])
            step(V.tensor_tensor(w16, L[:, :, NG:NG + NE].rearrange("p t (g e) -> p t g e", g=NG),
                                 w4[1].unsqueeze(3).broadcast_to([P, TT, NG, EG]), ALU.mult))
            step(V.tensor_tensor(w4[3], w16[:, :, 0, :], w16[:, :, 1, :], ALU.add))
            step(V.tensor_tensor(w4[3], w4[3], w16[:, :, 2, :], ALU.add))
            step(V.tensor_tensor(w4[3], w4[3], w16[:, :, 3, :], ALU.add))
            step(V.tensor_reduce(w1[2], w4[3], AX, ALU.max))
            step(V.tensor_tensor(w4[0], w4[3], b4(w1[2]), ALU.is_equal))
            first_of(w4[4], w4[0], w4[2], w1[1])
            step(V.scalar_tensor_tensor(w4[5], w4[4], -BIG, w4[3], ALU.mult, ALU.add))
            step(V.tensor_reduce(w1[3], w4[5], AX, ALU.max))
            V.tensor_tensor(ed, w1[3], w1[2], ALU.subtract).then_inc(*signal("ediff", l))
            step(V.tensor_tensor(w4[0], w4[5], b4(w1[3]), ALU.is_equal))
            first_of(w4[6], w4[0], w4[2], w1[1])
            ve.wait_ge(*made("gexp", l))
            step(V.tensor_reduce(w1[4], ge, AX, ALU.add))
            step(V.reciprocal(w1[5], w1[4]))
            ve.wait_ge(*made("eexp", l))
            step(V.tensor_scalar(w1[6], ee, 1.0, None, ALU.add))
            step(V.reciprocal(w1[7], w1[6]))
            step(V.tensor_tensor(w1[8], w1[7], w1[5], ALU.mult))
            step(V.tensor_tensor(w1[9], w1[8], ee, ALU.mult))
            sel = rt[:, 0:TT * NE].rearrange("p (t g e) -> p t g e", t=TT, g=NG)
            step(V.tensor_tensor(w4[5], w4[4], w4[6], ALU.add))
            V.tensor_tensor(sel, w4[1].unsqueeze(3).broadcast_to([P, TT, NG, EG]), w4[5].unsqueeze(2).broadcast_to([P, TT, NG, EG]),
                            ALU.mult).then_inc(*signal("sel", l))
            step(V.tensor_tensor(w4[4], w4[4], b4(w1[8]), ALU.mult))
            step(V.tensor_tensor(w4[6], w4[6], b4(w1[9]), ALU.mult))
            step(V.tensor_tensor(w4[7], w4[4], w4[6], ALU.add))
            V.tensor_tensor(comb, w4[1].unsqueeze(3).broadcast_to([P, TT, NG, EG]), w4[7].unsqueeze(2).broadcast_to([P, TT, NG, EG]),
                                 ALU.mult).then_inc(*signal("comb", l))

        def expert_unit(l, i):
            e, u = divmod(i, UNITS)
            name = f"{('eg', 'eu', 'ed')[u // 2]}{e}"
            return W(l, name)[:, (u % 2) * UNIT:(u % 2 + 1) * UNIT], index_of[l, name]

        def pe_short(pe, l, cur, slab, modulation):
            W_ = way[0]
            parts = ((0, 0), (0, 1), (1, 0))

            def rows_of_x():
                for t in range(TT):
                    for g in range(2):
                        key = ("ht", l, t, g)
                        ps, reader = take(key)
                        if reader:
                            pe.wait_ge(*reader)
                        for i in range(4):
                            mm = nc.tensor.transpose(ps[:, i * P:(i + 1) * P], hT[:, 4 * g + i, t * P:(t + 1) * P], con[:, IDN:IDN + P])
                        mm.then_inc(*fills(key))

            def gather(e):
                pe.wait_ge(*made("picked" + W_, e))
                for part in range(2):
                    for g in range(2):
                        key = ("ga", l, e, part, g)
                        ps, reader = take(key)
                        if reader:
                            pe.wait_ge(*reader)
                        if e == 0:
                            for t in range(TT):
                                pe.wait_ge(*freed_by(("ht", l, t, g)))
                        for i in range(4):
                            for t in range(TT):
                                mm = nc.tensor.matmul(ps[:, i * SLOTS:(i + 1) * SLOTS], lhsT=htok[:, part, t, (4 * g + i) * P:(4 * g + i + 1) * P],
                                                      rhs=pick[:, t, :], start=(t == 0), stop=(t == TT - 1))
                        mm.then_inc(*fills(key))
                ps, reader = take(("ws", l, e))
                if reader:
                    pe.wait_ge(*reader)
                if e == 0:
                    pe.wait_ge(*made("comb", l))
                for t in range(TT):
                    c = 64 + t * NE + e
                    mm = nc.tensor.matmul(ps[:, 0:1], lhsT=pick[:, t, :].bitcast(F32), rhs=rt[:, c:c + 1], start=(t == 0), stop=(t == TT - 1))
                mm.then_inc(*fills(("ws", l, e)))
                ps, reader = take(("bk", l, e))
                if reader:
                    pe.wait_ge(*reader)
                for t in range(TT):
                    mm = nc.tensor.transpose(ps[:, t * P:(t + 1) * P], pick[:, t, :].bitcast(F32), con[:, IDN:IDN + P])
                mm.then_inc(*fills(("bk", l, e)))

            def up(e):
                for n, name in enumerate(("gt", "up")):
                    key = (name, l, e)
                    ps, reader = take(key)
                    if reader:
                        pe.wait_ge(*reader)
                    if n == 0:
                        for part in range(2):
                            for g in range(2):
                                pe.wait_ge(*freed_by(("ga", l, e, part, g)))
                    for u in range(2):
                        i = UNITS * e + 2 * n + u
                        pe.wait_ge(*made("unit_free", (l, i)))
                        for k in range(4):
                            for a, w in parts:
                                mm = nc.tensor.matmul(ps[:, :], lhsT=hg[:, e % 2, a, 4 * u + k, :], rhs=split[:, i % SPLITS, w, k * FE:(k + 1) * FE],
                                                      start=(u == 0 and k == 0 and (a, w) == (0, 0)), stop=(u == 1 and k == 3 and (a, w) == (1, 0)))
                        if u == 0:
                            mm.then_inc(*signal("unit_used" + W_, i))
                            unit_read[l, i] = made_now("unit_used" + W_)
                        else:
                            mm.then_inc(*fills(key))
                            unit_read[l, i] = full(key)

            def turn(e):
                key = ("aT", l, e)
                ps, reader = take(key)
                pe.wait_ge(*reader)
                pe.wait_ge(*made("gated" + W_, e))
                for f in range(FT):
                    mm = nc.tensor.transpose(ps[:, f * SLOTS:(f + 1) * SLOTS], ag[:, f * P:(f + 1) * P], con[:, IDN:IDN + P])
                mm.then_inc(*fills(key))

            def down(e):
                ps = []
                for n in range(2):
                    b, reader = take(("y", l, e, n))
                    pe.wait_ge(*reader)
                    ps.append(b)
                pe.wait_ge(*freed_by(("aT", l, e)))
                for u in range(2):
                    i = UNITS * e + 4 + u
                    pe.wait_ge(*made("unit_free", (l, i)))
                    for k in range(2):
                        for n in range(2):
                            for a, w in parts:
                                o = k * D + n * 512
                                mm = nc.tensor.matmul(ps[n][:, :], lhsT=actT[:, a, 2 * u + k, :], rhs=split[:, i % SPLITS, w, o:o + 512],
                                                      start=(u == 0 and k == 0 and (a, w) == (0, 0)), stop=(u == 1 and k == 1 and (a, w) == (1, 0)))
                            if u == 1 and k == 1:
                                mm.then_inc(*fills(("y", l, e, n)))
                    if u == 0:
                        mm.then_inc(*signal("unit_used" + W_, i))
                        unit_read[l, i] = made_now("unit_used" + W_)
                    else:
                        unit_read[l, i] = full(("y", l, e, 1))

            def scatter(e):
                for j in range(KT):
                    key = ("sc", l, e, j)
                    ps, reader = take(key)
                    pe.wait_ge(*reader)
                    if j == 0:
                        pe.wait_ge(*freed_by(("bk", l, e)))
                    if j % 4 == 0:
                        pe.wait_ge(*freed_by(("y", l, e, j // 4)))
                    for a in range(2):
                        mm = nc.tensor.matmul(ps[:, 0:T], lhsT=yg[:, a, j * P:(j + 1) * P], rhs=back[e % 2][:, :], start=(a == 0), stop=(a == 1))
                    mm.then_inc(*fills(key))

            rows_of_x()
            gather(0)
            for e in range(NE):
                up(e)
                if e:
                    scatter(e - 1)
                if e + 1 < NE:
                    gather(e + 1)
                turn(e)
                down(e)
                if l + 1 < DEPTH and e < NMOD:
                    cur[0] = index_of[l, f"ed{e}"]
                    modulation(l + 1, e, W_)
            scatter(NE - 1)
            cur[0] = index_of[l, f"ed{NE - 1}"]

        def act_short(sc, l):
            W_ = f"s{l}_"

            def high(i):
                raw, s = expert_unit(l, i)
                sc.wait_ge(dma_slab[s % RING], 16 * (s // RING + 1))
                if i >= SPLITS:
                    sc.wait_ge(*unit_read[l, i - SPLITS])
                nc.scalar.activation(split[:, i % SPLITS, 0, :], raw, ACT.Copy).then_inc(*signal("high" + W_, i))

            def gathered(e):
                for g in range(2):
                    key = ("ga", l, e, 0, g)
                    sc.wait_ge(*full(key))
                    nc.scalar.activation(hg[:, e % 2, 0, 4 * g:4 * g + 4, :].rearrange("p k n -> p (k n)"), held(key)[:, :],
                                         ACT.Copy).then_inc(*frees(key))
                key = ("ws", l, e)
                sc.wait_ge(*full(key))
                nc.scalar.activation(wsl[:, e % 2:e % 2 + 1], held(key)[:, 0:1], ACT.Copy).then_inc(*frees(key))
                key = ("bk", l, e)
                sc.wait_ge(*full(key))
                nc.scalar.activation(back[e % 2][:, :], held(key)[:, 0:T], ACT.Copy).then_inc(*frees(key))

            for t in range(TT):
                for g in range(2):
                    key = ("ht", l, t, g)
                    sc.wait_ge(*full(key))
                    nc.scalar.activation(htok[:, 0, t, g * 512:(g + 1) * 512], held(key)[:, :], ACT.Copy).then_inc(*signal("ht_high" + W_, (t, g)))
            for i in range(SPLITS):
                high(i)
            gathered(0)
            for e in range(NE):
                i = UNITS * e
                high(i + 3)
                high(i + 4)
                sc.wait_ge(*full(("gt", l, e)))
                if e:
                    sc.wait_ge(*full(("aT", l, e - 1)))
                nc.scalar.activation(ag[:, :], held(("gt", l, e))[:, :], ACT.Silu).then_inc(*frees(("gt", l, e)))
                high(i + 5)
                if e + 1 < NE:
                    gathered(e + 1)
                key = ("aT", l, e)
                sc.wait_ge(*full(key))
                nc.scalar.activation(actT[:, 0, :, :].rearrange("p k n -> p (k n)"), held(key)[:, :], ACT.Copy).then_inc(*signal("actT_high" + W_, e))
                if e + 1 < NE:
                    high(i + 6)
                    high(i + 7)
                for n in range(2):
                    key = ("y", l, e, n)
                    sc.wait_ge(*full(key))
                    sc.wait_ge(*freed_by(("ws", l, e)))
                    nc.scalar.activation(yg[:, 0, n * 512:(n + 1) * 512], held(key)[:, :], ACT.Copy, scale=wsl[:, e % 2:e % 2 + 1])\
                      .then_inc(*signal("y_high" + W_, (e, n)))
                if e + 1 < NE:
                    high(i + 8)

        def dve_short(ve, l, modulation):
            V = nc.vector
            W_ = f"s{l}_"
            rank = rt[:, 340:388].rearrange("p (t n) -> p t n", t=TT)

            def low(i):
                raw, _ = expert_unit(l, i)
                ve.wait_ge(*made("high" + W_, i))
                V.tensor_tensor(split[:, i % SPLITS, 1, :], raw, split[:, i % SPLITS, 0, :].bitcast(F32), ALU.subtract)\
                 .then_inc(*signal("unit_free", (l, i)))

            def picks(e):
                if e:
                    ve.wait_ge(*full(("bk", l, e - 1)))
                for t in range(TT):
                    ins = V.tensor_scalar(pick[:, t, :], con[:, IOTA:IOTA + SLOTS], rank[:, t, e:e + 1], None, ALU.is_equal)
                ins.then_inc(*signal("picked" + W_, e))

            def gathered(e):
                for g in range(2):
                    key = ("ga", l, e, 1, g)
                    ve.wait_ge(*full(key))
                    V.tensor_copy(hg[:, e % 2, 1, 4 * g:4 * g + 4, :].rearrange("p k n -> p (k n)"), held(key)[:, :]).then_inc(*frees(key))

            def scattered(e):
                for j in range(KT):
                    key = ("sc", l, e, j)
                    ve.wait_ge(*full(key))
                    if e:
                        ve.wait_ge(*freed_by(("sc", l, e - 1, j)))
                        V.tensor_tensor(tmp[:, j, :], tmp[:, j, :], held(key)[:, 0:T], ALU.add).then_inc(*frees(key))
                    else:
                        V.tensor_copy(tmp[:, j, :], held(key)[:, 0:T]).then_inc(*frees(key))

            picks(0)
            for t in range(TT):
                for g in range(2):
                    key = ("ht", l, t, g)
                    ve.wait_ge(*full(key))
                    ve.wait_ge(*made("ht_high" + W_, (t, g)))
                    V.tensor_tensor(htok[:, 1, t, g * 512:(g + 1) * 512], held(key)[:, :], htok[:, 0, t, g * 512:(g + 1) * 512].bitcast(F32),
                                    ALU.subtract).then_inc(*frees(key))
            for i in range(SPLITS):
                low(i)
            gathered(0)
            for e in range(NE):
                i = UNITS * e
                low(i + 3)
                low(i + 4)
                if e + 1 < NE:
                    picks(e + 1)
                low(i + 5)
                key = ("up", l, e)
                ve.wait_ge(*full(key))
                ve.wait_ge(*freed_by(("gt", l, e)))
                V.tensor_tensor(ag[:, :], ag[:, :], held(key)[:, :], ALU.mult).then_inc(*frees(key))
                tally.also("gated" + W_, e)
                if e:
                    scattered(e - 1)
                if e + 1 < NE:
                    gathered(e + 1)
                key = ("aT", l, e)
                ve.wait_ge(*made("actT_high" + W_, e))
                V.tensor_tensor(actT[:, 1, :, :].rearrange("p k n -> p (k n)"), held(key)[:, :],
                                actT[:, 0, :, :].bitcast(F32).rearrange("p k n -> p (k n)"), ALU.subtract).then_inc(*frees(key))
                if e + 1 < NE:
                    low(i + 6)
                    low(i + 7)
                for n in range(2):
                    key = ("y", l, e, n)
                    ve.wait_ge(*made("y_high" + W_, (e, n)))
                    V.scalar_tensor_tensor(yg[:, 1, n * 512:(n + 1) * 512], held(key)[:, :], wsl[:, e % 2:e % 2 + 1],
                                           yg[:, 0, n * 512:(n + 1) * 512].bitcast(F32), ALU.mult, ALU.subtract).then_inc(*frees(key))
                if e + 1 < NE:
                    low(i + 8)
                if l + 1 < DEPTH and e < NMOD:
                    modulation(l + 1, e, W_)
                    V.memset(small[:, 0:1], 0.0).then_inc(*signal("mod_free", (l + 1, e)))
            scattered(NE - 1)
            for j in range(KT):
                ve.wait_ge(*freed_by(("sc", l, NE - 1, j)))
            if l + 1 < DEPTH:
                ve.wait_ge(*freed_by(("mod" + W_, l + 1, NMOD - 1)))

        def pe_general(pe, l, slab, gemm, tile, modulation):
            def up(e):
                slab(l, f"eg{e}")
                w = W(l, f"eg{e}").rearrange("p (k n) -> p k n", k=KT)
                for f in range(FT):
                    key = ("eg", l, e, f)
                    ps, reader = take(key)
                    if reader:
                        pe.wait_ge(*reader)
                    gemm(key, ps[:, 0:T], [(w[:, k, f * P:(f + 1) * P], hT[:, k, :]) for k in range(KT)])
                slab(l, f"eu{e}")
                w = W(l, f"eu{e}").rearrange("p (k n) -> p k n", k=KT)
                if e == 0:
                    ps, reader = take(("cT", l))
                    if reader:
                        pe.wait_ge(*reader)
                    pe.wait_ge(*made("comb", l))
                    for t in range(TT):
                        mm = nc.tensor.transpose(ps[0:NE, t * P:(t + 1) * P], rt[:, 64 + t * NE:64 + (t + 1) * NE], con[:, IDN:IDN + P])
                    mm.then_inc(*fills(("cT", l)))
                    pe.wait_ge(*freed_by(("cT", l)))
                ps, reader = take(("cb", l, e))
                if reader:
                    pe.wait_ge(*reader)
                gemm(("cb", l, e), ps[:, 0:T], [(con[0:NE, IDN + e:IDN + e + 1].broadcast_to([NE, P]), combT[0:NE, :])])
                for f in range(FT):
                    key = ("eu", l, e, f)
                    ps, reader = take(key)
                    if reader:
                        pe.wait_ge(*reader)
                    gemm(key, ps[:, 0:T], [(w[:, k, f * P:(f + 1) * P], hT[:, k, :]) for k in range(KT)])

            def down(e):
                slab(l, f"ed{e}")
                w = W(l, f"ed{e}").rearrange("p (k n) -> p k n", k=FT)
                for f in range(FT):
                    pe.wait_ge(*made(f"act_g{l}_", (e, f)))
                for j in range(KT):
                    key = ("ed", l, e, j)
                    ps, reader = take(key)
                    if reader:
                        pe.wait_ge(*reader)
                    gemm(key, ps[:, 0:T], [(w[:, k, j * P:(j + 1) * P], act[:, e % 2, k, :]) for k in range(FT)])

            for e in range(NE):
                up(e)
                down(e)
                if l + 1 < DEPTH and e < NMOD:
                    modulation(l + 1, e, f"g{l}_")

        def act_general(sc, l):
            for e in range(NE):
                for f in range(FT):
                    key = ("eg", l, e, f)
                    sc.wait_ge(*full(key))
                    if e:
                        sc.wait_ge(*made(f"act_g{l}_", (e - 1, f)))
                    nc.scalar.activation(hg4[:, f, :], held(key)[:, 0:T], ACT.Silu).then_inc(*frees(key))
                if e == 0:
                    sc.wait_ge(*full(("cT", l)))
                    nc.scalar.activation(combT[0:NE, :], held(("cT", l))[0:NE, 0:T], ACT.Copy).then_inc(*frees(("cT", l)))
                key = ("cb", l, e)
                sc.wait_ge(*full(key))
                nc.scalar.activation(cb[:, e % 2, :], held(key)[:, 0:T], ACT.Copy).then_inc(*frees(key))

        def dve_general(ve, l, modulation):
            V = nc.vector

            def slab_read(k):
                for i in (2 * k, 2 * k + 1):
                    V.memset(small[:, i % 2:i % 2 + 1], 0.0).then_inc(*signal("unit_free", (l, i)))

            for e in range(NE):
                ve.wait_ge(*freed_by(("cb", l, e)))
                for f in range(FT):
                    key = ("eu", l, e, f)
                    ve.wait_ge(*full(key))
                    ve.wait_ge(*freed_by(("eg", l, e, f)))
                    V.tensor_tensor(mt, held(key)[:, 0:T], hg4[:, f, :], ALU.mult).then_inc(*frees(key))
                    ve.wait_ge(*freed_by(key))
                    V.tensor_tensor(act[:, e % 2, f, :], mt, cb[:, e % 2, :], ALU.mult).then_inc(*signal(f"act_g{l}_", (e, f)))
                    ve.wait_ge(*made(f"act_g{l}_", (e, f)))
                slab_read(3 * e)
                slab_read(3 * e + 1)
                for j in range(KT):
                    key = ("ed", l, e, j)
                    ve.wait_ge(*full(key))
                    if e:
                        ve.wait_ge(*freed_by(("ed", l, e - 1, j)))
                        V.tensor_tensor(tmp[:, j, :], tmp[:, j, :], held(key)[:, 0:T], ALU.add).then_inc(*frees(key))
                    else:
                        V.tensor_copy(tmp[:, j, :], held(key)[:, 0:T]).then_inc(*frees(key))
                slab_read(3 * e + 2)
                if l + 1 < DEPTH and e < NMOD:
                    modulation(l + 1, e, f"g{l}_")
                    V.memset(small[:, 2:3], 0.0).then_inc(*signal("mod_free", (l + 1, e)))
            for j in range(KT):
                ve.wait_ge(*freed_by(("ed", l, NE - 1, j)))
            if l + 1 < DEPTH:
                ve.wait_ge(*freed_by(("mod" + f"g{l}_", l + 1, NMOD - 1)))

        block = ctx.enter_context(nc.Block())

        @block.tensor
        def _(pe):
            cur = [-1]

            def slab(l, name):
                i = [(a, b) for a, b, _ in order].index((l, name))
                if i != cur[0]:
                    assert i == cur[0] + 1, (l, name)
                    cur[0] = i
                    pe.wait_ge(dma_slab[i % RING], 16 * (i // RING + 1))

            def closes(key):
                closing[cur[0]] = key

            def gemm(key, out, pairs):
                n = len(pairs)
                for i, (w, a) in enumerate(pairs):
                    mm = nc.tensor.matmul(out, lhsT=w, rhs=a, start=(i == 0), stop=(i == n - 1))
                mm.then_inc(*fills(key))

            def norm(l, which):
                ps, reader = take(("n", l, which))
                if reader:
                    pe.wait_ge(*reader)
                for k in range(KT):
                    pe.wait_ge(*made("square", ("x", l, which, k)))
                    mm = nc.tensor.matmul(ps[:, 0:T], lhsT=con[:, ONES:ONES + P], rhs=tmp[:, k, :], start=(k == 0), stop=(k == KT - 1))
                mm.then_inc(*fills(("n", l, which)))

            def modulation(l, i, w=""):
                slab(l, f"m{i}")
                key = ("mod" + w, l, i)
                ps, reader = take(key)
                if reader:
                    pe.wait_ge(*reader)
                for c in range(4):
                    w = tile(l, f"m{i}", c)
                    for k in range(KT):
                        mm = nc.tensor.matmul(ps[:, 2 * c:2 * c + 2], lhsT=w[:, k, :], rhs=cv[:, k, :], start=(k == 0), stop=(k == KT - 1))
                mm.then_inc(*fills(key))
                closes(key)

            def project(l, name, c, key, last=False):
                slab(l, name)
                ps, reader = take(key)
                if reader:
                    pe.wait_ge(*reader)
                w = tile(l, name, c)
                gemm(key, ps[:, 0:T], [(w[:, k, :], hT[:, k, :]) for k in range(KT)])
                if last:
                    closes(key)

            def head_norm(l, key, lhs, sqs):
                ps, reader = take(("hn", l, key))
                if reader:
                    pe.wait_ge(*reader)
                for i, s in enumerate(sqs):
                    pe.wait_ge(*made("square", (key, l, i)))
                    mm = nc.tensor.matmul(ps[:, 0:T], lhsT=con[:, lhs:lhs + P], rhs=s, start=(i == 0), stop=(i == len(sqs) - 1))
                mm.then_inc(*fills(("hn", l, key)))

            def merge(l, n, j):
                if j == 0:
                    slab(l, f"br{n}")
                    br_slab = cur[0]
                    held[n] = br_slab
                project(l, f"g{n}{j // 4}", j % 4, ("g", l, n, j), last=(j % 4 == 3))
                key = ("p", l, n, j)
                ps, reader = take(key)
                if reader:
                    pe.wait_ge(*reader)
                if j == 0:
                    if n < 2:
                        pe.wait_ge(*made("o_ready", (l, n)))
                    else:
                        pe.wait_ge(*made("oc_gated", (l, BT - 1)))
                w = W(l, f"br{n}").rearrange("p (c k n) -> p c k n", c=KT, k=BT)[:, j]
                gemm(key, ps[:, 0:T], [(w[:, k, :], oBr[n][:, k, :]) for k in range(BT)])
                if j == KT - 1:
                    closing[held[n]] = key

            held = {}

            pe.wait_ge(dma_con, 16 * NCDMA)
            for i in range(NMOD):
                if i == 0:
                    pe.wait_ge(*made("cond", 0))
                modulation(0, i)

            for l in range(DEPTH):
                norm(l, 1)
                for k in range(KT):
                    pe.wait_ge(*made("h_ready", (l, 1, k)))
                for c in range(BT):
                    project(l, "qa", c, ("qa", l, c), last=(c == BT - 1))
                    if c:
                        head_norm(l, f"qa{c - 1}", BLK, [tmp[:, c - 1, :]])
                project(l, "kv", 0, ("ka", l))
                head_norm(l, "qa3", BLK, [tmp[:, 3, :]])
                va = tile(l, "kv", 1)
                ps, reader = take(("va", l))
                if reader:
                    pe.wait_ge(*reader)
                for t in range(TT):
                    for k in range(KT):
                        mm = nc.tensor.matmul(ps[:, t * P:(t + 1) * P], lhsT=hT[:, k, t * P:(t + 1) * P], rhs=va[:, k, :],
                                              start=(k == 0), stop=(k == KT - 1))
                mm.then_inc(*fills(("va", l)))
                head_norm(l, "ka", BLK, [tmp[:, 4, :]])
                kr = tile(l, "kv", 2)
                ps, reader = take(("kr", l))
                if reader:
                    pe.wait_ge(*reader)
                gemm(("kr", l), ps[NOPE:NOPE + ROPE, 0:T], [(kr[:, k, 0:ROPE], hT[:, k, :]) for k in range(KT)])
                project(l, "kv", 3, ("qr", l, 0), last=True)
                project(l, "qr", 0, ("qr", l, 1))
                project(l, "qr", 1, ("qr", l, 2))
                project(l, "qr", 2, ("kc", l, 0))
                head_norm(l, "qr", ONES, [tmp[:, 5 + c, :] for c in range(QT)])
                project(l, "qr", 3, ("kc", l, 1), last=True)
                head_norm(l, "kc", ONES, [tmp[:, c, :] for c in range(CT)])
                slab(l, "bwq")
                w = W(l, "bwq")[:, 0:QT * HEADS * QB_W].rearrange("p (k n) -> p k n", k=QT)
                for c in range(QT):
                    pe.wait_ge(*made("normed", (f"qr{c}", l)))
                for h in range(HEADS):
                    ps, reader = take(("qb", l, h))
                    if reader:
                        pe.wait_ge(*reader)
                    gemm(("qb", l, h), ps[0:QB_W, 0:T], [(w[:, k, h * QB_W:(h + 1) * QB_W], qr[:, k, :]) for k in range(QT)])
                closes(("qb", l, HEADS - 1))
                slab(l, "bwkv")
                w = W(l, "bwkv")[:, 0:CT * BW].rearrange("p (k n) -> p k n", k=CT)
                wv = W(l, "bwkv")[:, CT * BW:2 * CT * BW].rearrange("p (k n) -> p k n", k=CT)
                for c in range(CT):
                    pe.wait_ge(*made("normed", (f"kc{c}", l)))
                pe.wait_ge(dma_cache, 16 * NCACHE * (l + 1))
                for h in range(HEADS):
                    ps, reader = take(("kb", l, h))
                    if reader:
                        pe.wait_ge(*reader)
                    gemm(("kb", l, h), ps[0:NOPE, :], [(w[:, k, h * HD:(h + 1) * HD], ckvT[:, k, :]) for k in range(CT)])
                for t in range(4):
                    ps, reader = take(("vb", l, t))
                    if reader:
                        pe.wait_ge(*reader)
                    gemm(("vb", l, t), ps[:, :], [(ckvT[:, k, t * P:(t + 1) * P], wv[:, k, :]) for k in range(CT)])
                closes(("vb", l, 3))

                def scores(u):
                    br, hp, qt = units[u]
                    c0, c1 = key_cols(qt)
                    for i in range(2):
                        h = 2 * hp + i
                        ps, reader = take(("s", l, u, i))
                        if reader:
                            pe.wait_ge(*reader)
                        if br == 0:
                            r = slice(HD * i, HD * i + HD)
                            if u == 0 and i == 0:
                                pe.wait_ge(*made("dup", (l, 3)))
                            pe.wait_ge(*made("roped", (l, hp)))
                            q, k = qA[r, hp, qt * P:(qt + 1) * P], keysA[r, h // 4, c0:c1]
                        else:
                            pe.wait_ge(*made("roped", (l, "qb")))
                            pe.wait_ge(*made("kr_copied", l))
                            pe.wait_ge(*freed_by(("kb", l, h)))
                            q, k = qB[0:QB_W, h, qt * P:(qt + 1) * P], keysB[0:QB_W, h, c0:c1]
                        gemm(("s", l, u, i), ps[:, 0:c1 - c0], [(q, k)])

                def turn(u):
                    br, hp, qt = units[u]
                    for i in range(2):
                        ps, reader = take(("t", l, u, i))
                        if reader:
                            pe.wait_ge(*reader)
                        pe.wait_ge(*made("probs", (l, u, i)))
                        for t in range(len(key_tiles(qt))):
                            mm = nc.tensor.transpose(ps[:, t * P:(t + 1) * P], probs[:, u % 2, i, t * P:(t + 1) * P], con[:, IDN:IDN + P])
                        mm.then_inc(*fills(("t", l, u, i)))

                def values(u):
                    br, hp, qt = units[u]
                    ps, reader = take(("o", l, u))
                    if reader:
                        pe.wait_ge(*reader)
                    if u == 0:
                        pe.wait_ge(*freed_by(("va", l)))
                    if br == 1:
                        pe.wait_ge(*freed_by(("vb", l, 3)))
                    for i in range(2):
                        h = 2 * hp + i
                        pe.wait_ge(*freed_by(("t", l, u, i)))
                        for t, kt in enumerate(key_tiles(qt)):
                            v = vA[:, kt, (h // 4) * HD:(h // 4 + 1) * HD] if br == 0 else vB[:, kt, h * HD:(h + 1) * HD]
                            mm = nc.tensor.matmul(ps[HD * i:HD * i + HD, 0:P], lhsT=v, rhs=probsT[:, u % 2, i, t * P:(t + 1) * P],
                                                  start=(t == 0), stop=(t == len(key_tiles(qt)) - 1))
                    mm.then_inc(*fills(("o", l, u)))

                for s in range(len(units) + 2):
                    if s < len(units):
                        scores(s)
                    if 1 <= s <= len(units):
                        turn(s - 1)
                    if s >= 2:
                        values(s - 2)

                slab(l, "ic")
                w = W(l, "ic").rearrange("p (k n) -> p k n", k=KT)
                for t in range(TT):
                    ps, reader = take(("ic", l, t))
                    if reader:
                        pe.wait_ge(*reader)
                    gemm(("ic", l, t), ps[:, :], [(hT[:, k, t * P:(t + 1) * P], w[:, k, :]) for k in range(KT)])
                closes(("ic", l, TT - 1))
                for hh in range(2):
                    for c in range(4):
                        project(l, f"fb{hh}", c, ("fb", l, hh, c), last=(c == 3))
                    for c in range(2):
                        project(l, f"qc{hh}", c, ("qc", l, hh, c), last=(c == 1))
                    for tt in range(TT):
                        cols = slice(tt * P, (tt + 1) * P)
                        todo = list(fill[hh, tt])
                        for n in range(len(LEVELS) + 1):
                            ps, reader = take(("A", l, hh, tt, n))
                            if reader:
                                pe.wait_ge(*reader)
                            if n == 0:
                                pe.wait_ge(*made("fk_ready", (l, hh, 3)))
                                pe.wait_ge(*freed_by(("qc", l, hh, 1)))
                            else:
                                pe.wait_ge(*made("lev_f", (l, hh, tt, n - 1)))
                                pe.wait_ge(*made("lev_b", (l, hh, tt, n - 1)))
                            for d in range(4):
                                kk, qq = (Kg[:, d, cols], qd[:, d, cols]) if n == 0 else (Kl[n - 1][:, d, :], Ql[n - 1][:, d, :])
                                mm = nc.tensor.matmul(ps[:, d * P:(d + 1) * P], lhsT=kk, rhs=qq, start=True, stop=True)
                            mm.then_inc(*fills(("A", l, hh, tt, n)))
                            if n in (1, 3) and todo:
                                merge(l, *todo.pop(0))
                        ps, reader = take(("kt", l, hh, tt))
                        if reader:
                            pe.wait_ge(*reader)
                        pe.wait_ge(*made("kr_f", (l, hh, tt)))
                        pe.wait_ge(*made("kr_b", (l, hh, tt)))
                        for d in range(4):
                            mm = nc.tensor.transpose(ps[:, d * P:(d + 1) * P], Rr[:, d, :], con[:, IDN:IDN + P])
                        mm.then_inc(*fills(("kt", l, hh, tt)))
                        while todo:
                            merge(l, *todo.pop(0))
                        if hh == 0 and tt == 0:
                            pe.wait_ge(*freed_by(("ic", l, TT - 1)))
                        ps, reader = take(("U", l, hh, tt))
                        if reader:
                            pe.wait_ge(*reader)
                        pe.wait_ge(*freed_by(("kt", l, hh, tt)))
                        for d in range(4):
                            h = 4 * hh + d
                            mm = nc.tensor.matmul(ps[:, d * HD:(d + 1) * HD], lhsT=KRt[:, d, :], rhs=vC[:, tt, h * HD:(h + 1) * HD],
                                                  start=True, stop=True)
                        mm.then_inc(*fills(("U", l, hh, tt)))
                        ps, reader = take(("oi", l, hh, tt))
                        if reader:
                            pe.wait_ge(*reader)
                        pe.wait_ge(*freed_by(("A", l, hh, tt, len(LEVELS))))
                        for d in range(4):
                            h = 4 * hh + d
                            mm = nc.tensor.matmul(ps[HD * (d % 2):HD * (d % 2) + HD, (d // 2) * P:(d // 2 + 1) * P],
                                                  lhsT=vC[:, tt, h * HD:(h + 1) * HD], rhs=Am[:, d, :], start=True, stop=True)
                        mm.then_inc(*fills(("oi", l, hh, tt)))
                    ps, reader = take(("oe", l, hh))
                    if reader:
                        pe.wait_ge(*reader)
                    pe.wait_ge(*made("s_f", (l, hh)))
                    pe.wait_ge(*made("s_b", (l, hh)))
                    pe.wait_ge(*made("qp_f", (l, hh)))
                    pe.wait_ge(*made("qp_b", (l, hh)))
                    for t in range(2):
                        for d in range(4):
                            h = 4 * hh + d
                            o = (d // 2) * 2 * P + t * P
                            mm = nc.tensor.matmul(ps[HD * (d % 2):HD * (d % 2) + HD, o:o + P], lhsT=Sin[:, t, h, :], rhs=QP[:, t, d, :],
                                                  start=True, stop=True)
                    mm.then_inc(*fills(("oe", l, hh)))
                for c in range(BT):
                    project(l, "gc", c, ("gc", l, c), last=(c == BT - 1))
                    head_norm(l, f"oc{c}", BLK, [gsb[:, c % 2, :]])
                for j in range(KT):
                    merge(l, 2, j)
                for j in range(KT):
                    slab(l, f"o{j // 4}")
                    w = tile(l, f"o{j // 4}", j % 4)
                    if j == 0:
                        pe.wait_ge(*made("merged", (l, 2, KT - 1)))
                    ps, reader = take(("out", l, j))
                    if reader:
                        pe.wait_ge(*reader)
                    gemm(("out", l, j), ps[:, 0:T], [(w[:, k, :], tmp[:, k, :]) for k in range(KT)])
                    if j % 4 == 3:
                        closes(("out", l, j))

                norm(l, 2)
                for k in range(KT):
                    pe.wait_ge(*made("h_ready", (l, 2, k)))
                ps, reader = take(("r", l))
                if reader:
                    pe.wait_ge(*reader)
                rw = par[:, l, RW:RW + KT * (NG + NE)].rearrange("p (k n) -> p k n", k=KT)
                for t in range(TT):
                    for k in range(KT):
                        mm = nc.tensor.matmul(ps[:, t * 32:t * 32 + NG + NE], lhsT=hT[:, k, t * P:(t + 1) * P], rhs=rw[:, k, :],
                                              start=(k == 0), stop=(k == KT - 1))
                mm.then_inc(*fills(("r", l)))

                ps, reader = take(("rank", l))
                pe.wait_ge(*reader)
                pe.wait_ge(*made("sel", l))
                sel = rt[:, 0:TT * NE].rearrange("p (t n) -> p t n", t=TT)
                for t in range(TT):
                    for s in range(t + 1):
                        w = TRI if s == t else ONES
                        nc.tensor.matmul(ps[:, t * NE:(t + 1) * NE], lhsT=con[:, w:w + P], rhs=sel[:, s, :], start=(s == 0), stop=(s == t))
                for t in range(TT):
                    mm = nc.tensor.matmul(ps[:, TT * NE:(TT + 1) * NE], lhsT=con[:, ONES:ONES + P], rhs=sel[:, t, :], start=(t == 0),
                                          stop=(t == TT - 1))
                mm.then_inc(*fills(("rank", l)))
                for s in readers(""):
                    pe.wait_ge(*s)
                pe.wait_ge(*made("flag", l))
                many = pe.value_load(flag[0:1, 0:1], min_val=0, max_val=1)
                first = cur[0]
                with pe.If(many == 0):
                    way[0] = f"s{l}_"
                    pe_short(pe, l, cur, slab, modulation)
                    for s in readers(way[0]):
                        pe.wait_ge(*s)
                cur[0] = first
                with pe.Else():
                    way[0] = f"g{l}_"
                    pe_general(pe, l, slab, gemm, tile, modulation)
                    for s in readers(way[0]):
                        pe.wait_ge(*s)
                way[0] = ""
            norm(DEPTH, 1)

        @block.scalar
        def _(sc):
            def squares_x(l, which):
                for k in range(KT):
                    if not (l == 0 and which == 1):
                        sc.wait_ge(*made("x_ready", (l, which, k)))
                    nc.scalar.activation(tmp[:, k, :], xT[:, k, :], ACT.Square).then_inc(*signal("square", ("x", l, which, k)))
                root(("n", l, which), 1.0 / D, ("n", l, which))

            nroot = [0]

            def root(bkey, scale, key):
                sc.wait_ge(*full(bkey))
                ps = held(bkey)
                s = nroot[0] % 3
                if nroot[0] >= 3:
                    sc.wait_ge(*made("std_used", nroot[0] - 3))
                nc.scalar.activation(std[:, s, :], ps[:, 0:T], ACT.Sqrt, scale=scale, bias=eps[:, 0:1]).then_inc(*frees(bkey))
                nroot[0] += 1

            def split(bkey, dst, sq, key, l, i, wait=None):
                sc.wait_ge(*full(bkey))
                ps = held(bkey)
                if wait:
                    wait()
                nc.scalar.activation(sq, ps[:, 0:T], ACT.Square).then_inc(*signal("square", (key, l, i)))
                nc.scalar.activation(dst, ps[:, 0:T], ACT.Copy).then_inc(*frees(bkey))

            sc.wait_ge(dma_con, 16 * NCDMA)
            sc.wait_ge(*made("eps", 0))
            nc.scalar.activation(cv[:, :, :], cv[:, :, :], ACT.Silu).then_inc(*signal("cond", 0))
            sc.wait_ge(*made("lbmax", 0))
            nc.scalar.activation(lbw[:, 2:4, :], lbw[:, 0:2, :], ACT.Exp).then_inc(*signal("lbexp", 0))

            for l in range(DEPTH):
                squares_x(l, 1)
                for c in range(BT):
                    split(("qa", l, c), qA[:, c, :], tmp[:, c, :], f"qa{c}", l, 0)
                    if c:
                        root(("hn", l, f"qa{c - 1}"), 1.0 / HD, ("qa", c - 1))
                split(("ka", l), knT[:, :], tmp[:, 4, :], "ka", l, 0)
                root(("hn", l, "qa3"), 1.0 / HD, ("qa", 3))
                sc.wait_ge(*full(("va", l)))
                ps = held(("va", l))
                ins = nc.scalar.activation(vA[:, 0:TT, :].rearrange("p a n -> p (a n)"), ps[:, 0:T], ACT.Copy)
                ins.then_inc(*frees(("va", l)))
                root(("hn", l, "ka"), 1.0 / HD, "ka")
                sc.wait_ge(*full(("kr", l)))
                ps = held(("kr", l))
                nc.scalar.activation(krT[NOPE:NOPE + ROPE, 0:T], ps[NOPE:NOPE + ROPE, 0:T], ACT.Copy).then_inc(*frees(("kr", l)))
                for c in range(QT):
                    split(("qr", l, c), qr[:, c, :], tmp[:, 5 + c, :], "qr", l, c)
                split(("kc", l, 0), ckvT[:, 0, 0:T], tmp[:, 0, :], "kc", l, 0)
                root(("hn", l, "qr"), 1.0 / Q_RANK, "qr")
                split(("kc", l, 1), ckvT[:, 1, 0:T], tmp[:, 1, :], "kc", l, 1)
                root(("hn", l, "kc"), 1.0 / KV_RANK, "kc")
                sc.wait_ge(*made("roped", (l, "ka")))
                for j in range(KV_A):
                    for r in range(2):
                        nc.scalar.activation(keysA[HD * r:HD * r + HD, j, 0:T], knT[HD * j:HD * j + HD, :], ACT.Copy).then_inc(*signal("dup", (l, 2 * j + r)))
                for h in range(HEADS):
                    sc.wait_ge(*full(("qb", l, h)))
                    ps = held(("qb", l, h))
                    nc.scalar.activation(qB[0:QB_W, h, :], ps[0:QB_W, 0:T], ACT.Copy).then_inc(*frees(("qb", l, h)))
                for h in range(HEADS):
                    sc.wait_ge(*full(("kb", l, h)))
                    ps = held(("kb", l, h))
                    nc.scalar.activation(keysB[0:NOPE, h, :], ps[0:NOPE, :], ACT.Copy).then_inc(*frees(("kb", l, h)))
                for t in range(4):
                    sc.wait_ge(*full(("vb", l, t)))
                    ps = held(("vb", l, t))
                    nc.scalar.activation(vB[:, t, :], ps[:, :], ACT.Copy).then_inc(*frees(("vb", l, t)))

                def exps(u):
                    br, hp, qt = units[u]
                    c0, c1 = key_cols(qt)
                    for i in range(2):
                        sc.wait_ge(*made("negmax", (l, u, i)))
                        sc.wait_ge(*full(("s", l, u, i)))
                        ps = held(("s", l, u, i))
                        if u < 2 and i == 0:
                            sc.wait_ge(*made("roped", (l, "qb")))
                        if u >= 2:
                            sc.wait_ge(*full(("t", l, u - 2, i)))
                        nc.scalar.activation(probs[:, u % 2, i, 0:c1 - c0], ps[:, 0:c1 - c0], ACT.Exp, bias=nmx[:, u % 2, i:i + 1],
                                                   scale=(SCALE_A, SCALE_B)[br], accum_out=rsum[:, u % 2, i:i + 1]).then_inc(*frees(("s", l, u, i)))

                def probs_turned(u):
                    br, hp, qt = units[u]
                    n = P * len(key_tiles(qt))
                    sc.wait_ge(*full(("t", l, u, 1)))
                    ps = held(("t", l, u, 1))
                    if u >= 2:
                        sc.wait_ge(*full(("o", l, u - 2)))
                    nc.scalar.activation(probsT[:, u % 2, 1, 0:n], ps[:, 0:n], ACT.Copy).then_inc(*frees(("t", l, u, 1)))

                for s in range(len(units) + 1):
                    if s < len(units):
                        exps(s)
                    if s >= 1:
                        probs_turned(s - 1)

                sc.wait_ge(*made("o_ready", (l, 1)))
                sc.wait_ge(dma_out, 16 * (5 * l + 4))
                for t in range(TT):
                    sc.wait_ge(*full(("ic", l, t)))
                    ps = held(("ic", l, t))
                    nc.scalar.activation(vC[:, t, :], ps[:, :], ACT.Copy).then_inc(*frees(("ic", l, t)))
                gates = [0]

                def gate(n, j):
                    sc.wait_ge(*full(("g", l, n, j)))
                    ps = held(("g", l, n, j))
                    if gates[0] >= GATES:
                        sc.wait_ge(*made("gate_used", (l, gates[0] - GATES)))
                    nc.scalar.activation(gsb[:, gates[0] % GATES, :], ps[:, 0:T], ACT.Sigmoid).then_inc(*frees(("g", l, n, j)))
                    gates[0] += 1

                for hh in range(2):
                    for c in range(4):
                        sc.wait_ge(*full(("fb", l, hh, c)))
                        ps = held(("fb", l, hh, c))
                        if hh:
                            sc.wait_ge(*full(("oi", l, 0, TT - 1)))
                            sc.wait_ge(*made("kr_f", (l, 0, TT - 1)))
                            sc.wait_ge(*made("kr_b", (l, 0, TT - 1)))
                        nc.scalar.activation(Fg[:, c, :], ps[:, 0:T], ACT.Sigmoid).then_inc(*frees(("fb", l, hh, c)))
                    for c in range(2):
                        sc.wait_ge(*full(("qc", l, hh, c)))
                        ps = held(("qc", l, hh, c))
                        for i in range(2):
                            for r in range(2):
                                ins = nc.scalar.activation(qd[HD * r:HD * r + HD, 2 * c + i, :], ps[HD * i:HD * i + HD, 0:T], ACT.Copy)
                                if (i, r) == (1, 1):
                                    ins.then_inc(*frees(("qc", l, hh, c)))
                                else:
                                    ins.then_inc(*signal("qd_part", (l, hh, c, i, r)))
                    for tt in range(TT):
                        todo = list(fill[hh, tt])
                        for _ in range(2):
                            if todo:
                                gate(*todo.pop(0))
                        sc.wait_ge(*full(("kt", l, hh, tt)))
                        ps = held(("kt", l, hh, tt))
                        if not (hh == 0 and tt == 0):
                            ph, pt = batches[batches.index((hh, tt)) - 1]
                            sc.wait_ge(*full(("U", l, ph, pt)))
                        nc.scalar.activation(KRt[:, :, :].rearrange("p a n -> p (a n)"), ps[:, :], ACT.Copy).then_inc(*frees(("kt", l, hh, tt)))
                        while todo:
                            gate(*todo.pop(0))
                        sc.wait_ge(*full(("oi", l, hh, tt)))
                        ps = held(("oi", l, hh, tt))
                        nc.scalar.activation(oBr[2][:, 2 * hh:2 * hh + 2, tt * P:(tt + 1) * P],
                                                   ps[:, 0:2 * P].rearrange("p (a n) -> p a n", a=2), ACT.Copy).then_inc(*frees(("oi", l, hh, tt)))
                sc.wait_ge(*made("oc_sum", (l, 1)))
                sc.wait_ge(*made("gate_used", (l, gates[0] - 1)))
                for c in range(BT):
                    if c >= 2:
                        sc.wait_ge(*full(("hn", l, f"oc{c - 2}")))
                    nc.scalar.activation(gsb[:, c % 2, :], oBr[2][:, c, :], ACT.Square).then_inc(*signal("square", (f"oc{c}", l, 0)))
                    root(("hn", l, f"oc{c}"), 1.0 / HD, "oc")
                for c in range(BT):
                    sc.wait_ge(*full(("gc", l, c)))
                    ps = held(("gc", l, c))
                    nc.scalar.activation(Fg[:, c, :], ps[:, 0:T], ACT.Silu).then_inc(*frees(("gc", l, c)))
                gates[0] = 0
                sc.wait_ge(*made("oc_gated", (l, BT - 1)))
                sc.wait_ge(*full(("hn", l, "oc3")))
                for j in range(KT):
                    sc.wait_ge(*full(("g", l, 2, j)))
                    ps = held(("g", l, 2, j))
                    if j >= GATES:
                        sc.wait_ge(*made("gate_used", (l, "c", j - GATES)))
                    nc.scalar.activation(gsb[:, j % GATES, :], ps[:, 0:T], ACT.Sigmoid).then_inc(*frees(("g", l, 2, j)))

                sc.wait_ge(*full(("out", l, KT - 1)))
                squares_x(l, 2)
                sc.wait_ge(*made("glog", l))
                nc.scalar.activation(rt[:, 128:128 + TT * NG], rt[:, 112:112 + TT * NG], ACT.Exp).then_inc(*signal("gexp", l))
                sc.wait_ge(*made("ediff", l))
                nc.scalar.activation(rt[:, 144:144 + TT], rt[:, 140:140 + TT], ACT.Exp).then_inc(*signal("eexp", l))
                sc.wait_ge(*made("flag", l))
                many = sc.value_load(flag[0:1, 0:1], min_val=0, max_val=1)
                with sc.If(many == 0):
                    act_short(sc, l)
                with sc.Else():
                    act_general(sc, l)
            squares_x(DEPTH, 1)

        @block.vector
        def _(ve):
            V = nc.vector
            steps = [0]

            def step(ins):
                ins.then_inc(*signal("dve_step", steps[0]))
                steps[0] += 1
                ve.wait_ge(sem("dve_step"), steps[0])

            nrec = [0]

            def rstd(bkey):
                s = nrec[0] % 3
                nrec[0] += 1
                ve.wait_ge(*freed_by(bkey))
                step(V.reciprocal(std[:, s, :], std[:, s, :]))
                return std[:, s, :]

            def std_used():
                tally.also("std_used", nrec[0] - 1)

            def modulation(l, i, w=""):
                ve.wait_ge(*full(("mod" + w, l, i)))
                ps = held(("mod" + w, l, i))
                V.tensor_tensor(mod[:, l, 4 * i:4 * i + 4, :], ps[:, 0:8].rearrange("p (c g) -> p c g", g=2),
                                      par[:, l, BM + 4 * i:BM + 4 * i + 4].unsqueeze(2).broadcast_to([P, 4, 2]), ALU.add).then_inc(*frees(("mod" + w, l, i)))

            def norm(l, which):
                sh, n0 = (0, N1) if which == 1 else (3 * KT, N2)
                if l == 0:
                    ve.wait_ge(*freed_by(("mod", l, NMOD - 1)))
                step(V.scalar_tensor_tensor(gain[:, which - 1, :, :], mod[:, l, sh + KT:sh + 2 * KT, :], 1.0,
                                            par[:, l, n0:n0 + KT].unsqueeze(2).broadcast_to([P, KT, 2]), ALU.add, ALU.mult))
                r = rstd(("n", l, which))
                ve.wait_ge(*full(("n", l, which)))
                for k in range(KT):
                    step(V.tensor_tensor(tmp[:, k, :], xT[:, k, :], r, ALU.mult))
                    for g, a, b in GROUPS:
                        ins = V.tensor_scalar(hT[:, k, a:b], tmp[:, k, a:b], gain[:, which - 1, k, g:g + 1], mod[:, l, sh + k, g:g + 1],
                                              ALU.mult, ALU.add)
                    ins.then_inc(*signal("h_ready", (l, which, k)))
                std_used()

            def normalise(l, key, dst, name, col, r):
                V.scalar_tensor_tensor(dst, dst, par[:, l, col:col + 1], r, ALU.mult, ALU.mult).then_inc(*signal("normed", (name, l)))
                std_used()

            def rope(dst, work, c, s, half, key):
                step(V.stream_shuffle(work, dst, [(i // (2 * half)) * 2 * half + (i + half) % (2 * half) for i in range(32)]))
                step(V.tensor_tensor(work, work, s, ALU.mult))
                step(V.tensor_tensor(dst, dst, c, ALU.mult))
                V.tensor_tensor(dst, dst, work, ALU.add).then_inc(*signal("roped", key))

            V.memset(eps[:, :], EPS).then_inc(*signal("eps", 0))
            ve.wait_ge(dma_con, 16 * NCDMA)
            step(V.tensor_copy(lmask[:, :, :].rearrange("p n t -> p (n t)"), region[:, REGION - len(LEVELS) * P:]))
            step(V.tensor_tensor(small[:, 0:HEADS], lbl[:, 0, :], lbl[:, 1, :], ALU.max))
            V.tensor_tensor(lbw[:, 0:2, :], lbl[:, :, :], small[:, 0:HEADS].unsqueeze(1).broadcast_to([P, 2, HEADS]), ALU.subtract).then_inc(*signal("lbmax", 0))
            ve.wait_ge(*made("lbexp", 0))
            step(V.tensor_tensor(small[:, 0:HEADS], lbw[:, 2, :], lbw[:, 3, :], ALU.add))
            step(V.reciprocal(small[:, 8:16], small[:, 0:HEADS]))
            step(V.tensor_tensor(lbw[:, 0:2, :], lbw[:, 2:4, :], small[:, 8:16].unsqueeze(1).broadcast_to([P, 2, HEADS]), ALU.mult))
            step(V.tensor_tensor(lb[:, 0, :], lbw[:, 0, :], lbw[:, 0, :], ALU.subtract))
            step(V.tensor_tensor(small[:, 0:HEADS], lbw[:, 0, :], lbw[:, 1, :], ALU.add))
            step(V.tensor_tensor(lb[:, 1, :], small[:, 0:HEADS], lbw[:, 0, :], ALU.subtract))
            step(V.tensor_scalar(oml[:, :, :], lb[:, :, :], -1.0, 1.0, ALU.mult, ALU.add))
            for i in range(NMOD):
                modulation(0, i)

            for l in range(DEPTH):
                norm(l, 1)
                for c in range(BT):
                    r = rstd(("hn", l, f"qa{c}"))
                    normalise(l, None, qA[:, c, :], f"qa{c}", AQ, r)
                    ve.wait_ge(*made("normed", (f"qa{c}", l)))
                    rope(qA[:, c, CTX:T], swp, con[:, CA:CA + LAT], con[:, SA:SA + LAT], 16, (l, c))
                r = rstd(("hn", l, "ka"))
                normalise(l, None, knT[:, :], "ka", AK, r)
                ve.wait_ge(*made("normed", ("ka", l)))
                rope(knT[:, CTX:T], swp, con[:, CA:CA + LAT], con[:, SA:SA + LAT], 16, (l, "ka"))
                rows = slice(NOPE, NOPE + ROPE)
                ve.wait_ge(*freed_by(("kr", l)))
                ve.wait_ge(*made("roped", (l, "ka")))
                rope(krT[rows, CTX:T], swp[rows, :], con[rows, CB:CB + LAT], con[rows, SB:SB + LAT], 8, (l, "kr"))
                r = rstd(("hn", l, "qr"))
                for c in range(QT):
                    normalise(l, None, qr[:, c, :], f"qr{c}", BQ + c, r)
                r = rstd(("hn", l, "kc"))
                for c in range(CT):
                    normalise(l, None, ckvT[:, c, 0:T], f"kc{c}", BK + c, r)
                ve.wait_ge(*freed_by(("qb", l, HEADS - 1)))
                work = tmp[rows, :, :].rearrange("p a t -> p (a t)")[:, 0:HEADS * LAT].rearrange("p (h t) -> p h t", h=HEADS)
                tab = [con[rows, o:o + LAT].unsqueeze(1).broadcast_to([ROPE, HEADS, LAT]) for o in (CB, SB)]
                rope(qB[rows, :, CTX:T], work, tab[0], tab[1], 8, (l, "qb"))

                def maxima(u):
                    br, hp, qt = units[u]
                    c0, c1 = key_cols(qt)
                    for i in range(2):
                        ve.wait_ge(*full(("s", l, u, i)))
                        ps = held(("s", l, u, i))
                        if u >= 2:
                            ve.wait_ge(*freed_by(("s", l, u - 2, i)))
                        step(V.tensor_reduce(nmx[:, u % 2, i:i + 1], ps[:, 0:c1 - c0], AX, ALU.max, negate=True))
                        V.tensor_scalar(nmx[:, u % 2, i:i + 1], nmx[:, u % 2, i:i + 1], (SCALE_A, SCALE_B)[br], None, ALU.mult).then_inc(*signal("negmax", (l, u, i)))

                def softmax(u):
                    br, hp, qt = units[u]
                    n = P * len(key_tiles(qt))
                    for i in range(2):
                        ve.wait_ge(*freed_by(("s", l, u, i)))
                        step(V.reciprocal(rsum[:, u % 2, i:i + 1], rsum[:, u % 2, i:i + 1]))
                        pv = probs[:, u % 2, i, 0:n]
                        V.tensor_scalar(pv, pv, rsum[:, u % 2, i:i + 1], None, ALU.mult).then_inc(*signal("probs", (l, u, i)))

                def turned(u):
                    br, hp, qt = units[u]
                    n = P * len(key_tiles(qt))
                    ve.wait_ge(*full(("t", l, u, 0)))
                    ps = held(("t", l, u, 0))
                    if u >= 2:
                        ve.wait_ge(*full(("o", l, u - 2)))
                    V.tensor_copy(probsT[:, u % 2, 0, 0:n], ps[:, 0:n]).then_inc(*frees(("t", l, u, 0)))

                def outputs(u):
                    br, hp, qt = units[u]
                    ve.wait_ge(*full(("o", l, u)))
                    ps = held(("o", l, u))
                    V.tensor_copy(oBr[br][:, hp, qt * P:(qt + 1) * P], ps[:, 0:P]).then_inc(*frees(("o", l, u)))
                    tally.also("o_ready", (l, br))

                for s in range(len(units) + 2):
                    if s < len(units):
                        maxima(s)
                        softmax(s)
                    if 1 <= s <= len(units):
                        turned(s - 1)
                    if s >= 2:
                        outputs(s - 2)

                ve.wait_ge(dma_out, 16 * (5 * l + 4))
                ve.wait_ge(*made("o_ready", (l, 1)))
                merges = [0]

                def merge(n, j, slot, key):
                    ve.wait_ge(*full(("p", l, n, j)))
                    ps = held(("p", l, n, j))
                    ve.wait_ge(*freed_by(("g", l, n, j)))
                    if n == 0:
                        V.tensor_tensor(tmp[:, j, :], ps[:, 0:T], gsb[:, slot, :], ALU.mult).then_inc(*frees(("p", l, n, j)))
                        tally.also("gate_used", key)
                    else:
                        V.tensor_tensor(prod, ps[:, 0:T], gsb[:, slot, :], ALU.mult).then_inc(*frees(("p", l, n, j)))
                        tally.also("gate_used", key)
                        ve.wait_ge(*freed_by(("p", l, n, j)))
                        V.tensor_tensor(tmp[:, j, :], tmp[:, j, :], prod, ALU.add).then_inc(*signal("merged", (l, n, j)))
                        ve.wait_ge(*made("merged", (l, n, j)))

                def fill_merge(n, j):
                    merge(n, j, merges[0] % GATES, (l, merges[0]))
                    merges[0] += 1

                ve.wait_ge(*made("zeroed", l))
                for hh in range(2):
                    for c in range(4):
                        ve.wait_ge(*freed_by(("fb", l, hh, c)))
                        h = 4 * hh + c
                        step(V.tensor_scalar(Fg[:, c, :], Fg[:, c, :], oml[:, l, h:h + 1], lb[:, l, h:h + 1], ALU.mult, ALU.add))
                        step(V.tensor_scalar(Fg[:, c, :], Fg[:, c, :], F_FLOOR, None, ALU.max))
                        V.tensor_scalar(Kg[:, c, :], Fg[:, c, :], -1.0, 1.0, ALU.mult, ALU.add).then_inc(*signal("fk_ready", (l, hh, c)))
                    ve.wait_ge(*made("fk_ready", (l, hh, 3)))
                    ve.wait_ge(*freed_by(("qc", l, hh, 1)))
                    for tt in range(TT):
                        prev = batches[batches.index((hh, tt)) - 1] if (hh, tt) != batches[0] else None
                        todo = list(fill[hh, tt])
                        decays = decay_steps(V, ve, l, hh, tt, prev, slice(0, HD), 1, 0, "f", step)

                        def place(n):
                            key = ("A", l, hh, tt, n)
                            ve.wait_ge(*full(key))
                            ps = held(key)
                            v = ps[:, :].rearrange("p (d t) -> p d t", d=4)
                            if n == 0:
                                if prev:
                                    ve.wait_ge(*full(("oi", l, *prev)))
                                V.tensor_tensor(Am[:, :, :], v, con[:, IDN:IDN + P].unsqueeze(1).broadcast_to([P, 4, P]), ALU.mult).then_inc(*frees(key))
                            else:
                                V.copy_predicated(Am[:, :, :], lmask[:, n - 1, :].unsqueeze(1).broadcast_to([P, 4, P]), v).then_inc(*frees(key))
                            ve.wait_ge(*freed_by(key))

                        next(decays)
                        for n in range(len(LEVELS) + 1):
                            if n < len(LEVELS):
                                next(decays)
                            else:
                                next(decays)
                            place(n)
                            if n in (1, 3) and todo:
                                fill_merge(*todo.pop(0))
                        while todo:
                            fill_merge(*todo.pop(0))
                        key = ("U", l, hh, tt)
                        ve.wait_ge(*full(key))
                        ps = held(key)
                        hs = slice(4 * hh, 4 * hh + 4)
                        v = ps[:, 0:4 * HD].rearrange("p (d n) -> p d n", d=4)
                        if tt == 0:
                            V.tensor_copy(Sout[:, hs, :], v).then_inc(*frees(key))
                            tally.also("sout", (l, hh))
                        else:
                            ve.wait_ge(dma_state, 32 * (l + 1))
                            r, src, dst = (slice(0, HD), 0, 1) if tt == 1 else (slice(HD, P), 1, 0)
                            if tt == 2:
                                ve.wait_ge(*made("kr_b", (l, hh, 2)))
                            for d in range(4):
                                h = 4 * hh + d
                                ins = V.scalar_tensor_tensor(Sin[r, dst, h, :], Sin[r, src, h, :], dec[r, tt, h:h + 1], v[r, d, :], ALU.mult, ALU.add)
                            ins.then_inc(*frees(key))
                            tally.also("s_f" if tt == 1 else "s_b", (l, hh))
                    key = ("oe", l, hh)
                    ve.wait_ge(*full(key))
                    ps = held(key)
                    ve.wait_ge(*freed_by(("oi", l, hh, 1)))
                    ve.wait_ge(*freed_by(("oi", l, hh, 2)))
                    o = oBr[2][:, 2 * hh:2 * hh + 2, CTX:T]
                    V.tensor_tensor(o, o, ps[:, :].rearrange("p (a n) -> p a n", a=2), ALU.add).then_inc(*frees(key))
                    tally.also("oc_sum", (l, hh))
                for c in range(BT):
                    r = rstd(("hn", l, f"oc{c}"))
                    normalise(l, None, oBr[2][:, c, :], f"oc{c}", CO, r)
                for c in range(BT):
                    ve.wait_ge(*freed_by(("gc", l, c)))
                    ve.wait_ge(*made("normed", (f"oc{c}", l)))
                    V.tensor_tensor(oBr[2][:, c, :], oBr[2][:, c, :], Fg[:, c, :], ALU.mult).then_inc(*signal("oc_gated", (l, c)))
                for j in range(KT):
                    merge(2, j, j % GATES, (l, "c", j))

                def residual(src, key, l2, j, chunk, names):
                    for g, a, b in GROUPS:
                        ins = V.scalar_tensor_tensor(xT[:, j, a:b], src[:, a:b], mod[:, l, chunk * KT + j, g:g + 1], xT[:, j, a:b],
                                                     ALU.mult, ALU.add)
                    return ins

                for j in range(KT):
                    ve.wait_ge(*full(("out", l, j)))
                    ps = held(("out", l, j))
                    residual(ps, None, l, j, 2, None).then_inc(*frees(("out", l, j)))
                    tally.also("x_ready", (l, 2, j))

                norm(l, 2)
                ve.wait_ge(dma_out, 16 * (5 * l + 5))
                route(ve, V, l, step)
                rank = rt[:, 340:388]
                key = ("rank", l)
                ve.wait_ge(*full(key))
                step(V.scalar_tensor_tensor(rank, held(key)[:, 0:TT * NE], 1.0, rt[:, 0:TT * NE], ALU.add, ALU.mult))
                step(V.tensor_scalar(rank, rank, -1.0, None, ALU.add))
                V.tensor_reduce(rt[:, 320:321], held(key)[:, TT * NE:(TT + 1) * NE], AX, ALU.max).then_inc(*frees(key))
                ve.wait_ge(*freed_by(key))
                V.tensor_scalar(flag[:, :], rt[:, 320:321], float(SLOTS), None, ALU.is_gt).then_inc(*signal("flag", l))
                ve.wait_ge(*made("flag", l))
                many = ve.value_load(flag[0:1, 0:1], min_val=0, max_val=1)
                before = dict(tally.count)
                with ve.If(many == 0):
                    dve_short(ve, l, modulation)
                tally.count = before
                with ve.Else():
                    dve_general(ve, l, modulation)
                for j in range(KT):
                    residual(tmp[:, j, :], None, l, j, 5, None).then_inc(*signal("x_ready", (l + 1, 1, j)))

            r = rstd(("n", DEPTH, 1))
            ve.wait_ge(*full(("n", DEPTH, 1)))
            for k in range(KT):
                V.scalar_tensor_tensor(hT[:, k, :], xT[:, k, :], fing[:, k:k + 1], r, ALU.mult, ALU.mult).then_inc(*signal("y_ready", k))

        @block.gpsimd
        def _(po):
            G = nc.gpsimd
            steps = [0]

            def step(ins):
                ins.then_inc(*signal("pool_step", steps[0]))
                steps[0] += 1
                po.wait_ge(sem("pool_step"), steps[0])

            rows = slice(NOPE, NOPE + ROPE)
            for l in range(DEPTH):
                if l:
                    po.wait_ge(*made("x_ready", (l, 1, KT - 1)))
                po.dma_start(keysA[:, :, T:KEYS], A["kcT"][l]).then_inc(dma_cache, 16)
                po.dma_start(vA[:, 3, :], A["vc"][l]).then_inc(dma_cache, 16)
                po.dma_start(ckvT[:, :, T:KEYS], A["ckvcT"][l]).then_inc(dma_cache, 16)
                po.dma_start(krT[rows, T:KEYS], A["krcT"][l]).then_inc(dma_cache, 16)
                po.wait_ge(dma_cache, 16 * NCACHE * (l + 1))
                po.wait_ge(*made("roped", (l, "kr")))
                G.tensor_copy(keysB[rows, :, :], krT[rows, :].unsqueeze(1).broadcast_to([ROPE, HEADS, KEYS])).then_inc(*signal("kr_copied", l))
                po.wait_ge(*made("o_ready", (l, 1)))
                po.wait_ge(dma_out, 16 * (5 * l + 4))
                po.dma_start(Sin[0:HD, 0, :, :], A["s0"][l, 0:HD]).then_inc(dma_state, 16)
                po.dma_start(Sin[HD:P, 1, :, :], A["s0"][l, HD:P]).then_inc(dma_state, 16)
                po.wait_ge(*made("kr_copied", l))
                for i in range(len(LEVELS)):
                    G.memset(Ql[i], 0.0)
                    ins = G.memset(Kl[i], 0.0)
                ins.then_inc(*signal("zeroed", l))
                po.wait_ge(*made("zeroed", l))
                for hh, tt in batches:
                    prev = batches[batches.index((hh, tt)) - 1] if (hh, tt) != batches[0] else None
                    po.wait_ge(*made("fk_ready", (l, hh, 3)))
                    po.wait_ge(*freed_by(("qc", l, hh, 1)))
                    for _ in decay_steps(G, po, l, hh, tt, prev, slice(HD, P), 0, 1, "b", step):
                        pass

        @block.sync
        def _(sp):
            for dst, name in ((xT[:, :, :], "xT"), (con[:, :], "con"), (par[:, :, :], "par"), (cv[:, :, :], "cv"),
                              (lbl[:, :, :], "lbl"), (fing[:, :], "fing"), (region[:, REGION - len(LEVELS) * P:], "lmask")):
                sp.dma_start(dst, A[name]).then_inc(dma_con, 16)

            for i, (l, name, size) in enumerate(order):
                if i >= RING:
                    pl, pn, _ = order[i - RING]
                    if pn[0] == "e":
                        sp.wait_ge(*made("unit_free", (pl, UNITS * int(pn[2:]) + 2 * ("eg", "eu", "ed").index(pn[:2]) + 1)))
                    elif pn[0] == "m" and pl:
                        sp.wait_ge(*made("mod_free", (pl, int(pn[1:]))))
                    else:
                        sp.wait_ge(*full(closing[i - RING]))
                sp.dma_start(slabs[:, i % RING, 0:size], A["W"][i, :, 0:size]).then_inc(dma_slab[i % RING], 16)
                if name == "br0":
                    sp.wait_ge(*made("normed", ("ka", l)))
                    sp.dma_start(A["new_k"][l], knT[:, 0:CTX]).then_inc(dma_out, 16)
                    sp.wait_ge(*freed_by(("va", l)))
                    sp.dma_start(A["new_v"][l], vA[:, 0, :]).then_inc(dma_out, 16)
                    sp.wait_ge(*made("normed", ("kc1", l)))
                    sp.dma_start(A["new_ckv"][l], ckvT[:, :, 0:CTX]).then_inc(dma_out, 16)
                    sp.wait_ge(*freed_by(("kr", l)))
                    sp.dma_start(A["new_kr"][l], krT[NOPE:NOPE + ROPE, 0:CTX]).then_inc(dma_out, 16)
                if name == "o1":
                    sp.wait_ge(*made("sout", (l, 1)))
                    sp.dma_start(A["new_s"][l], Sout[:, :, :]).then_inc(dma_out, 16)
            sp.wait_ge(*made("y_ready", KT - 1))
            sp.dma_start(A["y"], hT[:, :, :]).then_inc(dma_out, 16)
            sp.wait_ge(dma_out, 16 * (5 * DEPTH + 1))

    return tally.here


_IN = ["W", "xT", "con", "lmask", "par", "lbl", "fing", "cv", "kcT", "vc", "ckvcT", "krcT", "s0"]
_OUT = [("y", (P, KT, T)), ("new_k", (DEPTH, P, CTX)), ("new_v", (DEPTH, CTX, P)), ("new_ckv", (DEPTH, P, CT, CTX)),
        ("new_kr", (DEPTH, ROPE, CTX)), ("new_s", (DEPTH, P, HEADS, HD))]


def constants():
    con = np.zeros((P, NCON), np.float32)
    p = np.arange(P)
    con[:, ONES:ONES + P] = 1.0
    con[:, BLK:BLK + P] = (p[:, None] // HD == p[None, :] // HD)
    con[:, IDN:IDN + P] = np.eye(P)
    con[:, TRI:TRI + P] = p[:, None] < p[None, :]
    con[:, IOTA:IOTA + P] = p[None, :]
    row, col = np.arange(LAT) // GRID_W, np.arange(LAT) % GRID_W

    def rotary(width, d):
        half = width // 2
        inv = (np.float32(10000.0) ** (-np.arange(0, half, 2, dtype=np.float32) / np.float32(half))).astype(np.float32)
        pos = np.where((d // half == 0)[:, None], row[None, :], col[None, :]).astype(np.float32)
        ang = pos * inv[d % (half // 2)][:, None]
        sign = np.where(d % half < half // 2, -1.0, 1.0)[:, None]
        return np.cos(ang), np.sin(ang) * sign

    con[:, CA:CA + LAT], con[:, SA:SA + LAT] = rotary(HD, p % HD)
    con[NOPE:QB_W, CB:CB + LAT], con[NOPE:QB_W, SB:SB + LAT] = rotary(ROPE, np.arange(ROPE))
    mask = np.zeros((P, len(LEVELS), P), np.float32)
    for n, b in enumerate(LEVELS):
        mask[:, n] = (p[:, None] // (2 * b) == p[None, :] // (2 * b)) & (p[:, None] // b != p[None, :] // b)
    return con, mask.reshape(P, -1)


def lay_out(inputs):
    x = {k: np.asarray(v) for k, v in inputs.items()}
    f = np.float32

    def tiles(w):
        K, N = w.shape
        return w.reshape(K // P, P, N // P, P).transpose(1, 2, 0, 3).reshape(P, -1)

    def rows(w):
        K, N = w.shape
        return w.reshape(K // P, P, N).transpose(1, 0, 2).reshape(P, -1)

    order = slab_order()
    W = np.zeros((len(order), P, SLAB), f)
    widths = (BW, KV_A * HD, KV_A * HD, Q_RANK, KV_RANK, ROPE, BW, BW, BW, BW, BW, N_BRANCH * D)
    cut = np.cumsum((0,) + widths)
    for i, (l, name, size) in enumerate(order):
        w_in = x["w_in"][l]
        qa, ka, va, qra, kva, kra, ff, fb, qc, ic, gc, gp = [w_in[:, cut[n]:cut[n + 1]] for n in range(12)]
        if name[0] == "m":
            n = int(name[1:])
            s = tiles(x["w_mod"][l][:, n * 512:(n + 1) * 512])
        elif name == "qa":
            s = tiles(qa)
        elif name == "kv":
            s = tiles(np.concatenate([ka, va, kra, np.zeros((D, P - ROPE), f), qra[:, 0:P]], 1))
        elif name == "qr":
            s = tiles(np.concatenate([qra[:, P:], kva], 1))
        elif name == "bwq":
            s = rows(x["b_wq"][l])
        elif name == "bwkv":
            w = x["b_wkv"][l].reshape(KV_RANK, HEADS, 2 * HD)
            s = np.concatenate([rows(w[:, :, :HD].reshape(KV_RANK, BW)), rows(w[:, :, HD:].reshape(KV_RANK, BW))], 1)
        elif name == "ic":
            s = rows(ic)
        elif name in ("fb0", "fb1"):
            w = np.stack([ff.reshape(D, HEADS, HD), fb.reshape(D, HEADS, HD)], 2).reshape(D, 2 * BW)
            s = tiles(w[:, int(name[2]) * BW:(int(name[2]) + 1) * BW])
        elif name in ("qc0", "qc1"):
            s = tiles(qc[:, int(name[2]) * 256:(int(name[2]) + 1) * 256])
        elif name == "gc":
            s = tiles(gc)
        elif name[:2] == "br":
            s = tiles(x["w_branch"][l, int(name[2])])
        elif name[0] == "g":
            n = int(name[1]) * D + int(name[2]) * BW
            s = tiles(gp[:, n:n + BW])
        elif name[:2] == "eg":
            s = rows(x["e_gate"][l, int(name[2:])])
        elif name[:2] == "eu":
            s = rows(x["e_up"][l, int(name[2:])])
        elif name[:2] == "ed":
            s = rows(x["e_down"][l, int(name[2:])])
        else:
            s = tiles(x["w_out"][l][:, int(name[1]) * 512:(int(name[1]) + 1) * 512])
        assert s.shape[1] == size, (name, s.shape, size)
        W[i, :, :size] = s

    col = lambda v: v.reshape(-1, P).T
    twice = lambda v: np.concatenate([v, v])[:, None]
    par = np.stack([np.concatenate([
        col(x["norm1_g"][l]), col(x["norm2_g"][l]), col(x["b_mod"][l]), twice(x["a_qnorm"][l]), twice(x["a_knorm"][l]),
        col(x["b_qnorm"][l]), col(x["b_kvnorm"][l]), twice(x["c_onorm"][l]),
        np.broadcast_to(np.concatenate([x["r_group_b"][l], x["r_expert_b"][l]])[None, :], (P, NG + NE)),
        rows(np.concatenate([x["r_group_w"][l], x["r_expert_w"][l]], 1))], 1) for l in range(DEPTH)], 1)
    con, mask = constants()
    tok = np.concatenate([x["x_prompt"][0], x["x_sample"][0]], 0)
    kc = x["cache_gqa_k"][0].transpose(0, 3, 2, 1)
    return {
        "W": W, "xT": tok.T.reshape(KT, P, T).transpose(1, 0, 2), "con": con, "lmask": mask, "par": par,
        "lbl": x["c_lb_logits"].reshape(DEPTH, 2, HEADS, HD).transpose(1, 3, 0, 2).reshape(P, DEPTH, HEADS),
        "fing": col(x["final_g"]), "cv": np.stack([col(x["c_ctx"]), col(x["c"][0])], 2),
        "kcT": np.concatenate([kc, kc], 1), "vc": x["cache_gqa_v"][0].reshape(DEPTH, PAST, KV_A * HD),
        "ckvcT": x["cache_mla_ckv"][0].transpose(0, 2, 1).reshape(DEPTH, CT, P, PAST).transpose(0, 2, 1, 3),
        "krcT": x["cache_mla_krope"][0].transpose(0, 2, 1),
        "s0": x["state_hgrn"][0].transpose(0, 1, 3, 2, 4).reshape(DEPTH, P, HEADS, HD),
    }


def kernel(**inputs):
    import concourse.bacc as bacc
    from concourse.bass_utils import run_bass_kernel_spmd

    arrays = {k: np.ascontiguousarray(v) for k, v in lay_out(inputs).items()}

    def build(known):
        nc = bacc.Bacc("TRN2", target_bir_lowering=False, num_devices=1)
        A = {n: nc.dram_tensor(f"in_{n}", arrays[n].shape, mybir.dt.from_np(arrays[n].dtype), kind="ExternalInput").ap() for n in _IN}
        for n, shape in _OUT:
            A[n] = nc.dram_tensor(f"out_{n}", shape, F32, kind="ExternalOutput").ap()
        return nc, program(nc, A, known)

    _, found = build({})
    nc, _ = build(found)
    r = run_bass_kernel_spmd(nc, [{f"in_{n}": arrays[n] for n in _IN}], core_ids=[0])
    o = {n: r.results[0][f"out_{n}"] for n, _ in _OUT}
    y = o["y"].transpose(2, 1, 0).reshape(T, D)
    return (y[None, :CTX], y[None, CTX:],
            o["new_k"].reshape(DEPTH, KV_A, HD, CTX).transpose(0, 3, 1, 2)[None],
            o["new_v"].reshape(DEPTH, CTX, KV_A, HD)[None],
            o["new_ckv"].transpose(0, 3, 2, 1).reshape(DEPTH, CTX, KV_RANK)[None],
            o["new_kr"].transpose(0, 2, 1)[None],
            o["new_s"].reshape(DEPTH, 2, HD, HEADS, HD).transpose(0, 1, 3, 2, 4)[None])
```

```python
from contextlib import ExitStack

import numpy as np

import concourse.bass as bass
from concourse import mybir

F32 = mybir.dt.float32
U8 = mybir.dt.uint8
I32 = mybir.dt.int32
F32R = mybir.dt.float32r
ALU = mybir.AluOpType
ACT = mybir.ActivationFunctionType
AX = mybir.AxisListType.X

P = 128
D = 1024
KT = D // P
DEPTH = 2
CTX, LAT, PAST = 128, 256, 128
T = CTX + LAT
TT = T // P
KEYS = T + PAST
GRID_W = 64
EPS = 1e-6
F_FLOOR = 1e-30
HD = 64
HEADS = 8
KV_A = 2
Q_RANK, KV_RANK = 384, 256
NOPE, ROPE = 64, 32
QB_W = NOPE + ROPE
QT, CT = Q_RANK // P, KV_RANK // P
BW = 512
BT = BW // P
N_BRANCH = 3
NCDMA = 5
NCACHE = 4
NG, EG = 4, 4
NE = NG * EG
SLOTS = 128
UNITS = 6
UNIT = 2048
SPLITS = 3
FE = 512
FT = FE // P
SLAB = 4096
RING = 4
GATES = 2
REGION = 19096
BANKS = 8
MODT = 6 * KT
LEVELS = [1 << i for i in range(7)]
GROUPS = ((0, 0, CTX), (1, CTX, T))
SCALE_A = HD ** -0.5
SCALE_B = QB_W ** -0.5
BIG = 1e30

N1, N2, BM, AQ, AK, BQ, BK, CO, RB, RW = np.cumsum([0, KT, KT, MODT, 1, 1, QT, CT, 1, NG + NE]).tolist()
NPAR = RW + KT * (NG + NE)
ONES, BLK, IDN, TRI, IOTA, CA, SA, CB, SB = np.cumsum([0, P, P, P, P, P, LAT, LAT, LAT]).tolist()
NCON = SB + LAT

MIXER = ([("qa", SLAB), ("kv", SLAB), ("qr", SLAB), ("bwq", QT * HEADS * QB_W), ("bwkv", CT * HEADS * 2 * HD), ("ic", SLAB),
          ("fb0", SLAB), ("qc0", SLAB // 2), ("br0", SLAB), ("g00", SLAB), ("g01", SLAB),
          ("fb1", SLAB), ("qc1", SLAB // 2), ("br1", SLAB), ("g10", SLAB), ("g11", SLAB),
          ("gc", SLAB), ("br2", SLAB), ("g20", SLAB), ("g21", SLAB), ("o0", SLAB), ("o1", SLAB)])
NMOD = MODT // 4
OWN = 2
NEXT = NMOD // 3
GAPS = [list(zip(("kr", "kc", "qb", "fb00", "fb01", "fb10", "fb11", "gc", "g2", "g5", "o0", "o1"),
                 [(0, i) for i in range(NEXT, NMOD)] + [(1, i) for i in range(NEXT)])),
        list(zip(("fb00", "fb01", "fb10", "fb11", "gc", "g2", "g5", "o0"), [(1, i) for i in range(NEXT, NMOD)]))]
LOADED_AFTER = {"kr": "kv", "kc": "qr", "qb": "bwq", "fb00": "fb0", "fb01": "fb0", "fb10": "fb1", "fb11": "fb1",
                "gc": "g11", "g2": "g20", "g5": "g21", "o0": "o0", "o1": "o1"}


def slab_order():
    out = [(0, f"m{i}", SLAB) for i in range(NEXT)]
    for l in range(DEPTH):
        for n, s in MIXER:
            out.append((l, n, s))
            out += [(ml, f"m{i}", SLAB) for gap, (ml, i) in GAPS[l] if LOADED_AFTER[gap] == n]
        for e in range(NE):
            out += [(l, f"eg{e}", SLAB), (l, f"eu{e}", SLAB), (l, f"ed{e}", SLAB)]
    return out


def slab_slots(order):
    index = {(l, n): i for i, (l, n, _) in enumerate(order)}
    ends = [index[l, f"g{n[2]}1"] if n[:2] == "br" else i for i, (l, n, _) in enumerate(order)]
    holds, times, out = [None] * RING, [0] * RING, []
    for i in range(len(order)):
        s = min(range(RING), key=lambda s: -1 if holds[s] is None else ends[holds[s]])
        times[s] += 1
        out.append((s, times[s], holds[s]))
        holds[s] = i
    return out


class Tally:

    def __init__(self, known):
        self.known, self.here, self.count, self.last = known, {}, {}, None

    def next(self, name, key):
        self.count[name] = self.count.get(name, 0) + 1
        self.last = self.here[name, key] = (name, self.count[name])

    def also(self, name, key):
        self.here[name, key] = self.last

    def of(self, name, key):
        return self.known.get((name, key), ("dummy", 1)) if not self.known else self.known[name, key]


def program(nc, A, known):
    tally = Tally(known)
    order = slab_order()
    slots = slab_slots(order)
    held_by_bank, closing = {}, {}

    with ExitStack() as ctx:
        def sb(name, shape, dt=F32):
            return ctx.enter_context(nc.sbuf_tensor("sb_" + name, shape, dt))

        sems = {}

        def sem(name):
            if name not in sems:
                sems[name] = ctx.enter_context(nc.semaphore(name))
            return sems[name]

        def signal(name, key):
            tally.next(name, key)
            return sem(name), 1

        def made(name, key):
            s, n = tally.of(name, key)
            return sem(s), n

        def made_now(name):
            return sem(name), tally.count[name]

        unit_read = {}
        index_of = {(l, n): i for i, (l, n, _) in enumerate(order)}

        psum = [ctx.enter_context(nc.psum_tensor(f"bank{b}", [P, 512], F32)) for b in range(BANKS)]
        way = [""]
        uses = {}

        def take(key):
            w = way[0]
            b, n = uses.get(w, 0) % BANKS, uses.get(w, 0) // BANKS
            uses[w] = uses.get(w, 0) + 1
            held_by_bank[key] = (w, b, n)
            return psum[b], (sem(f"bank_free{w}{b}"), n) if n else None

        def readers(w):
            total = uses.get(w, 0)
            return [(sem(f"bank_free{w}{b}"), (total - b + BANKS - 1) // BANKS) for b in range(BANKS) if total > b]

        def held(key):
            return psum[held_by_bank[key][1]]

        def fills(key):
            w, b, n = held_by_bank[key]
            return sem(f"bank_full{w}{b}"), 1

        def full(key):
            w, b, n = held_by_bank[key]
            return sem(f"bank_full{w}{b}"), n + 1

        def frees(key):
            w, b, n = held_by_bank[key]
            tally.last = (f"bank_free{w}{b}", n + 1)
            return sem(f"bank_free{w}{b}"), 1

        def freed_by(key):
            w, b, n = held_by_bank[key]
            return sem(f"bank_free{w}{b}"), n + 1

        con = sb("con", [P, NCON])
        lmask = sb("lmask", [P, len(LEVELS), P], U8)
        par = sb("par", [P, DEPTH, NPAR])
        lbl = sb("lbl", [P, DEPTH, HEADS])
        lbw = sb("lbw", [P, 4, HEADS])
        lb = sb("lb", [P, DEPTH, HEADS])
        oml = sb("oml", [P, DEPTH, HEADS])
        fing = sb("fing", [P, KT])
        cv = sb("cv", [P, KT, 2])
        eps = sb("eps", [P, 1])
        mod = sb("mod", [P, DEPTH, MODT, 2])
        gain = sb("gain", [P, 2, KT, 2])
        xT = sb("xT", [P, KT, T])
        tmp = sb("tmp", [P, KT, T])
        slabs = sb("slabs", [P, RING, SLAB])
        flag = sb("flag", [P, 1], I32)
        small = sb("small", [P, 16])

        base = nc.sbuf_base + (-nc.sbuf_base) % 32
        arena = sb("arena", [P, 3 * T + (KT + N_BRANCH * BT) * T + REGION])
        std = arena[:, 0:3 * T].rearrange("p (a t) -> p a t", a=3)
        hT = arena[:, 3 * T:(3 + KT) * T].rearrange("p (a t) -> p a t", a=KT)
        o0 = (3 + KT) * T
        oBr = [arena[:, o0 + n * BT * T:o0 + (n + 1) * BT * T].rearrange("p (a t) -> p a t", a=BT) for n in range(N_BRANCH)]
        r0 = o0 + N_BRANCH * BT * T
        region = arena[:, r0:r0 + REGION]
        at = [0]

        def part(shape, dt=F32):
            n = int(np.prod(shape[1:]))
            v = region[0:shape[0], at[0]:at[0] + n]
            at[0] += n
            assert at[0] <= REGION, at[0]
            names = "abcd"[:len(shape) - 1]
            if len(shape) > 2:
                v = v.rearrange(f"p ({' '.join(names)}) -> p {' '.join(names)}", **{c: s for c, s in zip(names, shape[1:])})
            return v

        qA = part([P, BT, T])
        knT = part([P, T])
        keysA = part([P, KV_A, KEYS])
        vA = part([P, 4, P])
        qr = part([P, QT, T])
        ckvT = part([P, CT, KEYS])
        krT = part([P, KEYS])
        qB = part([P, HEADS, T])
        keysB = part([P, HEADS, KEYS])
        vB = part([P, 4, BW])
        swp = part([P, LAT])
        nmx = part([P, 2, 2])
        rsum = part([P, 2, 2])
        early = part([P, 2, 4 * P])
        pr = tmp[:, 0:2, :].rearrange("p a t -> p (a t)").rearrange("p (a t) -> p a t", a=2)
        probs = tmp[:, 0:4, :].rearrange("p (u i) t -> p u i t", u=2)
        probsT = tmp[:, 4:8, :].rearrange("p (u i) t -> p u i t", u=2)
        at[0] = 0
        Fg = part([P, 4, T])
        Kg = part([P, 4, T])
        qd = part([P, 4, T])
        vC = part([P, TT, BW])
        Ql = [part([P, 4, P]) for _ in LEVELS]
        Kl = [part([P, 4, P]) for _ in LEVELS]
        after = at[0]
        Pp = part([P, 4, P])
        Rr = part([P, 4, P])
        KRt = part([P, 4, P])
        QP = part([P, 2, 4, P])
        Am = part([P, 4, P])
        end = at[0]
        Sin = part([P, 2, HEADS, HD])
        Sout = part([P, HEADS, HD])
        dec = part([P, TT, HEADS])
        gsb = part([P, GATES, T])
        prod = part([P, T])
        at[0] = 0
        act = part([P, 2, FT, T])
        hg4 = part([P, FT, T])
        cb = part([P, 2, T])
        mt = part([P, T])
        combT = part([P, T])
        at[0] = REGION - 400
        rt = part([P, 400])
        def over(name, shape, offset, dt=F32R):
            return nc.alloc_sbuf_tensor_at("sb_" + name, shape, dt, offset=base + 4 * offset)

        htok = over("htok", [P, 2, TT, D], r0)
        split = over("split", [P, SPLITS, 2, UNIT], r0 + 2 * TT * D)
        wsl = over("wsl", [P, 2], r0 + 2 * TT * D + SPLITS * 2 * UNIT, F32)
        hg = over("hg", [P, 2, 2, KT, SLOTS], 0)
        actT = over("actT", [P, 2, FT, SLOTS], 4096)
        yg = over("yg", [P, 2, D], 5120)
        ag = over("ag", [P, FE], 4096, F32)
        pick = over("pick", [P, TT, 2 * SLOTS], 7168)
        back = [over(f"back{i}", [P, T], 7936 + i * T) for i in range(2)]

        dma_con = sem("dma_con")
        dma_x = sem("dma_x")
        dma_mask = sem("dma_mask")
        dma_cache = sem("dma_cache")
        dma_state = sem("dma_state")
        dma_out = sem("dma_out")
        dma_slab = [sem(f"dma_slab{i}") for i in range(RING)]
        outs = [0]

        def W(l, name):
            return slabs[:, slots[index_of[l, name]][0], :]

        def loaded(l, name):
            s, times, _ = slots[index_of[l, name]]
            return dma_slab[s], 16 * times

        def tile(l, name, c, k=KT):
            return W(l, name)[:, c * k * P:(c + 1) * k * P].rearrange("p (k n) -> p k n", k=k)

        units = [(br, hp, qt) for br in range(2) for hp in range(4) for qt in range(TT)]
        key_cols = lambda qt: (0, CTX) if qt == 0 else (CTX, KEYS)
        key_tiles = lambda qt: [0] if qt == 0 else [1, 2, 3]
        batches = [(hh, tt) for hh in range(2) for tt in range(TT)]
        fill = {(hh, tt): [(hh, j) for j in range(3 * tt, min(3 * tt + 3, KT))] for hh, tt in batches}

        def sums_in(flat):
            return flat.rearrange("p (g n) -> p g n", g=2)

        n_sums = 2 * 4 * P
        mixer_c = arena[:, o0 + 2 * BT * T:o0 + 2 * BT * T + n_sums]
        sums_of = {(0, i): (early, sums_in(mixer_c))[i % 2] for i in range(NEXT)}
        for plan in GAPS:
            for gap, key in plan:
                if gap in ("kr", "kc", "qb"):
                    sums_of[key] = (early, sums_in(mixer_c))[key[1] % 2]
                elif gap[:2] == "fb":
                    i = int(gap[3])
                    sums_of[key] = sums_in(region[:, end - (2 - i) * n_sums:end - (1 - i) * n_sums])
                else:
                    i = ("gc", "g2", "g5", "o0", "o1").index(gap)
                    sums_of[key] = sums_in(region[:, after - (i + 1) * n_sums:after - i * n_sums])

        FILL_STEPS = {3: (0, 1, 2, 3, 5), 2: (0, 2, 4)}
        FILL_READ = {3: (2, 4), 2: (3,)}

        def decay_steps(E, eng, l, hh, tt, prev, r, qs, ks, tag, step):
            cols = slice(tt * P, (tt + 1) * P)
            if prev:
                eng.wait_ge(*full(("kt", l, *prev)))
            E.memset(Rr[r], 1.0)
            step(E.tensor_copy(Pp[r], Fg[r, :, cols]))
            yield
            for n, b in enumerate(LEVELS):
                def halves(x, s, i=None):
                    v = x.rearrange("p a (m s b) -> p a m s b", s=2, b=b)[:, :, :, s, :]
                    if i is None:
                        return v
                    return v[:, :, :, i:i + 1].broadcast_to([HD, 4, P // (2 * b), b])

                edge = b - 1 if qs == 1 else 0
                if prev:
                    eng.wait_ge(*full(("A", l, *prev, n + 1)))
                E.tensor_tensor(halves(Ql[n][r], qs), halves(qd[r, :, cols], qs), halves(Pp[r], qs), ALU.mult)
                E.tensor_tensor(halves(Kl[n][r], ks), halves(Kg[r, :, cols], ks), halves(Rr[r], ks), ALU.mult).then_inc(*signal(f"lev_{tag}", (l, hh, tt, n)))
                eng.wait_ge(*made(f"lev_{tag}", (l, hh, tt, n)))
                step(E.tensor_tensor(halves(Rr[r], ks), halves(Rr[r], ks), halves(Pp[r], qs, edge), ALU.mult))
                step(E.tensor_tensor(halves(Pp[r], qs), halves(Pp[r], qs), halves(Pp[r], ks, edge), ALU.mult))
                yield
            last = P - 1 if qs == 1 else 0
            E.tensor_copy(dec[r, tt, 4 * hh:4 * hh + 4], Pp[r, :, last])
            if tt:
                if hh:
                    eng.wait_ge(*full(("oe", l, 0)))
                E.tensor_tensor(QP[r, tt - 1], qd[r, :, cols], Pp[r], ALU.mult)
            E.tensor_tensor(Rr[r], Rr[r], Kg[r, :, cols], ALU.mult).then_inc(*signal(f"kr_{tag}", (l, hh, tt)))
            if tt == 2:
                tally.also(f"qp_{tag}", (l, hh))
            yield

        def route(ve, V, l, step):
            L = rt[:, 0:TT * (NG + NE)].rearrange("p (t n) -> p t n", t=TT)
            comb = rt[:, 64:64 + TT * NE].rearrange("p (t g e) -> p t g e", t=TT, g=NG)
            gx = rt[:, 112:124].rearrange("p (t n) -> p t n", t=TT)
            ge = rt[:, 128:140].rearrange("p (t n) -> p t n", t=TT)
            ed, ee = rt[:, 140:143], rt[:, 144:147]
            w4 = [rt[:, 160 + 12 * i:172 + 12 * i].rearrange("p (t n) -> p t n", t=TT) for i in range(8)]
            w1 = [rt[:, 280 + 4 * i:283 + 4 * i] for i in range(12)]
            w16 = rt[:, 340:388].rearrange("p (t g e) -> p t g e", t=TT, g=NG)
            pref = rt[:, 392:396]
            b4 = lambda v: v.unsqueeze(2).broadcast_to([P, TT, 4])

            def first_of(out, eq, work, m):
                step(V.tensor_tensor(work, eq, pref.unsqueeze(1).broadcast_to([P, TT, 4]), ALU.mult))
                step(V.tensor_reduce(m, work, AX, ALU.max))
                step(V.tensor_tensor(out, work, b4(m), ALU.is_equal))

            for i in range(4):
                step(V.memset(rt[:, 392 + i:393 + i], float(4 - i)))
            for t in range(TT):
                ve.wait_ge(*full(("r", l, t)))
                V.tensor_tensor(L[:, t, :], held(("r", l, t))[:, 0:NG + NE], par[:, l, RB:RB + NG + NE], ALU.add).then_inc(*frees(("r", l, t)))
            for t in range(TT):
                ve.wait_ge(*freed_by(("r", l, t)))
            step(V.tensor_reduce(w1[0], L[:, :, 0:NG], AX, ALU.max))
            V.tensor_tensor(gx, L[:, :, 0:NG], b4(w1[0]), ALU.subtract).then_inc(*signal("glog", l))
            step(V.tensor_tensor(w4[0], L[:, :, 0:NG], b4(w1[0]), ALU.is_equal))
            first_of(w4[1], w4[0], w4[2], w1[1])
            step(V.tensor_tensor(w16, L[:, :, NG:NG + NE].rearrange("p t (g e) -> p t g e", g=NG),
                                 w4[1].unsqueeze(3).broadcast_to([P, TT, NG, EG]), ALU.mult))
            step(V.tensor_tensor(w4[3], w16[:, :, 0, :], w16[:, :, 1, :], ALU.add))
            step(V.tensor_tensor(w4[3], w4[3], w16[:, :, 2, :], ALU.add))
            step(V.tensor_tensor(w4[3], w4[3], w16[:, :, 3, :], ALU.add))
            step(V.tensor_reduce(w1[2], w4[3], AX, ALU.max))
            step(V.tensor_tensor(w4[0], w4[3], b4(w1[2]), ALU.is_equal))
            first_of(w4[4], w4[0], w4[2], w1[1])
            step(V.scalar_tensor_tensor(w4[5], w4[4], -BIG, w4[3], ALU.mult, ALU.add))
            step(V.tensor_reduce(w1[3], w4[5], AX, ALU.max))
            V.tensor_tensor(ed, w1[3], w1[2], ALU.subtract).then_inc(*signal("ediff", l))
            step(V.tensor_tensor(w4[0], w4[5], b4(w1[3]), ALU.is_equal))
            first_of(w4[6], w4[0], w4[2], w1[1])
            ve.wait_ge(*made("gexp", l))
            step(V.tensor_reduce(w1[4], ge, AX, ALU.add))
            step(V.reciprocal(w1[5], w1[4]))
            ve.wait_ge(*made("eexp", l))
            step(V.tensor_scalar(w1[6], ee, 1.0, None, ALU.add))
            step(V.reciprocal(w1[7], w1[6]))
            step(V.tensor_tensor(w1[8], w1[7], w1[5], ALU.mult))
            step(V.tensor_tensor(w1[9], w1[8], ee, ALU.mult))
            sel = rt[:, 0:TT * NE].rearrange("p (t g e) -> p t g e", t=TT, g=NG)
            step(V.tensor_tensor(w4[5], w4[4], w4[6], ALU.add))
            V.tensor_tensor(sel, w4[1].unsqueeze(3).broadcast_to([P, TT, NG, EG]), w4[5].unsqueeze(2).broadcast_to([P, TT, NG, EG]),
                            ALU.mult).then_inc(*signal("sel", l))
            step(V.tensor_tensor(w4[4], w4[4], b4(w1[8]), ALU.mult))
            step(V.tensor_tensor(w4[6], w4[6], b4(w1[9]), ALU.mult))
            step(V.tensor_tensor(w4[7], w4[4], w4[6], ALU.add))
            V.tensor_tensor(comb, w4[1].unsqueeze(3).broadcast_to([P, TT, NG, EG]), w4[7].unsqueeze(2).broadcast_to([P, TT, NG, EG]),
                                 ALU.mult).then_inc(*signal("comb", l))

        def expert_unit(l, i):
            e, u = divmod(i, UNITS)
            name = f"{('eg', 'eu', 'ed')[u // 2]}{e}"
            return W(l, name)[:, (u % 2) * UNIT:(u % 2 + 1) * UNIT], loaded(l, name)

        SCATTERED = 4

        def pe_short(pe, l, cur):
            W_ = way[0]
            parts = ((0, 0), (0, 1), (1, 0))

            def gather(p):
                pe.wait_ge(*made("picked" + W_, p))
                for part in range(2):
                    for g in range(4):
                        key = ("ga", l, p, part, g)
                        ps, reader = take(key)
                        if reader:
                            pe.wait_ge(*reader)
                        if p == 0:
                            for t in range(TT):
                                pe.wait_ge(*freed_by(("ht", l, t, g // 2)))
                        for i in range(2):
                            c = 2 * g + i
                            for t in range(TT):
                                mm = nc.tensor.matmul(ps[:, i * 2 * SLOTS:(i + 1) * 2 * SLOTS], lhsT=htok[:, part, t, c * P:(c + 1) * P],
                                                      rhs=pick[:, t, :], start=(t == 0), stop=(t == TT - 1))
                        mm.then_inc(*fills(key))

            def way_back(e):
                mine = slice((e % 2) * SLOTS, (e % 2 + 1) * SLOTS)
                ps, reader = take(("ws", l, e))
                if reader:
                    pe.wait_ge(*reader)
                if e == 0:
                    pe.wait_ge(*made("comb", l))
                for t in range(TT):
                    c = 64 + t * NE + e
                    mm = nc.tensor.matmul(ps[:, 0:1], lhsT=pick[:, t, mine].bitcast(F32), rhs=rt[:, c:c + 1], start=(t == 0), stop=(t == TT - 1))
                mm.then_inc(*fills(("ws", l, e)))
                ps, reader = take(("bk", l, e))
                if reader:
                    pe.wait_ge(*reader)
                for t in range(TT):
                    mm = nc.tensor.transpose(ps[:, t * P:(t + 1) * P], pick[:, t, mine].bitcast(F32), con[:, IDN:IDN + P])
                mm.then_inc(*fills(("bk", l, e)))

            def up(e):
                for n, name in enumerate(("gt", "up")):
                    key = (name, l, e)
                    ps, reader = take(key)
                    if reader:
                        pe.wait_ge(*reader)
                    if n == 0:
                        for part in range(2):
                            for g in range(4):
                                pe.wait_ge(*freed_by(("ga", l, e // 2, part, g)))
                    for u in range(2):
                        i = UNITS * e + 2 * n + u
                        pe.wait_ge(*made("unit_free", (l, i)))
                        for k in range(4):
                            for a, w in parts:
                                mm = nc.tensor.matmul(ps[:, :], lhsT=hg[:, e % 2, a, 4 * u + k, :], rhs=split[:, i % SPLITS, w, k * FE:(k + 1) * FE],
                                                      start=(u == 0 and k == 0 and (a, w) == (0, 0)), stop=(u == 1 and k == 3 and (a, w) == (1, 0)))
                        if u == 0:
                            mm.then_inc(*signal("unit_used" + W_, i))
                            unit_read[l, i] = made_now("unit_used" + W_)
                        else:
                            mm.then_inc(*fills(key))
                            unit_read[l, i] = full(key)

            def turn(e):
                key = ("aT", l, e)
                ps, reader = take(key)
                pe.wait_ge(*reader)
                pe.wait_ge(*made("gated" + W_, e))
                for f in range(FT):
                    mm = nc.tensor.transpose(ps[:, f * SLOTS:(f + 1) * SLOTS], ag[:, f * P:(f + 1) * P], con[:, IDN:IDN + P])
                mm.then_inc(*fills(key))

            def down(e):
                ps = []
                for n in range(2):
                    b, reader = take(("y", l, e, n))
                    pe.wait_ge(*reader)
                    ps.append(b)
                pe.wait_ge(*freed_by(("aT", l, e)))
                for u in range(2):
                    i = UNITS * e + 4 + u
                    pe.wait_ge(*made("unit_free", (l, i)))
                    for k in range(2):
                        for n in range(2):
                            for a, w in parts:
                                o = k * D + n * 512
                                mm = nc.tensor.matmul(ps[n][:, :], lhsT=actT[:, a, 2 * u + k, :], rhs=split[:, i % SPLITS, w, o:o + 512],
                                                      start=(u == 0 and k == 0 and (a, w) == (0, 0)), stop=(u == 1 and k == 1 and (a, w) == (1, 0)))
                            if u == 1 and k == 1:
                                mm.then_inc(*fills(("y", l, e, n)))
                    if u == 0:
                        mm.then_inc(*signal("unit_used" + W_, i))
                        unit_read[l, i] = made_now("unit_used" + W_)
                    else:
                        unit_read[l, i] = full(("y", l, e, 1))

            def scatter(e, tiles):
                for j in tiles:
                    key = ("sc", l, e, j)
                    ps, reader = take(key)
                    pe.wait_ge(*reader)
                    if j == 0:
                        pe.wait_ge(*freed_by(("bk", l, e)))
                    if j % 4 == 0:
                        pe.wait_ge(*freed_by(("y", l, e, j // 4)))
                    for a in range(2):
                        mm = nc.tensor.matmul(ps[:, 0:T], lhsT=yg[:, a, j * P:(j + 1) * P], rhs=back[e % 2][:, :], start=(a == 0), stop=(a == 1))
                    mm.then_inc(*fills(key))

            gather(0)
            way_back(0)
            for e in range(NE):
                up(e)
                if e:
                    scatter(e - 1, range(SCATTERED))
                turn(e)
                if e:
                    scatter(e - 1, range(SCATTERED, KT))
                if e + 1 < NE:
                    way_back(e + 1)
                if e % 2 and e + 1 < NE:
                    gather((e + 1) // 2)
                down(e)
            scatter(NE - 1, range(KT))
            cur[0] = index_of[l, f"ed{NE - 1}"]

        def act_high(sc, l, i):
            raw, landed = expert_unit(l, i)
            sc.wait_ge(*landed)
            if i >= SPLITS:
                sc.wait_ge(*unit_read[l, i - SPLITS])
            nc.scalar.activation(split[:, i % SPLITS, 0, :], raw, ACT.Copy).then_inc(*signal(f"highs{l}_", i))

        def act_rows(sc, l, t):
            for g in range(2):
                key = ("ht", l, t, g)
                sc.wait_ge(*full(key))
                nc.scalar.activation(htok[:, 0, t, g * 512:(g + 1) * 512], held(key)[:, :], ACT.Copy).then_inc(*signal("ht_high", (l, t, g)))

        def act_short(sc, l):
            W_ = f"s{l}_"

            def high(i):
                act_high(sc, l, i)

            def gathered(p):
                for part in range(2):
                    for g in range(4):
                        key = ("ga", l, p, part, g)
                        sc.wait_ge(*full(key))
                        nc.scalar.activation(hg[:, :, part, 2 * g:2 * g + 2, :].rearrange("p e k n -> p k e n"),
                                             held(key)[:, :].rearrange("p (k e n) -> p k e n", k=2, e=2), ACT.Copy).then_inc(*frees(key))

            def way_back(e):
                key = ("ws", l, e)
                sc.wait_ge(*full(key))
                nc.scalar.activation(wsl[:, e % 2:e % 2 + 1], held(key)[:, 0:1], ACT.Copy).then_inc(*frees(key))
                key = ("bk", l, e)
                sc.wait_ge(*full(key))
                nc.scalar.activation(back[e % 2][:, :], held(key)[:, 0:T], ACT.Copy).then_inc(*frees(key))

            gathered(0)
            way_back(0)
            for e in range(NE):
                i = UNITS * e
                high(i + 3)
                high(i + 4)
                sc.wait_ge(*full(("gt", l, e)))
                nc.scalar.activation(ag[:, :], held(("gt", l, e))[:, :], ACT.Silu).then_inc(*frees(("gt", l, e)))
                high(i + 5)
                key = ("aT", l, e)
                sc.wait_ge(*full(key))
                nc.scalar.activation(actT[:, 0, :, :].rearrange("p k n -> p (k n)"), held(key)[:, :], ACT.Copy).then_inc(*signal("actT_high" + W_, e))
                if e + 1 < NE and e % 2 == 0:
                    high(i + 6)
                    way_back(e + 1)
                elif e + 1 < NE:
                    way_back(e + 1)
                    gathered((e + 1) // 2)
                    high(i + 6)
                if e + 1 < NE:
                    high(i + 7)
                    high(i + 8)
                for n in range(2):
                    key = ("y", l, e, n)
                    sc.wait_ge(*full(key))
                    sc.wait_ge(*freed_by(("ws", l, e)))
                    nc.scalar.activation(yg[:, 0, n * 512:(n + 1) * 512], held(key)[:, :], ACT.Copy, scale=wsl[:, e % 2:e % 2 + 1])\
                      .then_inc(*signal("y_high" + W_, (e, n)))

        def dve_short(ve, l):
            V = nc.vector
            W_ = f"s{l}_"
            rank = rt[:, 340:388].rearrange("p (t n) -> p t n", t=TT)

            def low(i):
                raw, _ = expert_unit(l, i)
                ve.wait_ge(*made(f"highs{l}_", i))
                V.tensor_tensor(split[:, i % SPLITS, 1, :], raw, split[:, i % SPLITS, 0, :].bitcast(F32), ALU.subtract)\
                 .then_inc(*signal("unit_free", (l, i)))

            def picks(p):
                if p:
                    ve.wait_ge(*full(("bk", l, 2 * p - 1)))
                for t in range(TT):
                    for i in range(2):
                        e = 2 * p + i
                        ins = V.tensor_scalar(pick[:, t, i * SLOTS:(i + 1) * SLOTS], con[:, IOTA:IOTA + SLOTS], rank[:, t, e:e + 1], None, ALU.is_equal)
                ins.then_inc(*signal("picked" + W_, p))

            def scattered(e, tiles):
                for j in tiles:
                    key = ("sc", l, e, j)
                    ve.wait_ge(*full(key))
                    if e:
                        ve.wait_ge(*freed_by(("sc", l, e - 1, j)))
                        V.tensor_tensor(tmp[:, j, :], tmp[:, j, :], held(key)[:, 0:T], ALU.add).then_inc(*frees(key))
                    else:
                        V.tensor_copy(tmp[:, j, :], held(key)[:, 0:T]).then_inc(*frees(key))

            picks(0)
            for i in range(SPLITS):
                low(i)
            for e in range(NE):
                i = UNITS * e
                low(i + 3)
                low(i + 4)
                if e % 2 and e + 1 < NE:
                    picks((e + 1) // 2)
                key = ("up", l, e)
                ve.wait_ge(*full(key))
                ve.wait_ge(*freed_by(("gt", l, e)))
                V.tensor_tensor(ag[:, :], ag[:, :], held(key)[:, :], ALU.mult).then_inc(*frees(key))
                tally.also("gated" + W_, e)
                if e:
                    scattered(e - 1, range(SCATTERED))
                key = ("aT", l, e)
                ve.wait_ge(*made("actT_high" + W_, e))
                V.tensor_tensor(actT[:, 1, :, :].rearrange("p k n -> p (k n)"), held(key)[:, :],
                                actT[:, 0, :, :].bitcast(F32).rearrange("p k n -> p (k n)"), ALU.subtract).then_inc(*frees(key))
                if e % 2:
                    scattered(e - 1, range(SCATTERED, KT))
                    low(i + 5)
                    if e + 1 < NE:
                        low(i + 6)
                else:
                    low(i + 5)
                    low(i + 6)
                    if e:
                        scattered(e - 1, range(SCATTERED, KT))
                if e + 1 < NE:
                    low(i + 7)
                    low(i + 8)
                for n in range(2):
                    key = ("y", l, e, n)
                    ve.wait_ge(*made("y_high" + W_, (e, n)))
                    V.scalar_tensor_tensor(yg[:, 1, n * 512:(n + 1) * 512], held(key)[:, :], wsl[:, e % 2:e % 2 + 1],
                                           yg[:, 0, n * 512:(n + 1) * 512].bitcast(F32), ALU.mult, ALU.subtract).then_inc(*frees(key))
            scattered(NE - 1, range(KT))
            for j in range(KT):
                ve.wait_ge(*freed_by(("sc", l, NE - 1, j)))

        def pe_general(pe, l, slab, gemm):
            def up(e):
                slab(l, f"eg{e}")
                w = W(l, f"eg{e}").rearrange("p (k n) -> p k n", k=KT)
                for f in range(FT):
                    key = ("eg", l, e, f)
                    ps, reader = take(key)
                    if reader:
                        pe.wait_ge(*reader)
                    gemm(key, ps[:, 0:T], [(w[:, k, f * P:(f + 1) * P], hT[:, k, :]) for k in range(KT)])
                slab(l, f"eu{e}")
                w = W(l, f"eu{e}").rearrange("p (k n) -> p k n", k=KT)
                if e == 0:
                    ps, reader = take(("cT", l))
                    if reader:
                        pe.wait_ge(*reader)
                    pe.wait_ge(*made("comb", l))
                    for t in range(TT):
                        mm = nc.tensor.transpose(ps[0:NE, t * P:(t + 1) * P], rt[:, 64 + t * NE:64 + (t + 1) * NE], con[:, IDN:IDN + P])
                    mm.then_inc(*fills(("cT", l)))
                    pe.wait_ge(*freed_by(("cT", l)))
                ps, reader = take(("cb", l, e))
                if reader:
                    pe.wait_ge(*reader)
                gemm(("cb", l, e), ps[:, 0:T], [(con[0:NE, IDN + e:IDN + e + 1].broadcast_to([NE, P]), combT[0:NE, :])])
                for f in range(FT):
                    key = ("eu", l, e, f)
                    ps, reader = take(key)
                    if reader:
                        pe.wait_ge(*reader)
                    gemm(key, ps[:, 0:T], [(w[:, k, f * P:(f + 1) * P], hT[:, k, :]) for k in range(KT)])

            def down(e):
                slab(l, f"ed{e}")
                w = W(l, f"ed{e}").rearrange("p (k n) -> p k n", k=FT)
                for f in range(FT):
                    pe.wait_ge(*made(f"act_g{l}_", (e, f)))
                for j in range(KT):
                    key = ("ed", l, e, j)
                    ps, reader = take(key)
                    if reader:
                        pe.wait_ge(*reader)
                    gemm(key, ps[:, 0:T], [(w[:, k, j * P:(j + 1) * P], act[:, e % 2, k, :]) for k in range(FT)])

            for e in range(NE):
                up(e)
                down(e)

        def act_general(sc, l):
            for e in range(NE):
                for f in range(FT):
                    key = ("eg", l, e, f)
                    sc.wait_ge(*full(key))
                    if e:
                        sc.wait_ge(*made(f"act_g{l}_", (e - 1, f)))
                    nc.scalar.activation(hg4[:, f, :], held(key)[:, 0:T], ACT.Silu).then_inc(*frees(key))
                if e == 0:
                    sc.wait_ge(*full(("cT", l)))
                    nc.scalar.activation(combT[0:NE, :], held(("cT", l))[0:NE, 0:T], ACT.Copy).then_inc(*frees(("cT", l)))
                key = ("cb", l, e)
                sc.wait_ge(*full(key))
                nc.scalar.activation(cb[:, e % 2, :], held(key)[:, 0:T], ACT.Copy).then_inc(*frees(key))

        def dve_general(ve, l):
            V = nc.vector

            def slab_read(k):
                for i in (2 * k, 2 * k + 1):
                    V.memset(small[:, i % 2:i % 2 + 1], 0.0).then_inc(*signal("unit_free", (l, i)))
                    ve.wait_ge(*made("unit_free", (l, i)))

            for e in range(NE):
                ve.wait_ge(*freed_by(("cb", l, e)))
                for f in range(FT):
                    key = ("eu", l, e, f)
                    ve.wait_ge(*full(key))
                    ve.wait_ge(*freed_by(("eg", l, e, f)))
                    V.tensor_tensor(mt, held(key)[:, 0:T], hg4[:, f, :], ALU.mult).then_inc(*frees(key))
                    ve.wait_ge(*freed_by(key))
                    V.tensor_tensor(act[:, e % 2, f, :], mt, cb[:, e % 2, :], ALU.mult).then_inc(*signal(f"act_g{l}_", (e, f)))
                    ve.wait_ge(*made(f"act_g{l}_", (e, f)))
                slab_read(3 * e)
                slab_read(3 * e + 1)
                for j in range(KT):
                    key = ("ed", l, e, j)
                    ve.wait_ge(*full(key))
                    if e:
                        ve.wait_ge(*freed_by(("ed", l, e - 1, j)))
                        V.tensor_tensor(tmp[:, j, :], tmp[:, j, :], held(key)[:, 0:T], ALU.add).then_inc(*frees(key))
                    else:
                        V.tensor_copy(tmp[:, j, :], held(key)[:, 0:T]).then_inc(*frees(key))
                slab_read(3 * e + 2)
            for j in range(KT):
                ve.wait_ge(*freed_by(("ed", l, NE - 1, j)))

        block = ctx.enter_context(nc.Block())

        @block.tensor
        def _(pe):
            cur = [-1]

            def slab(l, name):
                i = index_of[l, name]
                if i != cur[0]:
                    assert all(n[0] == "m" for _, n, _ in order[cur[0] + 1:i]), (l, name)
                    cur[0] = i
                    pe.wait_ge(*loaded(l, name))

            def closes(key):
                closing[cur[0]] = key

            def gemm(key, out, pairs):
                n = len(pairs)
                for i, (w, a) in enumerate(pairs):
                    mm = nc.tensor.matmul(out, lhsT=w, rhs=a, start=(i == 0), stop=(i == n - 1))
                mm.then_inc(*fills(key))

            def norm(l, which):
                ps, reader = take(("n", l, which))
                if reader:
                    pe.wait_ge(*reader)
                for k in range(KT):
                    pe.wait_ge(*made("square", ("x", l, which, k)))
                    mm = nc.tensor.matmul(ps[:, 0:T], lhsT=con[:, ONES:ONES + P], rhs=tmp[:, k, :], start=(k == 0), stop=(k == KT - 1))
                mm.then_inc(*fills(("n", l, which)))

            def modulation(l, i):
                key = ("mod", l, i)
                ps, reader = take(key)
                if reader:
                    pe.wait_ge(*reader)
                own = OWN if (l, i) < (0, NEXT) else 0
                if own:
                    pe.wait_ge(*loaded(l, f"m{i}"))
                    w = W(l, f"m{i}").rearrange("p (k n) -> p k n", k=KT)
                    for c in range(4 - own, 4):
                        for k in range(KT):
                            nc.tensor.matmul(ps[:, 2 * c:2 * c + 2], lhsT=w[:, k, c * P:(c + 1) * P], rhs=cv[:, k, :], start=(k == 0), stop=(k == KT - 1))
                pe.wait_ge(*made("mod_summed", (l, i)))
                for c in range(4 - own):
                    for g in range(2):
                        mm = nc.tensor.matmul(ps[:, 2 * c + g:2 * c + g + 1], lhsT=sums_of[l, i][:, g, c * P:(c + 1) * P],
                                              rhs=con[:, ONES:ONES + 1], start=True, stop=True)
                mm.then_inc(*fills(key))

            def gap(l, name):
                for n, key in GAPS[l]:
                    if n == name:
                        modulation(*key)

            def project(l, name, c, key, last=False):
                slab(l, name)
                ps, reader = take(key)
                if reader:
                    pe.wait_ge(*reader)
                w = tile(l, name, c)
                gemm(key, ps[:, 0:T], [(w[:, k, :], hT[:, k, :]) for k in range(KT)])
                if last:
                    closes(key)

            def head_norm(l, key, lhs, sqs):
                ps, reader = take(("hn", l, key))
                if reader:
                    pe.wait_ge(*reader)
                for i, s in enumerate(sqs):
                    pe.wait_ge(*made("square", (key, l, i)))
                    mm = nc.tensor.matmul(ps[:, 0:T], lhsT=con[:, lhs:lhs + P], rhs=s, start=(i == 0), stop=(i == len(sqs) - 1))
                mm.then_inc(*fills(("hn", l, key)))

            def merge_gate(l, n, j):
                if j == 0:
                    slab(l, f"br{n}")
                    br_slab = cur[0]
                    held[n] = br_slab
                project(l, f"g{n}{j // 4}", j % 4, ("g", l, n, j), last=(j % 4 == 3))

            def merge_branch(l, n, j):
                key = ("p", l, n, j)
                ps, reader = take(key)
                if reader:
                    pe.wait_ge(*reader)
                if j == 0:
                    if n < 2:
                        pe.wait_ge(*made("o_ready", (l, n)))
                    else:
                        pe.wait_ge(*made("oc_gated", (l, BT - 1)))
                w = W(l, f"br{n}").rearrange("p (c k n) -> p c k n", c=KT, k=BT)[:, j]
                gemm(key, ps[:, 0:T], [(w[:, k, :], oBr[n][:, k, :]) for k in range(BT)])
                if j == KT - 1:
                    closing[held[n]] = key

            def merge(l, n, j):
                merge_gate(l, n, j)
                merge_branch(l, n, j)

            held = {}

            pe.wait_ge(dma_con, 16 * NCDMA)
            pe.wait_ge(*made("cond", 0))
            for i in range(NEXT):
                modulation(0, i)

            for l in range(DEPTH):
                norm(l, 1)
                slab(l, "qa")
                banks = []
                for c in range(BT):
                    ps, reader = take(("qa", l, c))
                    if reader:
                        pe.wait_ge(*reader)
                    banks.append(ps)
                for k in range(KT):
                    pe.wait_ge(*made("h_ready", (l, 1, k)))
                    for c in range(BT):
                        mm = nc.tensor.matmul(banks[c][:, 0:T], lhsT=tile(l, "qa", c)[:, k, :], rhs=hT[:, k, :], start=(k == 0), stop=(k == KT - 1))
                        if k == KT - 1:
                            mm.then_inc(*fills(("qa", l, c)))
                closes(("qa", l, BT - 1))
                project(l, "kv", 0, ("ka", l))
                for c in range(BT):
                    head_norm(l, f"qa{c}", BLK, [tmp[:, c, :]])
                va = tile(l, "kv", 1)
                ps, reader = take(("va", l))
                if reader:
                    pe.wait_ge(*reader)
                for t in range(TT):
                    for k in range(KT):
                        mm = nc.tensor.matmul(ps[:, t * P:(t + 1) * P], lhsT=hT[:, k, t * P:(t + 1) * P], rhs=va[:, k, :],
                                              start=(k == 0), stop=(k == KT - 1))
                mm.then_inc(*fills(("va", l)))
                head_norm(l, "ka", BLK, [tmp[:, 4, :]])
                kr = tile(l, "kv", 2)
                ps, reader = take(("kr", l))
                if reader:
                    pe.wait_ge(*reader)
                gemm(("kr", l), ps[NOPE:NOPE + ROPE, 0:T], [(kr[:, k, 0:ROPE], hT[:, k, :]) for k in range(KT)])
                project(l, "kv", 3, ("qr", l, 0), last=True)
                project(l, "qr", 0, ("qr", l, 1))
                project(l, "qr", 1, ("qr", l, 2))
                project(l, "qr", 2, ("kc", l, 0))
                head_norm(l, "qr", ONES, [tmp[:, 5 + c, :] for c in range(QT)])
                project(l, "qr", 3, ("kc", l, 1), last=True)
                gap(l, "kr")
                head_norm(l, "kc", ONES, [tmp[:, c, :] for c in range(CT)])
                slab(l, "bwq")
                w = W(l, "bwq")[:, 0:QT * HEADS * QB_W].rearrange("p (k n) -> p k n", k=QT)
                for c in range(QT):
                    pe.wait_ge(*made("normed", (f"qr{c}", l)))
                for h in range(HEADS):
                    ps, reader = take(("qb", l, h))
                    if reader:
                        pe.wait_ge(*reader)
                    gemm(("qb", l, h), ps[0:QB_W, 0:T], [(w[:, k, h * QB_W:(h + 1) * QB_W], qr[:, k, :]) for k in range(QT)])
                closes(("qb", l, HEADS - 1))
                gap(l, "kc")
                slab(l, "bwkv")
                w = W(l, "bwkv")[:, 0:CT * BW].rearrange("p (k n) -> p k n", k=CT)
                wv = W(l, "bwkv")[:, CT * BW:2 * CT * BW].rearrange("p (k n) -> p k n", k=CT)
                for c in range(CT):
                    pe.wait_ge(*made("normed", (f"kc{c}", l)))
                pe.wait_ge(dma_cache, 16 * NCACHE * (l + 1))
                for hp in range(HEADS // 2):
                    ps, reader = take(("kb", l, hp))
                    if reader:
                        pe.wait_ge(*reader)
                    gemm(("kb", l, hp), ps[:, :], [(w[:, k, hp * P:(hp + 1) * P], ckvT[:, k, :]) for k in range(CT)])
                for t in range(4):
                    ps, reader = take(("vb", l, t))
                    if reader:
                        pe.wait_ge(*reader)
                    gemm(("vb", l, t), ps[:, :], [(ckvT[:, k, t * P:(t + 1) * P], wv[:, k, :]) for k in range(CT)])
                closes(("vb", l, 3))
                gap(l, "qb")

                def scores(u):
                    br, hp, qt = units[u]
                    c0, c1 = key_cols(qt)
                    for i in range(2):
                        h = 2 * hp + i
                        ps, reader = take(("s", l, u, i))
                        if reader:
                            pe.wait_ge(*reader)
                        if br == 0:
                            r = slice(HD * i, HD * i + HD)
                            if u == 0 and i == 0:
                                pe.wait_ge(*made("dup", (l, 3)))
                            pe.wait_ge(*made("roped", (l, hp)))
                            q, k = qA[r, hp, qt * P:(qt + 1) * P], keysA[r, h // 4, c0:c1]
                        else:
                            pe.wait_ge(*made("roped", (l, "qb")))
                            pe.wait_ge(*made("kr_copied", l))
                            pe.wait_ge(*freed_by(("kb", l, hp)))
                            q, k = qB[0:QB_W, h, qt * P:(qt + 1) * P], keysB[0:QB_W, h, c0:c1]
                        gemm(("s", l, u, i), ps[:, 0:c1 - c0], [(q, k)])

                def turn(u):
                    br, hp, qt = units[u]
                    for i in range(2):
                        ps, reader = take(("t", l, u, i))
                        if reader:
                            pe.wait_ge(*reader)
                        pe.wait_ge(*made("probs", (l, u, i)))
                        for t in range(len(key_tiles(qt))):
                            mm = nc.tensor.transpose(ps[:, t * P:(t + 1) * P], probs[:, u % 2, i, t * P:(t + 1) * P], con[:, IDN:IDN + P])
                        mm.then_inc(*fills(("t", l, u, i)))

                def values(u):
                    br, hp, qt = units[u]
                    ps, reader = take(("o", l, u))
                    if reader:
                        pe.wait_ge(*reader)
                    if u == 0:
                        pe.wait_ge(*freed_by(("va", l)))
                    if br == 1:
                        pe.wait_ge(*freed_by(("vb", l, 3)))
                    for i in range(2):
                        h = 2 * hp + i
                        pe.wait_ge(*freed_by(("t", l, u, i)))
                        for t, kt in enumerate(key_tiles(qt)):
                            v = vA[:, kt, (h // 4) * HD:(h // 4 + 1) * HD] if br == 0 else vB[:, kt, h * HD:(h + 1) * HD]
                            mm = nc.tensor.matmul(ps[HD * i:HD * i + HD, 0:P], lhsT=v, rhs=probsT[:, u % 2, i, t * P:(t + 1) * P],
                                                  start=(t == 0), stop=(t == len(key_tiles(qt)) - 1))
                    mm.then_inc(*fills(("o", l, u)))

                for s in range(len(units) + 2):
                    if s < len(units):
                        scores(s)
                    if 1 <= s <= len(units):
                        turn(s - 1)
                    if s >= 2:
                        values(s - 2)

                slab(l, "ic")
                w = W(l, "ic").rearrange("p (k n) -> p k n", k=KT)
                for t in range(TT):
                    ps, reader = take(("ic", l, t))
                    if reader:
                        pe.wait_ge(*reader)
                    gemm(("ic", l, t), ps[:, :], [(hT[:, k, t * P:(t + 1) * P], w[:, k, :]) for k in range(KT)])
                closes(("ic", l, TT - 1))
                for hh in range(2):
                    for c in range(4):
                        project(l, f"fb{hh}", c, ("fb", l, hh, c), last=(c == 3))
                    for c in range(2):
                        project(l, f"qc{hh}", c, ("qc", l, hh, c), last=(c == 1))
                        gap(l, f"fb{hh}{c}")
                    for tt in range(TT):
                        cols = slice(tt * P, (tt + 1) * P)
                        todo = [(half, *m) for m in fill[hh, tt] for half in (merge_gate, merge_branch)]
                        for n in range(len(LEVELS) + 1):
                            ps, reader = take(("A", l, hh, tt, n))
                            if reader:
                                pe.wait_ge(*reader)
                            if n == 0:
                                pe.wait_ge(*made("fk_ready", (l, hh, 3)))
                                pe.wait_ge(*freed_by(("qc", l, hh, 1)))
                            else:
                                pe.wait_ge(*made("lev_f", (l, hh, tt, n - 1)))
                                pe.wait_ge(*made("lev_b", (l, hh, tt, n - 1)))
                            for d in range(4):
                                kk, qq = (Kg[:, d, cols], qd[:, d, cols]) if n == 0 else (Kl[n - 1][:, d, :], Ql[n - 1][:, d, :])
                                mm = nc.tensor.matmul(ps[:, d * P:(d + 1) * P], lhsT=kk, rhs=qq, start=True, stop=True)
                            mm.then_inc(*fills(("A", l, hh, tt, n)))
                            if n in FILL_STEPS[len(fill[hh, tt])]:
                                half, *m = todo.pop(0)
                                half(l, *m)
                        ps, reader = take(("kt", l, hh, tt))
                        if reader:
                            pe.wait_ge(*reader)
                        pe.wait_ge(*made("kr_f", (l, hh, tt)))
                        pe.wait_ge(*made("kr_b", (l, hh, tt)))
                        for d in range(4):
                            mm = nc.tensor.transpose(ps[:, d * P:(d + 1) * P], Rr[:, d, :], con[:, IDN:IDN + P])
                        mm.then_inc(*fills(("kt", l, hh, tt)))
                        for half, *m in todo:
                            half(l, *m)
                        if hh == 0 and tt == 0:
                            pe.wait_ge(*freed_by(("ic", l, TT - 1)))
                        ps, reader = take(("U", l, hh, tt))
                        if reader:
                            pe.wait_ge(*reader)
                        pe.wait_ge(*freed_by(("kt", l, hh, tt)))
                        for d in range(4):
                            h = 4 * hh + d
                            mm = nc.tensor.matmul(ps[:, d * HD:(d + 1) * HD], lhsT=KRt[:, d, :], rhs=vC[:, tt, h * HD:(h + 1) * HD],
                                                  start=True, stop=True)
                        mm.then_inc(*fills(("U", l, hh, tt)))
                        ps, reader = take(("oi", l, hh, tt))
                        if reader:
                            pe.wait_ge(*reader)
                        pe.wait_ge(*freed_by(("A", l, hh, tt, len(LEVELS))))
                        for d in range(4):
                            h = 4 * hh + d
                            mm = nc.tensor.matmul(ps[HD * (d % 2):HD * (d % 2) + HD, (d // 2) * P:(d // 2 + 1) * P],
                                                  lhsT=vC[:, tt, h * HD:(h + 1) * HD], rhs=Am[:, d, :], start=True, stop=True)
                        mm.then_inc(*fills(("oi", l, hh, tt)))
                    ps, reader = take(("oe", l, hh))
                    if reader:
                        pe.wait_ge(*reader)
                    pe.wait_ge(*made("s_f", (l, hh)))
                    pe.wait_ge(*made("s_b", (l, hh)))
                    pe.wait_ge(*made("qp_f", (l, hh)))
                    pe.wait_ge(*made("qp_b", (l, hh)))
                    for t in range(2):
                        for d in range(4):
                            h = 4 * hh + d
                            o = (d // 2) * 2 * P + t * P
                            mm = nc.tensor.matmul(ps[HD * (d % 2):HD * (d % 2) + HD, o:o + P], lhsT=Sin[:, t, h, :], rhs=QP[:, t, d, :],
                                                  start=True, stop=True)
                    mm.then_inc(*fills(("oe", l, hh)))
                for c in range(BT):
                    project(l, "gc", c, ("gc", l, c), last=(c == BT - 1))
                    head_norm(l, f"oc{c}", BLK, [gsb[:, c % 2, :]])
                for j in range(KT):
                    merge(l, 2, j)
                    if j == 2:
                        gap(l, "gc")
                    if j == 5:
                        gap(l, "g2")
                for j in range(KT):
                    slab(l, f"o{j // 4}")
                    w = tile(l, f"o{j // 4}", j % 4)
                    if j == 0:
                        pe.wait_ge(*made("merged", (l, 2, KT - 1)))
                    ps, reader = take(("out", l, j))
                    if reader:
                        pe.wait_ge(*reader)
                    gemm(("out", l, j), ps[:, 0:T], [(w[:, k, :], tmp[:, k, :]) for k in range(KT)])
                    if j == 1:
                        gap(l, "g5")
                    if j % 4 == 3:
                        closes(("out", l, j))
                        gap(l, f"o{j // 4}")

                norm(l, 2)
                logits = []
                for t in range(TT):
                    ps, reader = take(("r", l, t))
                    pe.wait_ge(*reader)
                    logits.append(ps)
                rw = par[:, l, RW:RW + KT * (NG + NE)].rearrange("p (k n) -> p k n", k=KT)
                for k in range(KT):
                    pe.wait_ge(*made("h_ready", (l, 2, k)))
                    for t in range(TT):
                        mm = nc.tensor.matmul(logits[t][:, 0:NG + NE], lhsT=hT[:, k, t * P:(t + 1) * P], rhs=rw[:, k, :],
                                              start=(k == 0), stop=(k == KT - 1))
                        if k == KT - 1:
                            mm.then_inc(*fills(("r", l, t)))
                for t in range(TT):
                    for g in range(2):
                        key = ("ht", l, t, g)
                        ps, reader = take(key)
                        pe.wait_ge(*reader)
                        for i in range(4):
                            mm = nc.tensor.transpose(ps[:, i * P:(i + 1) * P], hT[:, 4 * g + i, t * P:(t + 1) * P], con[:, IDN:IDN + P])
                        mm.then_inc(*fills(key))

                ps, reader = take(("rank", l))
                pe.wait_ge(*reader)
                pe.wait_ge(*made("sel", l))
                sel = rt[:, 0:TT * NE].rearrange("p (t n) -> p t n", t=TT)
                for t in range(TT):
                    for s in range(t + 1):
                        w = TRI if s == t else ONES
                        nc.tensor.matmul(ps[:, t * NE:(t + 1) * NE], lhsT=con[:, w:w + P], rhs=sel[:, s, :], start=(s == 0), stop=(s == t))
                for t in range(TT):
                    mm = nc.tensor.matmul(ps[:, TT * NE:(TT + 1) * NE], lhsT=con[:, ONES:ONES + P], rhs=sel[:, t, :], start=(t == 0),
                                          stop=(t == TT - 1))
                mm.then_inc(*fills(("rank", l)))
                for s in readers(""):
                    pe.wait_ge(*s)
                pe.wait_ge(*made("flag", l))
                many = pe.value_load(flag[0:1, 0:1], min_val=0, max_val=1)
                first = cur[0]
                with pe.If(many == 0):
                    way[0] = f"s{l}_"
                    pe_short(pe, l, cur)
                    for s in readers(way[0]):
                        pe.wait_ge(*s)
                cur[0] = first
                with pe.Else():
                    way[0] = f"g{l}_"
                    pe_general(pe, l, slab, gemm)
                    for s in readers(way[0]):
                        pe.wait_ge(*s)
                way[0] = ""
            norm(DEPTH, 1)

        @block.scalar
        def _(sc):
            def squares_x(l, which):
                if l == 0 and which == 1:
                    sc.wait_ge(dma_x, 16)
                for k in range(KT):
                    if not (l == 0 and which == 1):
                        sc.wait_ge(*made("x_ready", (l, which, k)))
                    nc.scalar.activation(tmp[:, k, :], xT[:, k, :], ACT.Square).then_inc(*signal("square", ("x", l, which, k)))
                root(("n", l, which), 1.0 / D, ("n", l, which))

            nroot = [0]

            def root(bkey, scale, key):
                sc.wait_ge(*full(bkey))
                ps = held(bkey)
                s = nroot[0] % 3
                if nroot[0] >= 3:
                    sc.wait_ge(*made("std_used", nroot[0] - 3))
                nc.scalar.activation(std[:, s, :], ps[:, 0:T], ACT.Sqrt, scale=scale, bias=eps[:, 0:1]).then_inc(*frees(bkey))
                nroot[0] += 1

            def split(bkey, dst, sq, key, l, i, wait=None):
                sc.wait_ge(*full(bkey))
                ps = held(bkey)
                if wait:
                    wait()
                nc.scalar.activation(sq, ps[:, 0:T], ACT.Square).then_inc(*signal("square", (key, l, i)))
                nc.scalar.activation(dst, ps[:, 0:T], ACT.Copy).then_inc(*frees(bkey))

            sc.wait_ge(dma_con, 16 * NCDMA)
            sc.wait_ge(*made("eps", 0))
            nc.scalar.activation(cv[:, :, :], cv[:, :, :], ACT.Silu).then_inc(*signal("cond", 0))
            sc.wait_ge(*made("lbmax", 0))
            nc.scalar.activation(lbw[:, 2:4, :], lbw[:, 0:2, :], ACT.Exp).then_inc(*signal("lbexp", 0))

            for l in range(DEPTH):
                squares_x(l, 1)
                for c in range(BT):
                    split(("qa", l, c), qA[:, c, :], tmp[:, c, :], f"qa{c}", l, 0)
                for c in range(BT - 1):
                    root(("hn", l, f"qa{c}"), 1.0 / HD, ("qa", c))
                split(("ka", l), knT[:, :], tmp[:, 4, :], "ka", l, 0)
                root(("hn", l, "qa3"), 1.0 / HD, ("qa", 3))
                sc.wait_ge(*full(("va", l)))
                ps = held(("va", l))
                ins = nc.scalar.activation(vA[:, 0:TT, :].rearrange("p a n -> p (a n)"), ps[:, 0:T], ACT.Copy)
                ins.then_inc(*frees(("va", l)))
                root(("hn", l, "ka"), 1.0 / HD, "ka")
                sc.wait_ge(*full(("kr", l)))
                ps = held(("kr", l))
                nc.scalar.activation(krT[NOPE:NOPE + ROPE, 0:T], ps[NOPE:NOPE + ROPE, 0:T], ACT.Copy).then_inc(*frees(("kr", l)))
                for c in range(QT):
                    split(("qr", l, c), qr[:, c, :], tmp[:, 5 + c, :], "qr", l, c)
                split(("kc", l, 0), ckvT[:, 0, 0:T], tmp[:, 0, :], "kc", l, 0)
                root(("hn", l, "qr"), 1.0 / Q_RANK, "qr")
                split(("kc", l, 1), ckvT[:, 1, 0:T], tmp[:, 1, :], "kc", l, 1)
                root(("hn", l, "kc"), 1.0 / KV_RANK, "kc")
                sc.wait_ge(*made("roped", (l, "ka")))
                for j in range(KV_A):
                    for r in range(2):
                        nc.scalar.activation(keysA[HD * r:HD * r + HD, j, 0:T], knT[HD * j:HD * j + HD, :], ACT.Copy).then_inc(*signal("dup", (l, 2 * j + r)))
                for h in range(HEADS):
                    sc.wait_ge(*full(("qb", l, h)))
                    ps = held(("qb", l, h))
                    nc.scalar.activation(qB[0:QB_W, h, :], ps[0:QB_W, 0:T], ACT.Copy).then_inc(*frees(("qb", l, h)))
                for hp in range(HEADS // 2):
                    sc.wait_ge(*full(("kb", l, hp)))
                    ps = held(("kb", l, hp))
                    nc.scalar.activation(keysB[0:NOPE, 2 * hp, :], ps[0:HD, :], ACT.Copy).then_inc(*signal("kb_part", (l, hp)))
                    nc.scalar.activation(keysB[0:NOPE, 2 * hp + 1, :], ps[HD:P, :], ACT.Copy).then_inc(*frees(("kb", l, hp)))
                for t in range(4):
                    sc.wait_ge(*full(("vb", l, t)))
                    ps = held(("vb", l, t))
                    nc.scalar.activation(vB[:, t, :], ps[:, :], ACT.Copy).then_inc(*frees(("vb", l, t)))

                def exps(u):
                    br, hp, qt = units[u]
                    c0, c1 = key_cols(qt)
                    for i in range(2):
                        sc.wait_ge(*made("negmax", (l, u, i)))
                        sc.wait_ge(*full(("s", l, u, i)))
                        ps = held(("s", l, u, i))
                        if u < 2 and i == 0:
                            sc.wait_ge(*made("roped", (l, "qb")))
                        if u >= 2:
                            sc.wait_ge(*full(("t", l, u - 2, i)))
                        nc.scalar.activation(probs[:, u % 2, i, 0:c1 - c0], ps[:, 0:c1 - c0], ACT.Exp, bias=nmx[:, u % 2, i:i + 1],
                                                   scale=(SCALE_A, SCALE_B)[br], accum_out=rsum[:, u % 2, i:i + 1]).then_inc(*frees(("s", l, u, i)))

                def probs_turned(u):
                    br, hp, qt = units[u]
                    n = P * len(key_tiles(qt))
                    if u >= 2:
                        sc.wait_ge(*full(("o", l, u - 2)))
                    for i in range(2):
                        sc.wait_ge(*full(("t", l, u, i)))
                        nc.scalar.activation(probsT[:, u % 2, i, 0:n], held(("t", l, u, i))[:, 0:n], ACT.Copy).then_inc(*frees(("t", l, u, i)))

                for s in range(len(units) + 1):
                    if s < len(units):
                        exps(s)
                    if s >= 1:
                        probs_turned(s - 1)

                sc.wait_ge(*made("o_ready", (l, 1)))
                sc.wait_ge(dma_out, 16 * (5 * l + 4))
                for t in range(TT):
                    sc.wait_ge(*full(("ic", l, t)))
                    ps = held(("ic", l, t))
                    nc.scalar.activation(vC[:, t, :], ps[:, :], ACT.Copy).then_inc(*frees(("ic", l, t)))
                gates = [0]

                def gate(n, j):
                    sc.wait_ge(*full(("g", l, n, j)))
                    ps = held(("g", l, n, j))
                    if gates[0] >= GATES:
                        sc.wait_ge(*made("gate_used", (l, gates[0] - GATES)))
                    nc.scalar.activation(gsb[:, gates[0] % GATES, :], ps[:, 0:T], ACT.Sigmoid).then_inc(*frees(("g", l, n, j)))
                    gates[0] += 1

                for hh in range(2):
                    for c in range(4):
                        sc.wait_ge(*full(("fb", l, hh, c)))
                        ps = held(("fb", l, hh, c))
                        if hh:
                            sc.wait_ge(*full(("oi", l, 0, TT - 1)))
                            sc.wait_ge(*made("kr_f", (l, 0, TT - 1)))
                            sc.wait_ge(*made("kr_b", (l, 0, TT - 1)))
                        nc.scalar.activation(Fg[:, c, :], ps[:, 0:T], ACT.Sigmoid).then_inc(*frees(("fb", l, hh, c)))
                    for c in range(2):
                        sc.wait_ge(*full(("qc", l, hh, c)))
                        ps = held(("qc", l, hh, c))
                        for i in range(2):
                            for r in range(2):
                                ins = nc.scalar.activation(qd[HD * r:HD * r + HD, 2 * c + i, :], ps[HD * i:HD * i + HD, 0:T], ACT.Copy)
                                if (i, r) == (1, 1):
                                    ins.then_inc(*frees(("qc", l, hh, c)))
                                else:
                                    ins.then_inc(*signal("qd_part", (l, hh, c, i, r)))
                    for tt in range(TT):
                        todo = list(fill[hh, tt])
                        while todo:
                            gate(*todo.pop(0))
                        sc.wait_ge(*full(("kt", l, hh, tt)))
                        ps = held(("kt", l, hh, tt))
                        if not (hh == 0 and tt == 0):
                            ph, pt = batches[batches.index((hh, tt)) - 1]
                            sc.wait_ge(*full(("U", l, ph, pt)))
                        nc.scalar.activation(KRt[:, :, :].rearrange("p a n -> p (a n)"), ps[:, :], ACT.Copy).then_inc(*frees(("kt", l, hh, tt)))
                        sc.wait_ge(*full(("oi", l, hh, tt)))
                        ps = held(("oi", l, hh, tt))
                        nc.scalar.activation(oBr[2][:, 2 * hh:2 * hh + 2, tt * P:(tt + 1) * P],
                                                   ps[:, 0:2 * P].rearrange("p (a n) -> p a n", a=2), ACT.Copy).then_inc(*frees(("oi", l, hh, tt)))
                sc.wait_ge(*made("oc_sum", (l, 1)))
                sc.wait_ge(*made("gate_used", (l, gates[0] - 1)))
                for c in range(BT):
                    if c >= 2:
                        sc.wait_ge(*full(("hn", l, f"oc{c - 2}")))
                    nc.scalar.activation(gsb[:, c % 2, :], oBr[2][:, c, :], ACT.Square).then_inc(*signal("square", (f"oc{c}", l, 0)))
                    root(("hn", l, f"oc{c}"), 1.0 / HD, "oc")
                for c in range(BT):
                    sc.wait_ge(*full(("gc", l, c)))
                    ps = held(("gc", l, c))
                    nc.scalar.activation(Fg[:, c, :], ps[:, 0:T], ACT.Silu).then_inc(*frees(("gc", l, c)))
                gates[0] = 0
                sc.wait_ge(*made("oc_gated", (l, BT - 1)))
                sc.wait_ge(*full(("hn", l, "oc3")))
                for j in range(KT):
                    sc.wait_ge(*full(("g", l, 2, j)))
                    ps = held(("g", l, 2, j))
                    if j >= GATES:
                        sc.wait_ge(*made("gate_used", (l, "c", j - GATES)))
                    nc.scalar.activation(gsb[:, j % GATES, :], ps[:, 0:T], ACT.Sigmoid).then_inc(*frees(("g", l, 2, j)))

                sc.wait_ge(*full(("out", l, KT - 1)))
                squares_x(l, 2)
                sc.wait_ge(*made("glog", l))
                nc.scalar.activation(rt[:, 128:128 + TT * NG], rt[:, 112:112 + TT * NG], ACT.Exp).then_inc(*signal("gexp", l))
                sc.wait_ge(*made("ediff", l))
                nc.scalar.activation(rt[:, 144:144 + TT], rt[:, 140:140 + TT], ACT.Exp).then_inc(*signal("eexp", l))
                sc.wait_ge(dma_out, 16 * (5 * l + 5))
                for t in range(TT):
                    act_rows(sc, l, t)
                for i in range(SPLITS):
                    act_high(sc, l, i)
                sc.wait_ge(*made("flag", l))
                many = sc.value_load(flag[0:1, 0:1], min_val=0, max_val=1)
                with sc.If(many == 0):
                    act_short(sc, l)
                with sc.Else():
                    act_general(sc, l)
            squares_x(DEPTH, 1)

        @block.vector
        def _(ve):
            V = nc.vector
            steps = [0]

            def step(ins):
                ins.then_inc(*signal("dve_step", steps[0]))
                steps[0] += 1
                ve.wait_ge(sem("dve_step"), steps[0])

            nrec = [0]

            def rstd(bkey):
                s = nrec[0] % 3
                nrec[0] += 1
                ve.wait_ge(*freed_by(bkey))
                step(V.reciprocal(std[:, s, :], std[:, s, :]))
                return std[:, s, :]

            def std_used():
                tally.also("std_used", nrec[0] - 1)

            def sum_modulation(l, i):
                n = (4 - OWN if (l, i) < (0, NEXT) else 4) * P
                w, sums = W(l, f"m{i}").rearrange("p (k n) -> p k n", k=KT), sums_of[l, i]
                ve.wait_ge(*loaded(l, f"m{i}"))
                for k in range(KT):
                    for g in range(2):
                        if k == 0:
                            ins = V.tensor_scalar(sums[:, g, 0:n], w[:, k, 0:n], cv[:, k, g:g + 1], None, ALU.mult)
                        else:
                            ve.wait_ge(*made("mod_partial", (l, i, k - 1, g)))
                            ins = V.scalar_tensor_tensor(sums[:, g, 0:n], w[:, k, 0:n], cv[:, k, g:g + 1], sums[:, g, 0:n], ALU.mult, ALU.add)
                        ins.then_inc(*signal("mod_partial", (l, i, k, g)))
                tally.also("mod_summed", (l, i))

            def modulation(l, i):
                ve.wait_ge(*full(("mod", l, i)))
                ps = held(("mod", l, i))
                V.tensor_tensor(mod[:, l, 4 * i:4 * i + 4, :], ps[:, 0:8].rearrange("p (c g) -> p c g", g=2),
                                par[:, l, BM + 4 * i:BM + 4 * i + 4].unsqueeze(2).broadcast_to([P, 4, 2]), ALU.add).then_inc(*frees(("mod", l, i)))

            def gap(l, name):
                for n, key in GAPS[l]:
                    if n == name:
                        sum_modulation(*key)

            def gap_done(l, name):
                for n, key in GAPS[l]:
                    if n == name:
                        modulation(*key)

            def norm(l, which):
                sh, n0 = (0, N1) if which == 1 else (3 * KT, N2)
                ve.wait_ge(*freed_by(("mod", l, NEXT - 1 if which == 1 else 5 * KT // 4 - 1)))
                step(V.scalar_tensor_tensor(gain[:, which - 1, :, :], mod[:, l, sh + KT:sh + 2 * KT, :], 1.0,
                                            par[:, l, n0:n0 + KT].unsqueeze(2).broadcast_to([P, KT, 2]), ALU.add, ALU.mult))
                r = rstd(("n", l, which))
                ve.wait_ge(*full(("n", l, which)))
                for k in range(KT):
                    step(V.tensor_tensor(tmp[:, k, :], xT[:, k, :], r, ALU.mult))
                    for g, a, b in GROUPS:
                        ins = V.tensor_scalar(hT[:, k, a:b], tmp[:, k, a:b], gain[:, which - 1, k, g:g + 1], mod[:, l, sh + k, g:g + 1],
                                              ALU.mult, ALU.add)
                    ins.then_inc(*signal("h_ready", (l, which, k)))
                std_used()

            def normalise(l, key, dst, name, col, r):
                V.scalar_tensor_tensor(dst, dst, par[:, l, col:col + 1], r, ALU.mult, ALU.mult).then_inc(*signal("normed", (name, l)))
                std_used()

            def rope(dst, work, c, s, half, key):
                step(V.stream_shuffle(work, dst, [(i // (2 * half)) * 2 * half + (i + half) % (2 * half) for i in range(32)]))
                step(V.tensor_tensor(work, work, s, ALU.mult))
                step(V.tensor_tensor(dst, dst, c, ALU.mult))
                V.tensor_tensor(dst, dst, work, ALU.add).then_inc(*signal("roped", key))

            V.memset(eps[:, :], EPS).then_inc(*signal("eps", 0))
            ve.wait_ge(dma_con, 16 * NCDMA)
            step(V.tensor_tensor(small[:, 0:HEADS], lbl[:, 0, :], lbl[:, 1, :], ALU.max))
            V.tensor_tensor(lbw[:, 0:2, :], lbl[:, :, :], small[:, 0:HEADS].unsqueeze(1).broadcast_to([P, 2, HEADS]), ALU.subtract).then_inc(*signal("lbmax", 0))
            ve.wait_ge(*made("lbexp", 0))
            step(V.tensor_tensor(small[:, 0:HEADS], lbw[:, 2, :], lbw[:, 3, :], ALU.add))
            step(V.reciprocal(small[:, 8:16], small[:, 0:HEADS]))
            step(V.tensor_tensor(lbw[:, 0:2, :], lbw[:, 2:4, :], small[:, 8:16].unsqueeze(1).broadcast_to([P, 2, HEADS]), ALU.mult))
            step(V.tensor_tensor(lb[:, 0, :], lbw[:, 0, :], lbw[:, 0, :], ALU.subtract))
            step(V.tensor_tensor(small[:, 0:HEADS], lbw[:, 0, :], lbw[:, 1, :], ALU.add))
            step(V.tensor_tensor(lb[:, 1, :], small[:, 0:HEADS], lbw[:, 0, :], ALU.subtract))
            step(V.tensor_scalar(oml[:, :, :], lb[:, :, :], -1.0, 1.0, ALU.mult, ALU.add))
            ve.wait_ge(*made("cond", 0))
            for i in range(NEXT):
                sum_modulation(0, i)
                if i:
                    modulation(0, i - 1)
            modulation(0, NEXT - 1)

            for l in range(DEPTH):
                if l == 0:
                    ve.wait_ge(dma_x, 16)
                norm(l, 1)
                if l == 0:
                    ve.wait_ge(dma_mask, 16)
                    step(V.tensor_copy(lmask[:, :, :].rearrange("p n t -> p (n t)"), region[:, REGION - len(LEVELS) * P:]))
                for c in range(BT):
                    r = rstd(("hn", l, f"qa{c}"))
                    normalise(l, None, qA[:, c, :], f"qa{c}", AQ, r)
                    ve.wait_ge(*made("normed", (f"qa{c}", l)))
                    rope(qA[:, c, CTX:T], swp, con[:, CA:CA + LAT], con[:, SA:SA + LAT], 16, (l, c))
                r = rstd(("hn", l, "ka"))
                normalise(l, None, knT[:, :], "ka", AK, r)
                ve.wait_ge(*made("normed", ("ka", l)))
                rope(knT[:, CTX:T], swp, con[:, CA:CA + LAT], con[:, SA:SA + LAT], 16, (l, "ka"))
                rows = slice(NOPE, NOPE + ROPE)
                ve.wait_ge(*freed_by(("kr", l)))
                ve.wait_ge(*made("roped", (l, "ka")))
                rope(krT[rows, CTX:T], swp[rows, :], con[rows, CB:CB + LAT], con[rows, SB:SB + LAT], 8, (l, "kr"))
                gap(l, "kr")
                r = rstd(("hn", l, "qr"))
                for c in range(QT):
                    normalise(l, None, qr[:, c, :], f"qr{c}", BQ + c, r)
                r = rstd(("hn", l, "kc"))
                for c in range(CT):
                    normalise(l, None, ckvT[:, c, 0:T], f"kc{c}", BK + c, r)
                gap_done(l, "kr")
                gap(l, "kc")
                ve.wait_ge(*freed_by(("qb", l, HEADS - 1)))
                work = tmp[rows, :, :].rearrange("p a t -> p (a t)")[:, 0:HEADS * LAT].rearrange("p (h t) -> p h t", h=HEADS)
                tab = [con[rows, o:o + LAT].unsqueeze(1).broadcast_to([ROPE, HEADS, LAT]) for o in (CB, SB)]
                rope(qB[rows, :, CTX:T], work, tab[0], tab[1], 8, (l, "qb"))
                gap(l, "qb")
                gap_done(l, "kc")

                def maxima(u):
                    br, hp, qt = units[u]
                    c0, c1 = key_cols(qt)
                    for i in range(2):
                        ve.wait_ge(*full(("s", l, u, i)))
                        ps = held(("s", l, u, i))
                        if u >= 2:
                            ve.wait_ge(*freed_by(("s", l, u - 2, i)))
                        step(V.tensor_reduce(nmx[:, u % 2, i:i + 1], ps[:, 0:c1 - c0], AX, ALU.max, negate=True))
                        V.tensor_scalar(nmx[:, u % 2, i:i + 1], nmx[:, u % 2, i:i + 1], (SCALE_A, SCALE_B)[br], None, ALU.mult).then_inc(*signal("negmax", (l, u, i)))

                def softmax(u):
                    br, hp, qt = units[u]
                    n = P * len(key_tiles(qt))
                    for i in range(2):
                        ve.wait_ge(*freed_by(("s", l, u, i)))
                        step(V.reciprocal(rsum[:, u % 2, i:i + 1], rsum[:, u % 2, i:i + 1]))
                        pv = probs[:, u % 2, i, 0:n]
                        V.tensor_scalar(pv, pv, rsum[:, u % 2, i:i + 1], None, ALU.mult).then_inc(*signal("probs", (l, u, i)))

                def outputs(u):
                    br, hp, qt = units[u]
                    ve.wait_ge(*full(("o", l, u)))
                    ps = held(("o", l, u))
                    V.tensor_copy(oBr[br][:, hp, qt * P:(qt + 1) * P], ps[:, 0:P]).then_inc(*frees(("o", l, u)))
                    tally.also("o_ready", (l, br))

                for s in range(len(units) + 2):
                    if s < len(units):
                        maxima(s)
                        softmax(s)
                    if s >= 2:
                        outputs(s - 2)
                    if s == 1:
                        gap_done(l, "qb")

                ve.wait_ge(dma_out, 16 * (5 * l + 4))
                ve.wait_ge(*made("o_ready", (l, 1)))
                merges = [0]

                def merge(n, j, slot, key):
                    ve.wait_ge(*full(("p", l, n, j)))
                    ps = held(("p", l, n, j))
                    ve.wait_ge(*freed_by(("g", l, n, j)))
                    if n == 0:
                        V.tensor_tensor(tmp[:, j, :], ps[:, 0:T], gsb[:, slot, :], ALU.mult).then_inc(*frees(("p", l, n, j)))
                        tally.also("gate_used", key)
                    else:
                        V.tensor_tensor(prod, ps[:, 0:T], gsb[:, slot, :], ALU.mult).then_inc(*frees(("p", l, n, j)))
                        tally.also("gate_used", key)
                        ve.wait_ge(*freed_by(("p", l, n, j)))
                        V.tensor_tensor(tmp[:, j, :], tmp[:, j, :], prod, ALU.add).then_inc(*signal("merged", (l, n, j)))
                        ve.wait_ge(*made("merged", (l, n, j)))

                def fill_merge(n, j):
                    merge(n, j, merges[0] % GATES, (l, merges[0]))
                    merges[0] += 1

                ve.wait_ge(*made("zeroed", l))
                for hh in range(2):
                    if hh:
                        ve.wait_ge(*full(("oe", l, 0)))
                    for c in range(4):
                        if c in (0, 2):
                            gap(l, f"fb{hh}{c // 2}")
                        if c == 3:
                            gap_done(l, f"fb{hh}0")
                            gap_done(l, f"fb{hh}1")
                        ve.wait_ge(*freed_by(("fb", l, hh, c)))
                        h = 4 * hh + c
                        step(V.tensor_scalar(Fg[:, c, :], Fg[:, c, :], oml[:, l, h:h + 1], lb[:, l, h:h + 1], ALU.mult, ALU.add))
                        step(V.tensor_scalar(Fg[:, c, :], Fg[:, c, :], F_FLOOR, None, ALU.max))
                        V.tensor_scalar(Kg[:, c, :], Fg[:, c, :], -1.0, 1.0, ALU.mult, ALU.add).then_inc(*signal("fk_ready", (l, hh, c)))
                    ve.wait_ge(*made("fk_ready", (l, hh, 3)))
                    ve.wait_ge(*freed_by(("qc", l, hh, 1)))
                    for tt in range(TT):
                        prev = batches[batches.index((hh, tt)) - 1] if (hh, tt) != batches[0] else None
                        todo = list(fill[hh, tt])
                        decays = decay_steps(V, ve, l, hh, tt, prev, slice(0, HD), 1, 0, "f", step)

                        def place(n):
                            key = ("A", l, hh, tt, n)
                            ve.wait_ge(*full(key))
                            ps = held(key)
                            v = ps[:, :].rearrange("p (d t) -> p d t", d=4)
                            if n == 0:
                                if prev:
                                    ve.wait_ge(*full(("oi", l, *prev)))
                                V.tensor_tensor(Am[:, :, :], v, con[:, IDN:IDN + P].unsqueeze(1).broadcast_to([P, 4, P]), ALU.mult).then_inc(*frees(key))
                            else:
                                V.copy_predicated(Am[:, :, :], lmask[:, n - 1, :].unsqueeze(1).broadcast_to([P, 4, P]), v).then_inc(*frees(key))
                            ve.wait_ge(*freed_by(key))

                        next(decays)
                        for n in range(len(LEVELS) + 1):
                            if n < len(LEVELS):
                                next(decays)
                            else:
                                next(decays)
                            place(n)
                            if n in FILL_READ[len(fill[hh, tt])]:
                                fill_merge(*todo.pop(0))
                        while todo:
                            fill_merge(*todo.pop(0))
                        key = ("U", l, hh, tt)
                        ve.wait_ge(*full(key))
                        ps = held(key)
                        hs = slice(4 * hh, 4 * hh + 4)
                        v = ps[:, 0:4 * HD].rearrange("p (d n) -> p d n", d=4)
                        if tt == 0:
                            V.tensor_copy(Sout[:, hs, :], v).then_inc(*frees(key))
                            tally.also("sout", (l, hh))
                        else:
                            ve.wait_ge(dma_state, 32 * (l + 1))
                            r, src, dst = (slice(0, HD), 0, 1) if tt == 1 else (slice(HD, P), 1, 0)
                            if tt == 2:
                                ve.wait_ge(*made("kr_b", (l, hh, 2)))
                            for d in range(4):
                                h = 4 * hh + d
                                ins = V.scalar_tensor_tensor(Sin[r, dst, h, :], Sin[r, src, h, :], dec[r, tt, h:h + 1], v[r, d, :], ALU.mult, ALU.add)
                            ins.then_inc(*frees(key))
                            tally.also("s_f" if tt == 1 else "s_b", (l, hh))
                    key = ("oe", l, hh)
                    ve.wait_ge(*full(key))
                    ps = held(key)
                    ve.wait_ge(*freed_by(("oi", l, hh, 1)))
                    ve.wait_ge(*freed_by(("oi", l, hh, 2)))
                    o = oBr[2][:, 2 * hh:2 * hh + 2, CTX:T]
                    V.tensor_tensor(o, o, ps[:, :].rearrange("p (a n) -> p a n", a=2), ALU.add).then_inc(*frees(key))
                    tally.also("oc_sum", (l, hh))
                for c in range(BT):
                    r = rstd(("hn", l, f"oc{c}"))
                    normalise(l, None, oBr[2][:, c, :], f"oc{c}", CO, r)
                for c in range(BT):
                    ve.wait_ge(*freed_by(("gc", l, c)))
                    ve.wait_ge(*made("normed", (f"oc{c}", l)))
                    V.tensor_tensor(oBr[2][:, c, :], oBr[2][:, c, :], Fg[:, c, :], ALU.mult).then_inc(*signal("oc_gated", (l, c)))
                gap(l, "gc")
                for j in range(KT):
                    merge(2, j, j % GATES, (l, "c", j))
                    if j == 2:
                        gap(l, "g2")
                    if j == 3:
                        gap_done(l, "gc")
                    if j == 5:
                        gap(l, "g5")
                    if j == 6:
                        gap_done(l, "g2")

                def residual(src, key, l2, j, chunk, names):
                    for g, a, b in GROUPS:
                        ins = V.scalar_tensor_tensor(xT[:, j, a:b], src[:, a:b], mod[:, l, chunk * KT + j, g:g + 1], xT[:, j, a:b],
                                                     ALU.mult, ALU.add)
                    return ins

                ve.wait_ge(*freed_by(("mod", l, 3 * KT // 4 - 1)))
                for j in range(KT):
                    if j % 4 == 0:
                        gap(l, f"o{j // 4}")
                    ve.wait_ge(*full(("out", l, j)))
                    ps = held(("out", l, j))
                    residual(ps, None, l, j, 2, None).then_inc(*frees(("out", l, j)))
                    tally.also("x_ready", (l, 2, j))
                    if j == 1:
                        gap_done(l, "g5")
                    if j % 4 == 3:
                        gap_done(l, f"o{j // 4}")

                norm(l, 2)
                ve.wait_ge(dma_out, 16 * (5 * l + 5))
                route(ve, V, l, step)
                for t in range(TT):
                    for g in range(2):
                        key = ("ht", l, t, g)
                        ve.wait_ge(*full(key))
                        ve.wait_ge(*made("ht_high", (l, t, g)))
                        V.tensor_tensor(htok[:, 1, t, g * 512:(g + 1) * 512], held(key)[:, :], htok[:, 0, t, g * 512:(g + 1) * 512].bitcast(F32),
                                        ALU.subtract).then_inc(*frees(key))
                rank = rt[:, 340:388]
                key = ("rank", l)
                ve.wait_ge(*full(key))
                step(V.scalar_tensor_tensor(rank, held(key)[:, 0:TT * NE], 1.0, rt[:, 0:TT * NE], ALU.add, ALU.mult))
                step(V.tensor_scalar(rank, rank, -1.0, None, ALU.add))
                V.tensor_reduce(rt[:, 320:321], held(key)[:, TT * NE:(TT + 1) * NE], AX, ALU.max).then_inc(*frees(key))
                ve.wait_ge(*freed_by(key))
                V.tensor_scalar(flag[:, :], rt[:, 320:321], float(SLOTS), None, ALU.is_gt).then_inc(*signal("flag", l))
                ve.wait_ge(*made("flag", l))
                many = ve.value_load(flag[0:1, 0:1], min_val=0, max_val=1)
                before = dict(tally.count)
                with ve.If(many == 0):
                    dve_short(ve, l)
                tally.count = before
                with ve.Else():
                    dve_general(ve, l)
                ve.wait_ge(*freed_by(("mod", l, NMOD - 1)))
                for j in range(KT):
                    residual(tmp[:, j, :], None, l, j, 5, None).then_inc(*signal("x_ready", (l + 1, 1, j)))

            r = rstd(("n", DEPTH, 1))
            ve.wait_ge(*full(("n", DEPTH, 1)))
            for k in range(KT):
                V.scalar_tensor_tensor(hT[:, k, :], xT[:, k, :], fing[:, k:k + 1], r, ALU.mult, ALU.mult).then_inc(*signal("y_ready", k))

        @block.gpsimd
        def _(po):
            G = nc.gpsimd
            steps = [0]

            def step(ins):
                ins.then_inc(*signal("pool_step", steps[0]))
                steps[0] += 1
                po.wait_ge(sem("pool_step"), steps[0])

            rows = slice(NOPE, NOPE + ROPE)
            for l in range(DEPTH):
                if l:
                    po.wait_ge(*made("x_ready", (l, 1, KT - 1)))
                po.dma_start(keysA[:, :, T:KEYS], A["kcT"][l]).then_inc(dma_cache, 16)
                po.dma_start(vA[:, 3, :], A["vc"][l]).then_inc(dma_cache, 16)
                po.dma_start(ckvT[:, :, T:KEYS], A["ckvcT"][l]).then_inc(dma_cache, 16)
                po.dma_start(krT[rows, T:KEYS], A["krcT"][l]).then_inc(dma_cache, 16)
                po.wait_ge(dma_cache, 16 * NCACHE * (l + 1))
                po.wait_ge(*made("roped", (l, "kr")))
                G.tensor_copy(keysB[rows, :, :], krT[rows, :].unsqueeze(1).broadcast_to([ROPE, HEADS, KEYS])).then_inc(*signal("kr_copied", l))
                po.wait_ge(*made("o_ready", (l, 1)))
                po.wait_ge(dma_out, 16 * (5 * l + 4))
                po.dma_start(Sin[0:HD, 0, :, :], A["s0"][l, 0:HD]).then_inc(dma_state, 16)
                po.dma_start(Sin[HD:P, 1, :, :], A["s0"][l, HD:P]).then_inc(dma_state, 16)
                po.wait_ge(*made("kr_copied", l))
                for i in range(len(LEVELS)):
                    G.memset(Ql[i], 0.0)
                    ins = G.memset(Kl[i], 0.0)
                ins.then_inc(*signal("zeroed", l))
                po.wait_ge(*made("zeroed", l))
                for hh, tt in batches:
                    prev = batches[batches.index((hh, tt)) - 1] if (hh, tt) != batches[0] else None
                    po.wait_ge(*made("fk_ready", (l, hh, 3)))
                    po.wait_ge(*freed_by(("qc", l, hh, 1)))
                    for _ in decay_steps(G, po, l, hh, tt, prev, slice(HD, P), 0, 1, "b", step):
                        pass

        @block.sync
        def _(sp):
            for dst, name in ((cv[:, :, :], "cv"), (con[:, :], "con"), (par[:, :, :], "par"), (lbl[:, :, :], "lbl"), (fing[:, :], "fing")):
                sp.dma_start(dst, A[name]).then_inc(dma_con, 16)

            for i, (l, name, size) in enumerate(order):
                slot, _, replaced = slots[i]
                if replaced is not None:
                    pl, pn, _ = order[replaced]
                    if pn[0] == "e":
                        sp.wait_ge(*made("unit_free", (pl, UNITS * int(pn[2:]) + 2 * ("eg", "eu", "ed").index(pn[:2]) + 1)))
                    elif pn[0] == "m":
                        sp.wait_ge(*made("mod_summed", (pl, int(pn[1:]))))
                        if (pl, int(pn[1:])) < (0, NEXT):
                            sp.wait_ge(*full(("mod", pl, int(pn[1:]))))
                    else:
                        sp.wait_ge(*full(closing[replaced]))
                sp.dma_start(slabs[:, slot, 0:size], A["W"][i, :, 0:size]).then_inc(dma_slab[slot], 16)
                if i == 0:
                    sp.dma_start(xT[:, :, :], A["xT"]).then_inc(dma_x, 16)
                if i == NEXT - 1:
                    sp.dma_start(region[:, REGION - len(LEVELS) * P:], A["lmask"]).then_inc(dma_mask, 16)
                if name == "ic":
                    sp.wait_ge(*made("normed", ("ka", l)))
                    sp.dma_start(A["new_k"][l], knT[:, 0:CTX]).then_inc(dma_out, 16)
                    sp.wait_ge(*freed_by(("va", l)))
                    sp.dma_start(A["new_v"][l], vA[:, 0, :]).then_inc(dma_out, 16)
                    sp.wait_ge(*made("normed", ("kc1", l)))
                    sp.dma_start(A["new_ckv"][l], ckvT[:, :, 0:CTX]).then_inc(dma_out, 16)
                    sp.wait_ge(*freed_by(("kr", l)))
                    sp.dma_start(A["new_kr"][l], krT[NOPE:NOPE + ROPE, 0:CTX]).then_inc(dma_out, 16)
                if name == "o1":
                    sp.wait_ge(*made("sout", (l, 1)))
                    sp.dma_start(A["new_s"][l], Sout[:, :, :]).then_inc(dma_out, 16)
            for k in (KT // 2, KT):
                sp.wait_ge(*made("y_ready", k - 1))
                sp.dma_start(A["y"][:, k - KT // 2:k, :], hT[:, k - KT // 2:k, :]).then_inc(dma_out, 16)
            sp.wait_ge(dma_out, 16 * (5 * DEPTH + 2))

    return tally.here


_IN = ["W", "xT", "con", "lmask", "par", "lbl", "fing", "cv", "kcT", "vc", "ckvcT", "krcT", "s0"]
_OUT = [("y", (P, KT, T)), ("new_k", (DEPTH, P, CTX)), ("new_v", (DEPTH, CTX, P)), ("new_ckv", (DEPTH, P, CT, CTX)),
        ("new_kr", (DEPTH, ROPE, CTX)), ("new_s", (DEPTH, P, HEADS, HD))]


def constants():
    con = np.zeros((P, NCON), np.float32)
    p = np.arange(P)
    con[:, ONES:ONES + P] = 1.0
    con[:, BLK:BLK + P] = (p[:, None] // HD == p[None, :] // HD)
    con[:, IDN:IDN + P] = np.eye(P)
    con[:, TRI:TRI + P] = p[:, None] < p[None, :]
    con[:, IOTA:IOTA + P] = p[None, :]
    row, col = np.arange(LAT) // GRID_W, np.arange(LAT) % GRID_W

    def rotary(width, d):
        half = width // 2
        inv = (np.float32(10000.0) ** (-np.arange(0, half, 2, dtype=np.float32) / np.float32(half))).astype(np.float32)
        pos = np.where((d // half == 0)[:, None], row[None, :], col[None, :]).astype(np.float32)
        ang = pos * inv[d % (half // 2)][:, None]
        sign = np.where(d % half < half // 2, -1.0, 1.0)[:, None]
        return np.cos(ang), np.sin(ang) * sign

    con[:, CA:CA + LAT], con[:, SA:SA + LAT] = rotary(HD, p % HD)
    con[NOPE:QB_W, CB:CB + LAT], con[NOPE:QB_W, SB:SB + LAT] = rotary(ROPE, np.arange(ROPE))
    mask = np.zeros((P, len(LEVELS), P), np.float32)
    for n, b in enumerate(LEVELS):
        mask[:, n] = (p[:, None] // (2 * b) == p[None, :] // (2 * b)) & (p[:, None] // b != p[None, :] // b)
    return con, mask.reshape(P, -1)


def lay_out(inputs):
    x = {k: np.asarray(v) for k, v in inputs.items()}
    f = np.float32

    def tiles(w):
        K, N = w.shape
        return w.reshape(K // P, P, N // P, P).transpose(1, 2, 0, 3).reshape(P, -1)

    def rows(w):
        K, N = w.shape
        return w.reshape(K // P, P, N).transpose(1, 0, 2).reshape(P, -1)

    order = slab_order()
    W = np.zeros((len(order), P, SLAB), f)
    widths = (BW, KV_A * HD, KV_A * HD, Q_RANK, KV_RANK, ROPE, BW, BW, BW, BW, BW, N_BRANCH * D)
    cut = np.cumsum((0,) + widths)
    for i, (l, name, size) in enumerate(order):
        w_in = x["w_in"][l]
        qa, ka, va, qra, kva, kra, ff, fb, qc, ic, gc, gp = [w_in[:, cut[n]:cut[n + 1]] for n in range(12)]
        if name[0] == "m":
            n = int(name[1:])
            s = rows(x["w_mod"][l][:, n * 512:(n + 1) * 512])
        elif name == "qa":
            s = tiles(qa)
        elif name == "kv":
            s = tiles(np.concatenate([ka, va, kra, np.zeros((D, P - ROPE), f), qra[:, 0:P]], 1))
        elif name == "qr":
            s = tiles(np.concatenate([qra[:, P:], kva], 1))
        elif name == "bwq":
            s = rows(x["b_wq"][l])
        elif name == "bwkv":
            w = x["b_wkv"][l].reshape(KV_RANK, HEADS, 2 * HD)
            s = np.concatenate([rows(w[:, :, :HD].reshape(KV_RANK, BW)), rows(w[:, :, HD:].reshape(KV_RANK, BW))], 1)
        elif name == "ic":
            s = rows(ic)
        elif name in ("fb0", "fb1"):
            w = np.stack([ff.reshape(D, HEADS, HD), fb.reshape(D, HEADS, HD)], 2).reshape(D, 2 * BW)
            s = tiles(w[:, int(name[2]) * BW:(int(name[2]) + 1) * BW])
        elif name in ("qc0", "qc1"):
            s = tiles(qc[:, int(name[2]) * 256:(int(name[2]) + 1) * 256])
        elif name == "gc":
            s = tiles(gc)
        elif name[:2] == "br":
            s = tiles(x["w_branch"][l, int(name[2])])
        elif name[0] == "g":
            n = int(name[1]) * D + int(name[2]) * BW
            s = tiles(gp[:, n:n + BW])
        elif name[:2] == "eg":
            s = rows(x["e_gate"][l, int(name[2:])])
        elif name[:2] == "eu":
            s = rows(x["e_up"][l, int(name[2:])])
        elif name[:2] == "ed":
            s = rows(x["e_down"][l, int(name[2:])])
        else:
            s = tiles(x["w_out"][l][:, int(name[1]) * 512:(int(name[1]) + 1) * 512])
        assert s.shape[1] == size, (name, s.shape, size)
        W[i, :, :size] = s

    col = lambda v: v.reshape(-1, P).T
    twice = lambda v: np.concatenate([v, v])[:, None]
    par = np.stack([np.concatenate([
        col(x["norm1_g"][l]), col(x["norm2_g"][l]), col(x["b_mod"][l]), twice(x["a_qnorm"][l]), twice(x["a_knorm"][l]),
        col(x["b_qnorm"][l]), col(x["b_kvnorm"][l]), twice(x["c_onorm"][l]),
        np.broadcast_to(np.concatenate([x["r_group_b"][l], x["r_expert_b"][l]])[None, :], (P, NG + NE)),
        rows(np.concatenate([x["r_group_w"][l], x["r_expert_w"][l]], 1))], 1) for l in range(DEPTH)], 1)
    con, mask = constants()
    tok = np.concatenate([x["x_prompt"][0], x["x_sample"][0]], 0)
    kc = x["cache_gqa_k"][0].transpose(0, 3, 2, 1)
    return {
        "W": W, "xT": tok.T.reshape(KT, P, T).transpose(1, 0, 2), "con": con, "lmask": mask, "par": par,
        "lbl": x["c_lb_logits"].reshape(DEPTH, 2, HEADS, HD).transpose(1, 3, 0, 2).reshape(P, DEPTH, HEADS),
        "fing": col(x["final_g"]), "cv": np.stack([col(x["c_ctx"]), col(x["c"][0])], 2),
        "kcT": np.concatenate([kc, kc], 1), "vc": x["cache_gqa_v"][0].reshape(DEPTH, PAST, KV_A * HD),
        "ckvcT": x["cache_mla_ckv"][0].transpose(0, 2, 1).reshape(DEPTH, CT, P, PAST).transpose(0, 2, 1, 3),
        "krcT": x["cache_mla_krope"][0].transpose(0, 2, 1),
        "s0": x["state_hgrn"][0].transpose(0, 1, 3, 2, 4).reshape(DEPTH, P, HEADS, HD),
    }


def kernel(**inputs):
    import concourse.bacc as bacc
    from concourse.bass_utils import run_bass_kernel_spmd

    arrays = {k: np.ascontiguousarray(v) for k, v in lay_out(inputs).items()}

    def build(known):
        nc = bacc.Bacc("TRN2", target_bir_lowering=False, num_devices=1)
        A = {n: nc.dram_tensor(f"in_{n}", arrays[n].shape, mybir.dt.from_np(arrays[n].dtype), kind="ExternalInput").ap() for n in _IN}
        for n, shape in _OUT:
            A[n] = nc.dram_tensor(f"out_{n}", shape, F32, kind="ExternalOutput").ap()
        return nc, program(nc, A, known)

    _, found = build({})
    nc, _ = build(found)
    r = run_bass_kernel_spmd(nc, [{f"in_{n}": arrays[n] for n in _IN}], core_ids=[0])
    o = {n: r.results[0][f"out_{n}"] for n, _ in _OUT}
    y = o["y"].transpose(2, 1, 0).reshape(T, D)
    return (y[None, :CTX], y[None, CTX:],
            o["new_k"].reshape(DEPTH, KV_A, HD, CTX).transpose(0, 3, 1, 2)[None],
            o["new_v"].reshape(DEPTH, CTX, KV_A, HD)[None],
            o["new_ckv"].transpose(0, 3, 2, 1).reshape(DEPTH, CTX, KV_RANK)[None],
            o["new_kr"].transpose(0, 2, 1)[None],
            o["new_s"].reshape(DEPTH, 2, HD, HEADS, HD).transpose(0, 1, 3, 2, 4)[None])
```
